# Optimizing a Trainium2 kernel written in Bass

```python
import jax, jax.numpy as jnp
from jax import lax
import numpy as np

D_MODEL = 1024
BATCH = 1
SEQ = 128
DEPTH = 2
DEC_BATCH = 1
DEC_SEQ = 512
PAST_LEN = 128

GRID_W = 64
ML_HEADS = 4
ML_HEAD_DIM = 128
ML_WIDTH = ML_HEADS * ML_HEAD_DIM
ML_CHUNK = 64
CV_WIDTH = 512
CV_TAPS = 3
NA_HEADS = 8
NA_HEAD_DIM = 64
NA_WIDTH = NA_HEADS * NA_HEAD_DIM
NA_WIN_ROWS = 8
NA_WIN_COLS = 16
NA_QBLOCK = 16
NA_KBAND = 32
N_BRANCH = 3
N_EXPERTS = 16
EC_CAPACITY_FACTOR = 2
MOE_FF = 1024
ROPE_BASE = 10000.0
NORM_EPS = 1e-6
PROJ_SIZES = (ML_WIDTH, ML_WIDTH, ML_WIDTH, ML_WIDTH, 2 * ML_HEADS, 2 * ML_HEADS,
              CV_WIDTH, CV_WIDTH, CV_WIDTH, NA_WIDTH, NA_WIDTH, NA_WIDTH, N_BRANCH * D_MODEL)
PROJ_WIDTH = sum(PROJ_SIZES)

kernel_name = 'hybrid_mlstm_conv_natten_ec_diffusion_step'

def rmsnorm(x, g):
    xf = x.astype(jnp.float32)
    y = xf * lax.rsqrt(jnp.mean(xf * xf, axis=-1, keepdims=True) + NORM_EPS)
    return (y * g.astype(jnp.float32)).astype(x.dtype)

def head_rms(x, g):
    return rmsnorm(x, g)

def modulation(cvec, w, b):
    m = jax.nn.silu(cvec) @ w + b
    return jnp.split(m, 6, axis=-1)

def rope_1d(x, pos):
    half = x.shape[-1] // 2
    freqs = ROPE_BASE ** (-jnp.arange(half, dtype=jnp.float32) / half)
    ang = pos[:, None] * freqs[None, :]
    cos = jnp.cos(ang)[None, :, None, :]
    sin = jnp.sin(ang)[None, :, None, :]
    x1, x2 = x[..., :half], x[..., half:]
    return jnp.concatenate([x1 * cos - x2 * sin, x1 * sin + x2 * cos], axis=-1).astype(x.dtype)

def rope_2d(x):
    t = jnp.arange(x.shape[1])
    row = (t // GRID_W).astype(jnp.float32)
    col = (t % GRID_W).astype(jnp.float32)
    half = x.shape[-1] // 2
    return jnp.concatenate([rope_1d(x[..., :half], row), rope_1d(x[..., half:], col)], axis=-1)

def mlstm_chunk_scan(q, k, v, ig, lf, c0, n0, m0):
    bsz, n_tok, n_h, d = q.shape
    n_chunk = n_tok // ML_CHUNK

    def chunks4(a):
        return a.reshape(bsz, n_chunk, ML_CHUNK, n_h, a.shape[-1]).transpose(1, 0, 3, 2, 4)

    def chunks3(a):
        return a.reshape(bsz, n_chunk, ML_CHUNK, n_h).transpose(1, 0, 3, 2)

    lower = jnp.tril(jnp.ones((ML_CHUNK, ML_CHUNK), dtype=bool))

    def step(carry, xs):
        c_prev, n_prev, m_prev = carry
        qc, kc, vc, ic, fc = xs
        b = jnp.cumsum(fc, axis=-1)
        dlog = jnp.where(lower, b[..., :, None] - b[..., None, :] + ic[..., None, :], -jnp.inf)
        m_t = jnp.maximum(b + m_prev[..., None], jnp.max(dlog, axis=-1))
        inter = jnp.exp(b + m_prev[..., None] - m_t)
        s = jnp.einsum('bhtd,bhsd->bhts', qc, kc) * jnp.exp(dlog - m_t[..., None])
        num = inter[..., None] * jnp.einsum('bhtd,bhdv->bhtv', qc, c_prev) + jnp.einsum('bhts,bhsv->bhtv', s, vc)
        den = inter * jnp.einsum('bhtd,bhd->bht', qc, n_prev) + jnp.sum(s, axis=-1)
        h = num / jnp.maximum(jnp.abs(den), jnp.exp(-m_t))[..., None]
        m_new = m_t[..., -1]
        w_end = jnp.exp(b[..., -1:] - b + ic - m_new[..., None])
        decay = jnp.exp(b[..., -1] + m_prev - m_new)
        c_new = decay[..., None, None] * c_prev + jnp.einsum('bhs,bhsd,bhsv->bhdv', w_end, kc, vc)
        n_new = decay[..., None] * n_prev + jnp.einsum('bhs,bhsd->bhd', w_end, kc)
        return (c_new, n_new, m_new), h

    (c_f, n_f, m_f), hs = lax.scan(step, (c0, n0, m0),
                                   (chunks4(q), chunks4(k), chunks4(v), chunks3(ig), chunks3(lf)))
    h = hs.transpose(1, 0, 3, 2, 4).reshape(bsz, n_tok, n_h, d)
    return h, c_f, n_f, m_f

def mlstm_bidir(q, k, v, ig, lf, c0, n0, m0):
    rev = lambda a: jnp.flip(a, axis=1)
    h_f, cf, nf, mf = mlstm_chunk_scan(q, k, v, ig[:, :, 0], lf[:, :, 0], c0[:, 0], n0[:, 0], m0[:, 0])
    h_b, cb, nb, mb = mlstm_chunk_scan(rev(q), rev(k), rev(v), rev(ig[:, :, 1]), rev(lf[:, :, 1]),
                                       c0[:, 1], n0[:, 1], m0[:, 1])
    return (h_f + rev(h_b), jnp.stack([cf, cb], axis=1), jnp.stack([nf, nb], axis=1),
            jnp.stack([mf, mb], axis=1))

def short_conv(x, w):
    pad = CV_TAPS // 2
    xp = jnp.pad(x, ((0, 0), (pad, pad), (0, 0)))
    n = x.shape[1]
    return sum(xp[:, j:j + n] * w[j] for j in range(CV_TAPS))

def na_context(q, k, v):
    s = jnp.einsum('bqhd,bkhd->bhqk', q, k, preferred_element_type=jnp.float32) * NA_HEAD_DIM ** -0.5
    p = jax.nn.softmax(s, axis=-1)
    return jnp.einsum('bhqk,bkhd->bqhd', p.astype(v.dtype), v)

def na_latent(q, k, v, ck, cv, rpb):
    bsz, n_tok, n_h, dh = q.shape
    rows = n_tok // GRID_W
    kh = min(NA_WIN_ROWS, rows)
    ncb = GRID_W // NA_QBLOCK
    scale = NA_HEAD_DIM ** -0.5
    qb = q.reshape(bsz, rows, ncb, NA_QBLOCK, n_h, dh)
    kg = k.reshape(bsz, rows, GRID_W, n_h, dh)
    vg = v.reshape(bsz, rows, GRID_W, n_h, dh)
    r = jnp.arange(rows)
    row_idx = jnp.clip(r - NA_WIN_ROWS // 2, 0, rows - kh)[:, None] + jnp.arange(kh)[None, :]
    col_start = jnp.clip(jnp.arange(GRID_W) - NA_WIN_COLS // 2, 0, GRID_W - NA_WIN_COLS)
    band_start = jnp.clip(col_start[::NA_QBLOCK], 0, GRID_W - NA_KBAND)
    band_idx = band_start[:, None] + jnp.arange(NA_KBAND)[None, :]
    ri = row_idx[:, :, None, None]
    bi = band_idx[None, None]
    k_blk = kg[:, ri, bi]
    v_blk = vg[:, ri, bi]
    sw = jnp.einsum('brnqhd,brinjhd->bhrnqij', qb, k_blk, preferred_element_type=jnp.float32) * scale
    qcol = jnp.arange(ncb)[:, None] * NA_QBLOCK + jnp.arange(NA_QBLOCK)[None, :]
    qs = col_start[qcol]
    kcol = band_idx[:, None, :]
    valid = (kcol >= qs[..., None]) & (kcol < qs[..., None] + NA_WIN_COLS)
    dr = row_idx - r[:, None] + NA_WIN_ROWS - 1
    dc = jnp.clip(kcol - qcol[..., None] + NA_WIN_COLS - 1, 0, 2 * NA_WIN_COLS - 2)
    bias = rpb[:, dr[:, None, None, :, None], dc[None, :, :, None, :]]
    sw = jnp.where(valid[:, :, None, :], sw + bias[None].astype(jnp.float32), -jnp.inf)
    sc = jnp.einsum('brnqhd,bmhd->bhrnqm', qb, ck, preferred_element_type=jnp.float32) * scale
    n_win = kh * NA_KBAND
    joint = jnp.concatenate([sw.reshape(sw.shape[:5] + (n_win,)), sc], axis=-1)
    p = jax.nn.softmax(joint, axis=-1).astype(v.dtype)
    pw = p[..., :n_win].reshape(sw.shape)
    pc = p[..., n_win:]
    out = (jnp.einsum('bhrnqij,brinjhd->brnqhd', pw, v_blk)
           + jnp.einsum('bhrnqm,bmhd->brnqhd', pc, cv))
    return out.reshape(bsz, n_tok, n_h, dh)

def token_mixer(h, ml_state, na_ctx, w_in, b_in, ml_fbias, ml_out_g, cv_w, na_q_g, na_k_g,
                w_pa, w_pb, w_pc, w_o):
    latent = na_ctx is not None
    bsz, n_tok, _ = h.shape
    f32 = jnp.float32
    p = h @ w_in + b_in
    (mq, mk, mv, mo, mi, mf, cb, cc, ch, nq, nk, nv, gt) = jnp.split(
        p, np.cumsum(PROJ_SIZES)[:-1].tolist(), axis=-1)
    ml_heads = lambda a: a.reshape(bsz, n_tok, ML_HEADS, ML_HEAD_DIM).astype(f32)
    mq, mk, mv = ml_heads(mq), ml_heads(mk), ml_heads(mv)
    if latent:
        mq, mk = rope_2d(mq), rope_2d(mk)
    mk = mk * ML_HEAD_DIM ** -0.5
    ig = mi.reshape(bsz, n_tok, 2, ML_HEADS).astype(f32)
    lf = jax.nn.log_sigmoid(mf.reshape(bsz, n_tok, 2, ML_HEADS).astype(f32) + ml_fbias.astype(f32))
    h_ml, c_s, n_s, m_s = mlstm_bidir(mq, mk, mv, ig, lf, ml_state[0], ml_state[1], ml_state[2])
    y_ml = head_rms(h_ml, ml_out_g.reshape(ML_HEADS, ML_HEAD_DIM)).reshape(
        bsz, n_tok, ML_WIDTH).astype(h.dtype) * jax.nn.sigmoid(mo)
    y_cv = cb * short_conv(cc * ch, cv_w)
    na_heads = lambda a: a.reshape(bsz, n_tok, NA_HEADS, NA_HEAD_DIM)
    nq = head_rms(na_heads(nq), na_q_g)
    nk = head_rms(na_heads(nk), na_k_g)
    nv = na_heads(nv)
    if latent:
        y_na = na_latent(nq, nk, nv, na_ctx[0], na_ctx[1], na_ctx[2])
    else:
        y_na = na_context(nq, nk, nv)
    y_na = y_na.reshape(bsz, n_tok, NA_WIDTH)
    g = jax.nn.sigmoid(gt.reshape(bsz, n_tok, N_BRANCH, D_MODEL))
    merged = g[:, :, 0] * (y_ml @ w_pa) + g[:, :, 1] * (y_cv @ w_pb) + g[:, :, 2] * (y_na @ w_pc)
    return merged @ w_o, (c_s, n_s, m_s), nk, nv

def expert_choice_ffn(h, w_router, w_gate, w_up, w_down):
    bsz, n_tok, d = h.shape
    cap = EC_CAPACITY_FACTOR * n_tok // N_EXPERTS
    aff = jax.nn.softmax((h @ w_router).astype(jnp.float32), axis=-1)
    gate, idx = lax.top_k(jnp.swapaxes(aff, 1, 2), cap)
    xg = jax.vmap(lambda hb, ib: hb[ib])(h, idx)
    a = jnp.einsum('becd,edf->becf', xg, w_gate)
    u = jnp.einsum('becd,edf->becf', xg, w_up)
    y = jnp.einsum('becf,efd->becd', jax.nn.silu(a) * u, w_down) * gate[..., None].astype(h.dtype)
    return jax.vmap(lambda yb, ib: jnp.zeros((n_tok, d), h.dtype).at[ib.reshape(-1)].add(
        yb.reshape(-1, d)))(y, idx)

def setup_inputs(seed: int = 0) -> dict:
    key = jax.random.key(seed)
    ks = jax.random.split(key, 32)

    def nrm(i, shape, s=1.0):
        return jax.random.normal(ks[i], shape, jnp.float32) * s

    return {
        'x_prompt': nrm(0, (BATCH, SEQ, D_MODEL)),
        'x_sample': nrm(1, (DEC_BATCH, DEC_SEQ, D_MODEL)),
        'c': nrm(2, (DEC_BATCH, D_MODEL)),
        'cache_ctx_k': nrm(3, (DEC_BATCH, DEPTH, PAST_LEN, NA_HEADS, NA_HEAD_DIM)),
        'cache_ctx_v': nrm(4, (DEC_BATCH, DEPTH, PAST_LEN, NA_HEADS, NA_HEAD_DIM)),
        'state_mlstm_c': nrm(5, (DEC_BATCH, DEPTH, 2, ML_HEADS, ML_HEAD_DIM, ML_HEAD_DIM), 0.3),
        'state_mlstm_n': nrm(6, (DEC_BATCH, DEPTH, 2, ML_HEADS, ML_HEAD_DIM), 0.3),
        'state_mlstm_m': jax.random.uniform(ks[7], (DEC_BATCH, DEPTH, 2, ML_HEADS), jnp.float32, 0.0, 3.0),
        'c_ctx': nrm(8, (D_MODEL,)),
        'ada_w': nrm(9, (DEPTH, D_MODEL, 6 * D_MODEL), 0.3 * D_MODEL ** -0.5),
        'ada_b': nrm(10, (DEPTH, 6 * D_MODEL), 0.02),
        'norm1_g': 1.0 + nrm(11, (DEPTH, D_MODEL), 0.02),
        'norm2_g': 1.0 + nrm(12, (DEPTH, D_MODEL), 0.02),
        'w_in': nrm(13, (DEPTH, D_MODEL, PROJ_WIDTH), D_MODEL ** -0.5),
        'b_in': nrm(14, (DEPTH, PROJ_WIDTH), 0.02),
        'ml_fbias': 3.0 + nrm(15, (DEPTH, 2, ML_HEADS), 0.5),
        'ml_out_g': 1.0 + nrm(16, (DEPTH, ML_WIDTH), 0.02),
        'cv_w': nrm(17, (DEPTH, CV_TAPS, CV_WIDTH), CV_TAPS ** -0.5),
        'na_q_g': 1.0 + nrm(18, (DEPTH, NA_HEAD_DIM), 0.02),
        'na_k_g': 1.0 + nrm(19, (DEPTH, NA_HEAD_DIM), 0.02),
        'na_rpb': nrm(20, (DEPTH, NA_HEADS, 2 * NA_WIN_ROWS - 1, 2 * NA_WIN_COLS - 1), 0.02),
        'w_pa': nrm(21, (DEPTH, ML_WIDTH, D_MODEL), ML_WIDTH ** -0.5),
        'w_pb': nrm(22, (DEPTH, CV_WIDTH, D_MODEL), CV_WIDTH ** -0.5),
        'w_pc': nrm(23, (DEPTH, NA_WIDTH, D_MODEL), NA_WIDTH ** -0.5),
        'w_o': nrm(24, (DEPTH, D_MODEL, D_MODEL), D_MODEL ** -0.5),
        'w_router': nrm(25, (DEPTH, D_MODEL, N_EXPERTS), D_MODEL ** -0.5),
        'w_gate': nrm(26, (DEPTH, N_EXPERTS, D_MODEL, MOE_FF), D_MODEL ** -0.5),
        'w_up': nrm(27, (DEPTH, N_EXPERTS, D_MODEL, MOE_FF), D_MODEL ** -0.5),
        'w_down': nrm(28, (DEPTH, N_EXPERTS, MOE_FF, D_MODEL), MOE_FF ** -0.5),
    }

def reference(x_prompt, x_sample, c, cache_ctx_k, cache_ctx_v, state_mlstm_c, state_mlstm_n,
              state_mlstm_m, c_ctx, ada_w, ada_b, norm1_g, norm2_g, w_in, b_in, ml_fbias, ml_out_g,
              cv_w, na_q_g, na_k_g, na_rpb, w_pa, w_pb, w_pc, w_o, w_router, w_gate, w_up, w_down):
    f32 = jnp.float32
    xp, xs = x_prompt, x_sample
    bp = xp.shape[0]
    ks_l, vs_l, cs_l, ns_l, ms_l = [], [], [], [], []
    for l in range(DEPTH):
        lw = (w_in[l], b_in[l], ml_fbias[l], ml_out_g[l], cv_w[l], na_q_g[l], na_k_g[l],
              w_pa[l], w_pb[l], w_pc[l], w_o[l])
        sh1, sc1, gt1, sh2, sc2, gt2 = modulation(c_ctx, ada_w[l], ada_b[l])
        zero_state = (jnp.zeros((bp, 2, ML_HEADS, ML_HEAD_DIM, ML_HEAD_DIM), f32),
                      jnp.zeros((bp, 2, ML_HEADS, ML_HEAD_DIM), f32),
                      jnp.zeros((bp, 2, ML_HEADS), f32))
        mix, (cst, nst, mst), nk, nv = token_mixer(
            rmsnorm(xp, norm1_g[l]) * (1 + sc1) + sh1, zero_state, None, *lw)
        xp = xp + gt1 * mix
        xp = xp + gt2 * expert_choice_ffn(rmsnorm(xp, norm2_g[l]) * (1 + sc2) + sh2,
                                          w_router[l], w_gate[l], w_up[l], w_down[l])
        ks_l.append(nk)
        vs_l.append(nv)
        cs_l.append(cst.astype(xp.dtype))
        ns_l.append(nst.astype(xp.dtype))
        ms_l.append(mst.astype(xp.dtype))
        sh1, sc1, gt1, sh2, sc2, gt2 = [m[:, None, :] for m in modulation(c, ada_w[l], ada_b[l])]
        ml_state = (state_mlstm_c[:, l].astype(f32), state_mlstm_n[:, l].astype(f32),
                    state_mlstm_m[:, l].astype(f32))
        mix, _, _, _ = token_mixer(rmsnorm(xs, norm1_g[l]) * (1 + sc1) + sh1, ml_state,
                                   (cache_ctx_k[:, l], cache_ctx_v[:, l], na_rpb[l]), *lw)
        xs = xs + gt1 * mix
        xs = xs + gt2 * expert_choice_ffn(rmsnorm(xs, norm2_g[l]) * (1 + sc2) + sh2,
                                          w_router[l], w_gate[l], w_up[l], w_down[l])
    new_ctx_k = jnp.stack(ks_l, axis=1)
    new_ctx_v = jnp.stack(vs_l, axis=1)
    new_mlstm_c = jnp.stack(cs_l, axis=1)
    new_mlstm_n = jnp.stack(ns_l, axis=1)
    new_mlstm_m = jnp.stack(ms_l, axis=1)
    return (xp, xs, new_ctx_k, new_ctx_v, new_mlstm_c, new_mlstm_n, new_mlstm_m)


_drawn_inputs = setup_inputs


def setup_inputs(seed=0):
    import zlib

    import numpy as np

    out = dict(_drawn_inputs(seed))
    spreads = {}
    factors = {'cache_ctx_k': 6.441,
     'cache_ctx_v': 5.195,
     'state_mlstm_c': 3.768,
     'state_mlstm_n': 7.507,
     'state_mlstm_m': 7.651,
     'norm2_g': 8.0,
     'ml_out_g': 8.0,
     'na_q_g': 8.0,
     'na_k_g': 2.914,
     'na_rpb': 8.0}
    for name, (base, spread) in spreads.items():
        noise = np.random.default_rng([zlib.crc32(name.encode()), seed]).standard_normal(out[name].shape)
        drawn = base * np.exp(spread * noise) if base else spread * noise
        out[name] = __import__('jax').numpy.asarray(drawn.astype(out[name].dtype))
    for name, factor in factors.items():
        out[name] = (out[name] * factor).astype(out[name].dtype)
    return out
```

```python
import concourse.bass as bass
from concourse import mybir
from contextlib import ExitStack
import numpy as np

F32 = mybir.dt.float32
ALU = mybir.AluOpType
ACT = mybir.ActivationFunctionType
AX = mybir.AxisListType

P = 128
D = 1024
KD = D // P
DEPTH = 2
TP, TS = 128, 512
T = TP + TS
HALF = T // 2
NTILE = T // P
GRID = 64
ROWS = TS // GRID
HM = 4
HN, DN = 8, 64
WB = 512
KB = WB // P
NBLK, QB, KBAND = 4, 16, 32
NE, FF = 16, 1024
CAP_P, CAP_S = 2 * TP // NE, 2 * TS // NE
CAP = CAP_S + CAP_P
NPAIR = NE // 2
EPS = 1e-6
ML_SCALE = float(P) ** -0.5
BAND0 = [min(max(16 * n - 8, 0), GRID - KBAND) for n in range(NBLK)]
WINK = ROWS * KBAND
NKEY = WINK + P

C_MQ, C_MK, C_MV, C_MO, C_G = 0, 512, 1024, 1536, 2048
C_CB, C_CC, C_CH = 2064, 2576, 3088
C_NQ, C_NK, C_NV, C_GT = 3600, 4112, 4624, 5136
PROJ = C_GT + 3 * D

Q_ADAB, Q_G1, Q_G2, Q_BIN = 0, 48, 56, 64
Q_OG, Q_CW, Q_GQ, Q_GK, Q_M0, Q_N0 = 128, 132, 144, 145, 146, 154
Q_BV = 162
NPRM = Q_BV + 2 * WB
B_MQ, B_MK, B_MO, B_CB, B_CC, B_CH, B_NQ, B_NK, B_GT = 0, 4, 12, 16, 20, 24, 28, 32, 40

K_ID, K_ONE, K_BLK, K_ROT, K_COS, K_SIN = 0, 128, 256, 384, 512, 1024
K_TRI, K_MASK, K_IOTA = 1536, 1792, 1920
NCONST = 1984

NSLOT = 4
ADA_CHUNKS = 6 * D // 512
(R_MQ, R_MK, R_MV, R_MO, R_NQ, R_NK, R_NV, R_CC, R_CH, R_CB) = range(ADA_CHUNKS, ADA_CHUNKS + 10)
R_MERGE = R_CB + 1
R_O = R_MERGE + 9
R_END = R_O + 2
R_EXP = -(-R_END // NSLOT) * NSLOT
PAIR_CHUNKS = 12


def slot_uses(q):
    return sum(1 for c in range(q % NSLOT, q, NSLOT) if c < R_END or c >= R_EXP)


SLOT_LAYER = [slot_uses(R_EXP + NPAIR * PAIR_CHUNKS + s) for s in range(NSLOT)]


class Signal:

    def __init__(self, sem, per_layer, unit=1):
        self.sem, self.per_layer, self.unit = sem, per_layer, unit

    def at(self, l, k):
        return self.sem, (l * self.per_layer + k) * self.unit


def step_program(nc, xT, cond, const, prm, rowp, biasT, ckT, cv, c0, ada_w, w_in, w_pa, w_pb, w_pc,
                 w_o, w_router, w_gate, w_up, w_down, yT, new_k, new_v, new_cn, new_m, nv_dram):
    with ExitStack() as ctx:
        def sb(name, shape):
            return ctx.enter_context(nc.sbuf_tensor(name, shape, F32))

        def signal(name, per_layer, unit=1):
            return Signal(ctx.enter_context(nc.semaphore(name)), per_layer, unit)

        def semaphore(name):
            return ctx.enter_context(nc.semaphore(name))

        ring = sb("ring", [P, NSLOT, 4096])
        x = sb("x", [P, KD, T])
        h = sb("h", [P, KD, T])
        cst = sb("cst", [P, NCONST])
        par = sb("par", [P, NPRM])
        rowpar = sb("rowpar", [8, 4])
        silu_c = sb("silu_c", [P, KD, 2])
        mod = sb("mod", [P, 48, 2])
        a1 = sb("a1", [P, KD, 2])
        a2 = sb("a2", [P, KD, 2])
        eps = sb("eps", [P, 1])
        acol = sb("acol", [P, 2, NTILE, 8])
        wr = sb("wr", [P, KD, NE])
        wg16 = sb("wg16", [P, KD, 16])
        gq = sb("gq", [P, 1])
        rbias = sb("rbias", [8, 1])
        wend = sb("wend", [P, 8])
        mx = sb("mx", [P, 2, 4])
        rs = sb("rs", [P, 2, 4])
        rstd = sb("rstd", [P, T])
        ARENA = 21760
        arena = sb("arena", [P, ARENA])
        ps = ctx.enter_context(nc.psum_tensor("ps", [P, 8, 512], F32))

        def view(at, *shape):
            n = int(np.prod(shape))
            assert at + n <= ARENA
            a = arena[:, at:at + n]
            if len(shape) == 1:
                return a
            names = "abcd"[:len(shape)]
            return a.rearrange("p (%s) -> p %s" % (" ".join(names), " ".join(names)),
                               **{c: s for c, s in zip(names, shape)})

        ident = cst[:, K_ID:K_ID + P]
        ones = cst[:, K_ONE:K_ONE + P]
        blkones = cst[:, K_BLK:K_BLK + P]
        rotate = cst[:, K_ROT:K_ROT + P]
        cosT = cst[:, K_COS:K_COS + TS]
        sinT = cst[:, K_SIN:K_SIN + TS]
        iota = cst[:, K_IOTA:K_IOTA + CAP_S]

        def tri(d):
            return cst[:, K_TRI + d * P:K_TRI + (d + 1) * P]

        Y_TOP = ARENA - KB * T
        y_ml = view(Y_TOP, KB, T)
        y_na = view(Y_TOP - KB * T, KB, T)
        y_cv = view(Y_TOP - 2 * KB * T, KB, T)
        mq = view(0, HM, T)
        mk = view(2560, HM, T)
        mv = view(5120, NTILE, WB)
        rowA = view(7680, 2, T)
        rowB = view(8960, 2, T)
        rowM = view(10240, 2, T)
        W_AT = 11520
        wmat = view(W_AT, 2, 4, 512)
        row_ig, row_lf, row_t, row_zero = (view(W_AT + T * i, T) for i in range(4))
        rope_tmp = view(W_AT + 2560, TS)
        ktok = view(W_AT + 2048, HM, P)
        vw = view(W_AT + 2560, 2, 129)
        cout = view(W_AT + 2818, 8, 129)
        qi = view(W_AT + 4096, 2, TS)
        emm = view(W_AT + 5120, 2, TS)
        c0s = view(W_AT + 6144, 8, P)
        assert W_AT + 6144 + 1024 <= Y_TOP
        ml_tmp = view(5120, KB, T)
        sig_mo = view(7680, KB, T)
        nq = view(0, KB, T)
        nk = view(2560, KB, T)
        na_tmp = view(10240, KB, T)
        bias_t = view(5120, 2, 4, NKEY)
        prob = view(8192, 2, 4, NKEY)
        vband = view(11264, 2, 2, WB)
        probT = view(13312, 2, NKEY)
        NA_C = 14080
        cks = view(NA_C, KB, P)
        cvs = view(NA_C + 512, WB)
        nvp = view(NA_C + 1024, WB)
        nvst = view(NA_C + 1536, 2, WB)
        assert NA_C + 2560 <= Y_TOP - KB * T
        cc_t = view(5120, KB, T)
        u_pad = view(7680, T + 4)
        conv_t = view(8324, T)
        merged = view(0, KD, T)
        gate_t = view(9728, 2, T)
        prod_t = view(11008, T)
        h_tok = view(0, NTILE, D)
        aff = view(5120, NTILE, NE)
        posT = view(5200, NTILE, NE)
        smax = view(5280, NTILE)
        affT = view(5312, T)
        work = view(5952, T)
        mask_r = view(6592, T)
        pos_r = view(7232, T)
        top8 = view(7872, 8)
        pick_s = view(7936, NTILE - 1, 2, CAP_S)
        pick_p = view(8448, 2, 32)
        gated_s = view(8512, NTILE - 1, 2, CAP_S)
        gated_p = view(9024, 2, 32)
        scat_s = view(9088, TS)
        scat_p = view(9600, TP)
        xg = view(9728, KD, 2, CAP)
        act_t = view(11008, 2, KD, CAP)
        silu_t = view(12288, 2, 4, CAP)
        y_s = view(12928, D)
        y_p = view(13952, D)

        slot_landed = [semaphore(f"slot{s}_landed") for s in range(NSLOT)]
        slot_used = [semaphore(f"slot{s}_used") for s in range(NSLOT)]
        start_in = semaphore("start_in")
        cond_ready = semaphore("cond_ready")
        consts_set = semaphore("consts_set")
        params_in = signal("params_in", 5, 16)
        mod_ps = signal("mod_ps", 1)
        mod_ready = signal("mod_ready", 1)
        scale_ready = signal("scale_ready", 2)
        x_sq = signal("x_sq", 2 * KD)
        x_ss = signal("x_ss", 2)
        x_root = signal("x_root", 2)
        x_normed = signal("x_normed", 2 * KD)
        h_ready = signal("h_ready", 2 * KD)
        layer_x = signal("layer_x", 1)
        unit_full = signal("unit_full", 1)
        act_emptied = signal("act_emptied", 1)
        dve_emptied = signal("dve_emptied", 1)
        rows_ready = signal("rows_ready", 1)
        lf_abs = signal("lf_abs", 1)
        lf_log = signal("lf_log", 1)
        acol_ps = signal("acol_ps", 1)
        acol_ready = signal("acol_ready", 1)
        roped = signal("roped", 2 * HM)
        st_ready = signal("st_ready", 2 * HM)
        bc_ready = signal("bc_ready", 16)
        am_ready = signal("am_ready", 16)
        z_ready = signal("z_ready", 16)
        e_ready = signal("e_ready", 40)
        w_ready = signal("w_ready", 40)
        qi_ready = signal("qi_ready", 8)
        nd_ready = signal("nd_ready", 16)
        h_done = signal("h_done", 16)
        ktok_ps = signal("ktok_ps", 1)
        ktok_ready = signal("ktok_ready", 1)
        vw_ready = signal("vw_ready", 8)
        state_ps = signal("state_ps", 8)
        state_copied = signal("state_copied", 8)
        state_out = signal("state_out", 3, 16)
        sq_ready = signal("sq_ready", 12)
        root_ready = signal("root_ready", 12)
        head_normed = signal("head_normed", 12)
        mo_ready = signal("mo_ready", KB)
        yml_ready = signal("yml_ready", KB)
        nv_staged = signal("nv_staged", NTILE)
        nv_stored = [signal("nv_even_stored", 3, 16), signal("nv_odd_stored", 2, 16)]
        newk_out = signal("newk_out", 1, 16)
        bias_zeroed = signal("bias_zeroed", 1)
        ctx_in = signal("ctx_in", 2, 16)
        band_in = [signal(f"band_in{b}", 4, 16) for b in range(2)]
        bias_in = [signal(f"bias_in{b}", 4, 16) for b in range(2)]
        bias_ready = signal("bias_ready", 8)
        score_ps = signal("score_ps", 40)
        score_max = signal("score_max", 10)
        prob_exp = signal("prob_exp", 10)
        prob_ready = signal("prob_ready", 40)
        probT_ps = signal("probT_ps", 40)
        probT_ready = signal("probT_ready", 40)
        att_ps = signal("att_ps", 5)
        att_copied = signal("att_copied", 5)
        cc_ready = signal("cc_ready", KB)
        conv_done = signal("conv_done", KB)
        gate_ready = signal("gate_ready", 24)
        merged_ready = signal("merged_ready", 24)
        x_mixed = signal("x_mixed", KD)
        tok_ps = signal("tok_ps", 10)
        tok_copied = signal("tok_copied", 10)
        logit_ps = signal("logit_ps", 1)
        logit_shift = signal("logit_shift", 1)
        logit_exp = signal("logit_exp", 1)
        aff_ready = signal("aff_ready", 1)
        affT_ps = signal("affT_ps", 1)
        pos_ready = signal("pos_ready", 1)
        posT_ps = signal("posT_ps", 1)
        posT_ready = signal("posT_ready", 1)
        pick_ready = signal("pick_ready", NPAIR)
        gated_ready = signal("gated_ready", NPAIR)
        scat_ps = signal("scat_ps", NPAIR)
        scat_ready = signal("scat_ready", NPAIR)
        gather_ps = signal("gather_ps", 3 * NPAIR)
        xg_ready = signal("xg_ready", 3 * NPAIR)
        up_ps = signal("up_ps", 2 * NE)
        silu_ready = signal("silu_ready", 2 * NE)
        act_ready = signal("act_ready", 2 * NE)
        down_ps = signal("down_ps", 2 * NE)
        down_copied = signal("down_copied", 2 * NE)
        spread_ps = signal("spread_ps", KD * NPAIR)
        x_added = signal("x_added", KD * NPAIR)
        stored = semaphore("stored")
        pe_passed = semaphore("pe_passed")
        dve_passed = semaphore("dve_passed")
        pool_passed = semaphore("pool_passed")

        units = []

        def unit(kind, count):
            at = len(units)
            units.extend([kind] * count)
            return at

        U_MQ, U_RQ = unit("act", HM), unit("dve", HM)
        U_MK, U_RK = unit("act", HM), unit("dve", HM)
        U_MV = unit("dve", NTILE)
        U_G = unit("dve", 2)
        U_NORM = unit("act", HM)
        U_MO = unit("act", KB)
        U_NQ, U_SQ = unit("act", KB), unit("act", KB)
        U_NK, U_SK = unit("act", KB), unit("act", KB)
        U_NV = unit("dve", NTILE)
        U_CV = unit("cv", 3 * KB)
        U_MG = unit("mg", 2 * 3 * KD)
        U_WO = unit("dve", KD)
        for i in range(KB):
            units[U_CV + 3 * i:U_CV + 3 * i + 3] = ["act", "dve", "dve"]
        for i in range(3 * KD):
            units[U_MG + 2 * i:U_MG + 2 * i + 2] = ["act", "dve"]
        act_before = [sum(1 for k in units[:u] if k == "act") for u in range(len(units) + 1)]
        dve_before = [sum(1 for k in units[:u] if k == "dve") for u in range(len(units) + 1)]
        unit_full.per_layer = len(units)
        act_emptied.per_layer = act_before[-1]
        dve_emptied.per_layer = dve_before[-1]

        def bank(u):
            return 2 * (u % 4)

        def emptied(l, u):
            if units[u] == "act":
                return act_emptied.at(l, act_before[u] + 1)
            return dve_emptied.at(l, dve_before[u] + 1)

        def pair_ps(u):
            b = bank(u)
            return ps[:, b:b + 2, 0:HALF]

        def cols(a):
            return a.rearrange("p (a b) -> p a b", a=2)

        SEG = [(0, TP), (TP, T)]
        steps = [(g, hd, d) for g in range(2) for hd in range(HM) for d in range(2)]
        e_before = [0]
        for g, _, _ in steps:
            e_before.append(e_before[-1] + (4 if g else 1))

        def stiles(g, d):
            if g == 0:
                return [(0, 0, P)]
            if d == 0:
                return [(i, i * P, TS) for i in range(4)]
            return [(i, 0, (i + 1) * P) for i in (3, 2, 1, 0)]

        asteps = [(None, 0), (None, 1)] + [(n, g) for n in range(NBLK) for g in range(2)]

        block = ctx.enter_context(nc.Block())

        @block.sync
        def _(sp):
            def load(l, q, src, i=None, j=None):
                s = (q if i is None else j) % NSLOT
                before = l * SLOT_LAYER[s] + slot_uses(q)
                if i is not None:
                    before = before + i * (PAIR_CHUNKS // NSLOT)
                sp.wait_ge(slot_used[s], before + 1)
                n = src.shape[2]
                dst = ring[:, s, :].rearrange("p (k n) -> p k n", n=n)
                sp.dma_start(dst, src).then_inc(slot_landed[s], 16)

            def rows_of(w, c, n=512):
                return w.rearrange("(k p) n -> p k n", p=P)[:, :, c:c + n]

            with sp.Fori(0, DEPTH) as l:
                ada_l = ada_w[l, :, :]
                win_l = w_in[l, :, :]
                for q in range(ADA_CHUNKS):
                    load(l, q, rows_of(ada_l, 512 * q))
                for q, c in ((R_MQ, C_MQ), (R_MK, C_MK), (R_MV, C_MV), (R_MO, C_MO), (R_NQ, C_NQ),
                             (R_NK, C_NK), (R_NV, C_NV), (R_CC, C_CC), (R_CH, C_CH), (R_CB, C_CB)):
                    load(l, q, rows_of(win_l, c))
                for b, w in enumerate((w_pa, w_pb, w_pc)):
                    load(l, R_MERGE + 3 * b, rows_of(w[l, :, :], 0, D))
                    for j in range(2):
                        load(l, R_MERGE + 3 * b + 1 + j, rows_of(win_l, C_GT + b * D + 512 * j))
                for j in range(2):
                    load(l, R_O + j, rows_of(w_o[l, :, :], 512 * j))
                with sp.Fori(0, NPAIR) as i:
                    for e in range(2):
                        for j, (w, half) in enumerate(((w_gate, 0), (w_up, 0), (w_gate, 1), (w_up, 1),
                                                       (w_down, 0), (w_down, 1))):
                            load(l, R_EXP + 6 * e + j, rows_of(w[l, 2 * i + e, :, :], 512 * half),
                                 i, 6 * e + j)

        @block.gpsimd
        def _(pool):
            pool.dma_start(x[:, :, :], xT.rearrange("(k p) t -> p k t", p=P)).then_inc(start_in, 16)
            pool.dma_start(cst[:, :], const).then_inc(start_in, 16)
            pool.dma_start(silu_c[:, :, :], cond.rearrange("(k p) c -> p k c", p=P)).then_inc(start_in, 16)
            with pool.Fori(0, DEPTH) as l:
                pool.dma_start(par[:, :], prm[l, :, :]).then_inc(params_in.sem, 16)
                pool.dma_start(rowpar[:, :], rowp[l, :, :]).then_inc(params_in.sem, 16)
                pool.dma_start(wr[:, :, :], w_router[l, :, :].rearrange("(k p) e -> p k e", p=P))\
                    .then_inc(params_in.sem, 16)
                pool.dma_start(wg16[:, :, :], w_in[l, :, :].rearrange("(k p) n -> p k n", p=P)[:, :, C_G:C_G + 16])\
                    .then_inc(params_in.sem, 16)
                pool.dma_start(c0s[:, :, :], c0[l, :, :, :].rearrange("g d v -> d g v")).then_inc(params_in.sem, 16)
                pool.wait_ge(*rows_ready.at(l, 1))
                pool.sem_inc(pool_passed, 1)
                pool.dma_start(new_m[l, 0:HM, :], rowM[0:HM, 0, TP - 1:TP]).then_inc(state_out.sem, 16)
                pool.dma_start(new_m[l, HM:8, :], rowM[HM:8, 1, 0:1]).then_inc(state_out.sem, 16)
                pool.wait_ge(*state_copied.at(l, 8))
                pool.sem_inc(pool_passed, 1)
                pool.dma_start(new_cn[l, :, :, :].rearrange("g d v -> d g v"), cout).then_inc(state_out.sem, 16)
                pool.wait_ge(*h_done.at(l, 16))
                pool.sem_inc(pool_passed, 1)
                pool.dma_start(cks[:, :, :], ckT[l, :, :].rearrange("(j p) t -> p j t", p=P)).then_inc(ctx_in.sem, 16)
                pool.dma_start(cvs, cv[l, :, :]).then_inc(ctx_in.sem, 16)
                for t in range(NTILE):
                    pool.wait_ge(*nv_staged.at(l, t + 1))
                    pool.sem_inc(pool_passed, 1)
                    if t == 0:
                        pool.wait_ge(*head_normed.at(l, 12))
                        pool.sem_inc(pool_passed, 1)
                        pool.dma_start(new_k[l, :, :].rearrange("(j p) t -> p j t", p=P), nk[:, :, 0:TP])\
                            .then_inc(newk_out.sem, 16)
                        pool.dma_start(new_v[l, :, :], nvp).then_inc(nv_stored[0].sem, 16)
                    else:
                        pool.dma_start(nv_dram[(t - 1) * P:t * P, :], nvst[:, t % 2, :])\
                            .then_inc(nv_stored[t % 2].sem, 16)
                pool.wait_ge(*nv_stored[0].at(l, 3))
                pool.wait_ge(*nv_stored[1].at(l, 2))
                pool.wait_ge(*bias_zeroed.at(l, 1))
                pool.sem_inc(pool_passed, 1)
                nv_grid = nv_dram.rearrange("(g i c) f -> g i c f", g=2, c=GRID)

                def band_load(n):
                    for g in range(2):
                        pool.dma_start(vband[:, n % 2, g, :], nv_grid[g, :, BAND0[n]:BAND0[n] + KBAND, :])\
                            .then_inc(band_in[n % 2].sem, 16)

                def bias_load(s):
                    n, g = asteps[s + 2]
                    pool.dma_start(bias_t[:, s % 2, :, 0:WINK], biasT[l, n, :, 4 * g:4 * g + 4, :])\
                        .then_inc(bias_in[s % 2].sem, 16)

                band_load(0)
                band_load(1)
                bias_load(0)
                bias_load(1)
                for s in range(8):
                    n, g = asteps[s + 2]
                    pool.wait_ge(*bias_in[s % 2].at(l, s // 2 + 1))
                    pool.tensor_tensor(
                        bias_t[:, s % 2, :, 0:WINK].rearrange("p a (i j) -> p a i j", j=KBAND),
                        bias_t[:, s % 2, :, 0:WINK].rearrange("p a (i j) -> p a i j", j=KBAND),
                        cst[:, K_MASK + n * KBAND:K_MASK + (n + 1) * KBAND][:, None, None, :]
                        .to_broadcast([P, 4, ROWS, KBAND]), ALU.add).then_inc(bias_ready.sem, 1)
                    if 1 <= s <= 6:
                        pool.wait_ge(*score_max.at(l, s + 2))
                        pool.sem_inc(pool_passed, 1)
                        bias_load(s + 1)
                    if s in (3, 5):
                        pool.wait_ge(*att_ps.at(l, (s - 1) // 2 + 1))
                        pool.sem_inc(pool_passed, 1)
                        band_load((s - 1) // 2 + 1)
                pool.wait_ge(*newk_out.at(l, 1))
                pool.wait_ge(*layer_x.at(l, 1))
            pool.dma_start(yT.rearrange("(k p) t -> p k t", p=P), x[:, :, :]).then_inc(stored, 16)
            pool.wait_ge(stored, 16)
            pool.wait_ge(*state_out.at(DEPTH - 1, 3))
            pool.wait_ge(*nv_stored[0].at(DEPTH - 1, 3))
            pool.wait_ge(*newk_out.at(DEPTH - 1, 1))

        @block.tensor
        def _(pe):
            def chunk(l, q, n, i=None, j=None):
                s = (q if i is None else j) % NSLOT
                before = l * SLOT_LAYER[s] + slot_uses(q)
                if i is not None:
                    before = before + i * (PAIR_CHUNKS // NSLOT)
                pe.wait_ge(slot_landed[s], (before + 1) * 16)
                return s, ring[:, s, :].rearrange("p (k n) -> p k n", n=n)

            def free_unit(l, u):
                if u >= 4:
                    pe.wait_ge(*emptied(l, u - 4))

            def tile_unit(l, u, weights, acts, nk):
                free_unit(l, u)
                for half in range(2):
                    for k in range(nk):
                        last = pe.matmul(ps[:, bank(u) + half, 0:HALF], weights(k),
                                         acts(k)[:, half * HALF:(half + 1) * HALF],
                                         start=(k == 0), stop=(k == nk - 1))
                return last.then_inc(unit_full.sem, 1)

            def project(l, q, u0, stride=1):
                s, w = chunk(l, q, 512)
                for f in range(4):
                    last = tile_unit(l, u0 + stride * f, lambda k: w[:, k, f * P:(f + 1) * P],
                                     lambda k: h[:, k, :], KD)
                release(s)

            def release(s):
                pe.drain()
                pe.sem_inc(slot_used[s], 1)

            def project_tokens(l, q, u0):
                s, w = chunk(l, q, 512)
                for t in range(NTILE):
                    free_unit(l, u0 + t)
                    for k in range(KD):
                        last = pe.matmul(ps[:, bank(u0 + t), :], h[:, k, t * P:(t + 1) * P], w[:, k, :],
                                         start=(k == 0), stop=(k == KD - 1))
                    last.then_inc(unit_full.sem, 1)
                release(s)

            def rope_rows(l, u0, src, first):
                for i in range(HM):
                    free_unit(l, u0 + i)
                    pe.wait_ge(*emptied(l, u0 - HM + i))
                    pe.matmul(ps[:, bank(u0 + i), :], rotate, src[:, i, TP:T], start=True, stop=True)\
                        .then_inc(unit_full.sem, 1)

            def head_sums(l, u0, n0, lhs, tmp):
                for i in range(KB):
                    pe.wait_ge(*sq_ready.at(l, n0 + i + 1))
                    tile_unit(l, u0 + i, lambda k: lhs, lambda k: tmp[:, i, :], 1)

            def modulation(l):
                for q in range(ADA_CHUNKS):
                    s, w = chunk(l, q, 512)
                    for f in range(4):
                        for k in range(KD):
                            last = pe.matmul(ps[:, 0, 2 * (4 * q + f):2 * (4 * q + f) + 2],
                                             w[:, k, f * P:(f + 1) * P], silu_c[:, k, :],
                                             start=(k == 0), stop=(k == KD - 1))
                    last.then_inc(slot_used[s], 1)

            def x_sums(l, r):
                for k in range(KD):
                    pe.wait_ge(*x_sq.at(l, r * KD + k + 1))
                    for half in range(2):
                        last = pe.matmul(ps[:, 2 + half, 0:HALF], ones, h[:, k, half * HALF:(half + 1) * HALF],
                                         start=(k == 0), stop=(k == KD - 1))
                last.then_inc(x_ss.sem, 1)

            def mlstm(l):
                def scores(s):
                    g, hd, d = steps[s]
                    n = g * HM + hd
                    if s:
                        pe.wait_ge(*w_ready.at(l, e_before[s]))
                    lo, hi = SEG[g]
                    for i in range((hi - lo) // P):
                        last = pe.matmul(ps[:, i, 0:hi - lo], mk[:, hd, lo + i * P:lo + (i + 1) * P],
                                         mq[:, hd, lo:hi], start=True, stop=True)
                    last.then_inc(st_ready.sem, 1)

                def broadcasts(s):
                    g, hd, d = steps[s]
                    lo, hi = SEG[g]
                    if s:
                        pe.wait_ge(*w_ready.at(l, e_before[s]))
                        pe.wait_ge(*am_ready.at(l, s))
                    pick = ident[0:8, d * HM + hd:d * HM + hd + 1].to_broadcast([8, P])
                    pe.matmul(ps[:, 4, 0:hi - lo], pick, rowB[0:8, d, lo:hi], start=True, stop=True)
                    pe.matmul(ps[:, 5, 0:hi - lo], pick, rowM[0:8, d, lo:hi], start=True, stop=True)\
                        .then_inc(bc_ready.sem, 1)

                def sums(s):
                    g, hd, d = steps[s]
                    lo, hi = SEG[g]
                    tiles = stiles(g, d)
                    if s:
                        pe.wait_ge(*h_done.at(l, s))
                    for j, (i, t0, t1) in enumerate(tiles):
                        pe.wait_ge(*w_ready.at(l, e_before[s] + j + 1))
                        w = wmat[:, s % 2, i, t0:t1]
                        end = g == 0
                        pe.matmul(ps[:, 6, t0:t1], mv[:, lo // P + i, hd * P:(hd + 1) * P], w,
                                  start=(j == 0), stop=end)
                        last = pe.matmul(ps[:, 7, t0:t1], ones, w, start=(j == 0), stop=end)
                    if g:
                        pe.wait_ge(*qi_ready.at(l, s - 8 + 1))
                        pe.matmul(ps[:, 6, :], c0s[:, d * HM + hd, :], qi[:, s % 2, :], start=False, stop=True)
                        last = pe.matmul(ps[:, 7, :],
                                         par[:, Q_N0 + d * HM + hd:Q_N0 + d * HM + hd + 1].to_broadcast([P, P]),
                                         qi[:, s % 2, :], start=False, stop=True)
                    last.then_inc(nd_ready.sem, 1)

                def final_states():
                    pe.wait_ge(*w_ready.at(l, e_before[8]))
                    for hd in range(HM):
                        last = pe.transpose(ps[:, 0, hd * P:(hd + 1) * P], mk[:, hd, 0:TP], ident)
                    last.then_inc(ktok_ps.sem, 1)
                    pe.wait_ge(*ktok_ready.at(l, 1))
                    for g in range(8):
                        hd = g % HM
                        pe.wait_ge(*vw_ready.at(l, g + 1))
                        if g >= 2:
                            pe.wait_ge(*state_copied.at(l, g - 1))
                        pe.matmul(ps[:, 1 + g % 2, 0:129], ktok[:, hd, :], vw[:, g % 2, :], start=True, stop=True)\
                            .then_inc(state_ps.sem, 1)
                    pe.wait_ge(*state_copied.at(l, 8))

                for s in range(16):
                    if s == 8:
                        sums(7)
                        final_states()
                    if steps[s][2] == 0:
                        scores(s)
                    broadcasts(s)
                    if s and s != 8:
                        sums(s - 1)
                sums(15)

            def attention(l):
                def scores(s):
                    n, g = asteps[s]
                    for a in range(4):
                        hd = 4 * g + a
                        lo = DN * (hd % 2)
                        j = hd // 2
                        if s:
                            pe.wait_ge(*score_max.at(l, s))
                        if n is None:
                            last = pe.matmul(ps[:, a, 0:P], nq[lo:lo + DN, j, 0:TP], nk[lo:lo + DN, j, 0:TP],
                                             start=True, stop=True)
                        else:
                            kg = nk[lo:lo + DN, j, TP:T].rearrange("p (r c) -> p r c", c=GRID)
                            qblk = nq[lo:lo + DN, j, TP + n * P:TP + (n + 1) * P]
                            pe.matmul(ps[:, a, 0:WINK], qblk, kg[:, :, BAND0[n]:BAND0[n] + KBAND],
                                      start=True, stop=True)
                            last = pe.matmul(ps[:, a, WINK:NKEY], qblk, cks[lo:lo + DN, j, :],
                                             start=True, stop=True)
                        last.then_inc(score_ps.sem, 1)

                def outputs(s):
                    n, g = asteps[s]
                    nb = s // 2
                    nt = 1 if n is None else 3

                    def turn(a):
                        r = 4 * s + a
                        pe.wait_ge(*prob_ready.at(l, r + 1))
                        if r >= 2:
                            pe.wait_ge(*probT_ready.at(l, r - 1))
                        for i in range(nt):
                            last = pe.transpose(ps[:, 4 + r % 2, i * P:(i + 1) * P],
                                                prob[:, s % 2, a, i * P:(i + 1) * P], ident)
                        last.then_inc(probT_ps.sem, 1)

                    def weigh(a):
                        r = 4 * s + a
                        hd = 4 * g + a
                        lo = DN * (hd % 2)
                        pe.wait_ge(*probT_ready.at(l, r + 1))
                        for i in range(nt):
                            if n is None:
                                v = nvp[:, hd * DN:(hd + 1) * DN]
                            elif i < 2:
                                v = vband[:, n % 2, i, hd * DN:(hd + 1) * DN]
                            else:
                                v = cvs[:, hd * DN:(hd + 1) * DN]
                            last = pe.matmul(ps[lo:lo + DN, 6 + nb % 2, (hd // 2) * P:(hd // 2 + 1) * P], v,
                                             probT[:, r % 2, i * P:(i + 1) * P],
                                             start=(i == 0), stop=(i == nt - 1))
                        return last

                    if g == 0 and nb >= 2:
                        pe.wait_ge(*att_copied.at(l, nb - 1))
                    if n is not None and g == 0:
                        pe.wait_ge(*band_in[n % 2].at(l, 2 * (n // 2) + 2))
                    turn(0)
                    for a in range(4):
                        if a < 3:
                            turn(a + 1)
                        last = weigh(a)
                    if g == 1:
                        last.then_inc(att_ps.sem, 1)

                for s in range(10):
                    if s == 2:
                        pe.wait_ge(*ctx_in.at(l, 2))
                    scores(s)
                    if s:
                        outputs(s - 1)
                outputs(9)

            def convolution(l):
                slots = [chunk(l, q, 512) for q in (R_CC, R_CH, R_CB)]
                for f in range(KB):
                    for j, (s, w) in enumerate(slots):
                        tile_unit(l, U_CV + 3 * f + j, lambda k: w[:, k, f * P:(f + 1) * P],
                                  lambda k: h[:, k, :], KD)
                pe.drain()
                for s, _ in slots:
                    pe.sem_inc(slot_used[s], 1)

            def merge(l):
                for b, y in enumerate((y_ml, y_cv, y_na)):
                    if b == 0:
                        pe.wait_ge(*yml_ready.at(l, KB))
                    if b == 1:
                        pe.wait_ge(*conv_done.at(l, KB))
                    if b == 2:
                        pe.wait_ge(*att_copied.at(l, 5))
                    sp_, wp = chunk(l, R_MERGE + 3 * b, D)
                    for j in range(2):
                        sg, wgt = chunk(l, R_MERGE + 3 * b + 1 + j, 512)
                        for f in range(4):
                            dt = 4 * j + f
                            u = U_MG + 2 * (b * KD + dt)
                            tile_unit(l, u, lambda k: wgt[:, k, f * P:(f + 1) * P], lambda k: h[:, k, :], KD)
                            tile_unit(l, u + 1, lambda k: wp[:, k, dt * P:(dt + 1) * P], lambda k: y[:, k, :], KB)
                        release(sg)
                    release(sp_)

            def mix_out(l):
                pe.wait_ge(*merged_ready.at(l, 24))
                for j in range(2):
                    s, w = chunk(l, R_O + j, 512)
                    for f in range(4):
                        tile_unit(l, U_WO + 4 * j + f, lambda k: w[:, k, f * P:(f + 1) * P],
                                  lambda k: merged[:, k, :], KD)
                    release(s)

            def route(l):
                for t in range(NTILE):
                    for k in range(KD):
                        last = pe.matmul(ps[:, 0, t * NE:(t + 1) * NE], h[:, k, t * P:(t + 1) * P], wr[:, k, :],
                                         start=(k == 0), stop=(k == KD - 1))
                last.then_inc(logit_ps.sem, 1)
                for n in range(2 * NTILE):
                    t, half = n // 2, n % 2
                    if n >= 4:
                        pe.wait_ge(*tok_copied.at(l, n - 3))
                    for k in range(4):
                        last = pe.transpose(ps[:, 4 + n % 4, k * P:(k + 1) * P],
                                            h[:, 4 * half + k, t * P:(t + 1) * P], ident)
                    last.then_inc(tok_ps.sem, 1)
                pe.wait_ge(*aff_ready.at(l, 1))
                for t in range(NTILE):
                    last = pe.transpose(ps[0:NE, 1 + t // 4, (t % 4) * P:(t % 4 + 1) * P], aff[:, t, :], ident)
                last.then_inc(affT_ps.sem, 1)
                pe.wait_ge(*pos_ready.at(l, 1))
                pe.sem_inc(pe_passed, 1)
                for t in range(NTILE):
                    last = pe.transpose(ps[:, 3, t * NE:(t + 1) * NE], pos_r[0:NE, t * P:(t + 1) * P],
                                        ident[0:NE, 0:NE])
                last.then_inc(posT_ps.sem, 1)

            def experts(l, i):
                n = l * NPAIR + i
                pe.wait_ge(pick_ready.sem, n + 1)
                for dt in range(KD):
                    out = ps[:, dt // 3, (dt % 3) * 2 * CAP:(dt % 3 + 1) * 2 * CAP]\
                        .rearrange("p (e c) -> p e c", e=2)
                    for t in range(1, NTILE):
                        last = pe.matmul(out[:, :, 0:CAP_S], h_tok[:, t, dt * P:(dt + 1) * P],
                                         pick_s[:, t - 1, :, :], start=(t == 1), stop=(t == NTILE - 1))
                    last = pe.matmul(out[:, :, CAP_S:CAP], h_tok[:, 0, dt * P:(dt + 1) * P],
                                     pick_p[:, :, 0:CAP_P], start=True, stop=True)
                    if dt % 3 == 2 or dt == KD - 1:
                        last.then_inc(gather_ps.sem, 1)
                pe.wait_ge(gated_ready.sem, n + 1)
                for t in range(NTILE - 1):
                    pe.transpose(ps[:, 7, t * P:(t + 1) * P],
                                 gated_s[:, t, :, :].rearrange("p e c -> p (e c)"), ident)
                pe.transpose(ps[0:64, 3, 0:TP], gated_p[:, :, :].rearrange("p e c -> p (e c)"), ident)\
                    .then_inc(scat_ps.sem, 1)
                for e in range(2):
                    m = n * 2 + e
                    for half in range(2):
                        c = 6 * e + 2 * half
                        sg, wg = chunk(l, R_EXP + c, 512, i, c)
                        su, wu = chunk(l, R_EXP + c + 1, 512, i, c + 1)
                        if half == 0 and e == 0:
                            pe.wait_ge(xg_ready.sem, 3 * n + 3)
                            pe.wait_ge(scat_ready.sem, n + 1)
                        if half == 0 and e == 1:
                            pe.wait_ge(act_ready.sem, 2 * m - 1)
                        if half == 1 and e == 1:
                            pe.wait_ge(act_ready.sem, 2 * m)
                        for b, w, s in ((3 + 2 * half, wg, sg), (4 + 2 * half, wu, su)):
                            for f in range(4):
                                for k in range(KD):
                                    last = pe.matmul(ps[:, b, f * CAP:(f + 1) * CAP], w[:, k, f * P:(f + 1) * P],
                                                     xg[:, k, e, :], start=(k == 0), stop=(k == KD - 1))
                            last.then_inc(slot_used[s], 1)
                        pe.drain()
                        pe.sem_inc(up_ps.sem, 1)
                    for half in range(2):
                        c = 6 * e + 4 + half
                        s, w = chunk(l, R_EXP + c, 512, i, c)
                        pe.wait_ge(act_ready.sem, 2 * m + 1 + 1)
                        if e == 1:
                            pe.wait_ge(down_copied.sem, 2 * m - 1 + half)
                        for f in range(KD):
                            last = pe.matmul(ps[0:CAP, half, :], act_t[:, e, f, :], w[:, f, :],
                                             start=(f == 0), stop=(f == KD - 1))
                        last.then_inc(slot_used[s], 1)
                        pe.drain()
                        pe.sem_inc(down_ps.sem, 1)
                pe.wait_ge(down_copied.sem, 4 * n + 4)
                for dt in range(KD):
                    b = 2 if dt % 2 == 0 else 6
                    q = 7 if dt % 2 == 0 else 5
                    if dt >= 2:
                        pe.wait_ge(x_added.sem, KD * n + dt - 1)
                    pe.matmul(ps[:, b, :], y_s[:, dt * P:(dt + 1) * P], scat_s, start=True, stop=True)
                    pe.matmul(ps[:, q, 0:TP], y_p[0:64, dt * P:(dt + 1) * P], scat_p[0:64, :],
                              start=True, stop=True).then_inc(spread_ps.sem, 1)
                pe.wait_ge(x_added.sem, KD * n + KD)

            for s in range(NSLOT):
                pe.sem_inc(slot_used[s], 1)
            pe.wait_ge(cond_ready, 1)
            with pe.Fori(0, DEPTH) as l:
                modulation(l)
                pe.drain()
                pe.sem_inc(mod_ps.sem, 1)
                x_sums(l, 0)
                pe.wait_ge(*h_ready.at(l, KD))
                project(l, R_MQ, U_MQ)
                rope_rows(l, U_RQ, mq, 0)
                project(l, R_MK, U_MK)
                rope_rows(l, U_RK, mk, HM)
                project_tokens(l, R_MV, U_MV)
                for j in range(2):
                    u = U_G + j
                    free_unit(l, u)
                    for half in range(2):
                        for k in range(KD):
                            last = pe.matmul(ps[0:8, bank(u) + half, 0:HALF], wg16[:, k, 8 * j:8 * j + 8],
                                             h[:, k, half * HALF:(half + 1) * HALF],
                                             start=(k == 0), stop=(k == KD - 1))
                    last.then_inc(unit_full.sem, 1)
                pe.wait_ge(*rows_ready.at(l, 1))
                pe.wait_ge(*roped.at(l, 2 * HM))
                pe.sem_inc(pe_passed, 1)
                for d in range(2):
                    for t in range(NTILE):
                        last = pe.transpose(ps[:, 0, (d * NTILE + t) * 8:(d * NTILE + t + 1) * 8],
                                            rowA[0:8, d, t * P:(t + 1) * P], ident[0:8, 0:8])
                last.then_inc(acol_ps.sem, 1)
                pe.wait_ge(*acol_ready.at(l, 1))
                mlstm(l)
                pe.wait_ge(*h_done.at(l, 16))
                head_sums(l, U_NORM, 0, ones, ml_tmp)
                project(l, R_MO, U_MO)
                project(l, R_NQ, U_NQ)
                head_sums(l, U_SQ, HM, blkones, na_tmp)
                project(l, R_NK, U_NK)
                head_sums(l, U_SK, HM + KB, blkones, na_tmp)
                project_tokens(l, R_NV, U_NV)
                pe.wait_ge(*head_normed.at(l, 12))
                pe.wait_ge(*emptied(l, U_NV + NTILE - 1))
                attention(l)
                pe.wait_ge(*att_copied.at(l, 5))
                convolution(l)
                merge(l)
                mix_out(l)
                pe.wait_ge(*x_mixed.at(l, KD))
                x_sums(l, 1)
                pe.wait_ge(*h_ready.at(l, 2 * KD))
                route(l)
                pe.wait_ge(*tok_copied.at(l, 10))
                pe.wait_ge(*posT_ready.at(l, 1))
                pe.sem_inc(pe_passed, 1)
                with pe.Fori(0, NPAIR) as i:
                    experts(l, i)

        @block.scalar
        def _(act):
            def square_x(l, r):
                for k in range(KD):
                    act.activation(h[:, k, :], x[:, k, :], ACT.Square).then_inc(x_sq.sem, 1)

            def norm_x(l, r):
                act.wait_ge(*x_ss.at(l, r + 1))
                act.activation(cols(rstd[:, :]), ps[:, 2:4, 0:HALF], ACT.Sqrt, bias=eps[:, :], scale=1.0 / D)\
                    .then_inc(x_root.sem, 1)
                act.wait_ge(*scale_ready.at(l, 2))
                a, b0 = (a1, 0) if r == 0 else (a2, 24)
                for k in range(KD):
                    act.wait_ge(*x_normed.at(l, r * KD + k + 1))
                    for g, (lo, hi) in enumerate(SEG):
                        last = act.activation(h[:, k, lo:hi], h[:, k, lo:hi], ACT.Identity,
                                              bias=mod[:, b0 + k, g:g + 1], scale=a[:, k, g:g + 1])
                    last.then_inc(h_ready.sem, 1)

            def empty(l, u, out, bias, func=ACT.Identity, scale=1.0):
                act.wait_ge(*unit_full.at(l, u + 1))
                return act.activation(cols(out), pair_ps(u), func, bias=bias, scale=scale)\
                    .then_inc(act_emptied.sem, 1)

            def empty_queries(l, u, out, bias):
                act.wait_ge(*unit_full.at(l, u + 1))
                b = bank(u)
                act.activation(out[:, 0:TP], ps[:, b, 0:TP], ACT.Identity, bias=bias)
                blocks = out[:, TP:T].rearrange("p (n r c) -> p r n c", n=NBLK, r=ROWS)
                cut = (HALF - TP) // GRID
                for r0, r1, src in ((0, cut, ps[:, b, TP:HALF]), (cut, ROWS, ps[:, b + 1, 0:HALF])):
                    src = src.rearrange("p (r n c) -> p r n c", n=NBLK, c=QB)
                    for r in range(r0, r1):
                        last = act.activation(blocks[:, r, :, :], src[:, r - r0, :, :], ACT.Identity, bias=bias)
                last.then_inc(act_emptied.sem, 1)

            def bcol(i):
                return par[:, Q_BIN + i:Q_BIN + i + 1]

            def head_roots(l, u0, tmp, scale):
                for i in range(KB):
                    empty(l, u0 + i, tmp[:, i, :], eps[:, :], ACT.Sqrt, scale)
                    act.drain()
                    act.sem_inc(root_ready.sem, 1)

            def mlstm(l):
                for s, (g, hd, d) in enumerate(steps):
                    if s == 8:
                        act.wait_ge(*ktok_ps.at(l, 1))
                        act.activation(ktok, ps[:, 0, :].rearrange("p (a b) -> p a b", a=HM), ACT.Copy,
                                       scale=ML_SCALE).then_inc(ktok_ready.sem, 1)
                        for c in range(8):
                            act.wait_ge(*state_ps.at(l, c + 1))
                            act.activation(cout[:, c, :], ps[:, 1 + c % 2, 0:129], ACT.Copy)\
                                .then_inc(state_copied.sem, 1)
                    if s == 9:
                        act.wait_ge(*state_out.at(l, 3))
                    lo, hi = SEG[g]
                    n = hi - lo
                    act.wait_ge(*bc_ready.at(l, s + 1))
                    act.wait_ge(*z_ready.at(l, s + 1))
                    if s >= 2:
                        act.wait_ge(*nd_ready.at(l, s - 1))
                        act.wait_ge(*h_done.at(l, s - 1))
                    if g:
                        act.activation(qi[:, s % 2, :], ps[:, 4, :], ACT.Exp,
                                       bias=par[:, Q_M0 + d * HM + hd:Q_M0 + d * HM + hd + 1])
                    else:
                        end = TP - 1 if d == 0 else 0
                        act.activation(wend[:, d * HM + hd:d * HM + hd + 1], ps[:, 4, end:end + 1], ACT.Exp,
                                       bias=acol[:, d, 0, d * HM + hd:d * HM + hd + 1])
                    act.activation(emm[:, s % 2, 0:n], ps[:, 5, 0:n], ACT.Exp, scale=-1.0).then_inc(am_ready.sem, 1)
                    for i, t0, t1 in stiles(g, d):
                        bias = acol[:, d, lo // P + i, d * HM + hd:d * HM + hd + 1]
                        dg = i * P
                        last = act.activation(wmat[:, s % 2, i, dg:dg + P], wmat[:, s % 2, i, dg:dg + P], ACT.Exp,
                                              bias=bias)
                        a, b = (dg + P, t1) if d == 0 else (t0, dg)
                        if b > a:
                            last = act.activation(wmat[:, s % 2, i, a:b], ps[:, 4, a:b], ACT.Exp, bias=bias)
                        last.then_inc(e_ready.sem, 1)

            def attention(l):
                def exps(s):
                    n, g = asteps[s]
                    w = TP if n is None else NKEY
                    act.wait_ge(*score_max.at(l, s + 1))
                    for a in range(4):
                        last = act.activation(prob[:, s % 2, a, 0:w], prob[:, s % 2, a, 0:w], ACT.Exp,
                                              bias=mx[:, s % 2, a:a + 1], accum_out=rs[:, s % 2, a:a + 1])
                    last.then_inc(prob_exp.sem, 1)

                def copies(s):
                    w = TP if asteps[s][0] is None else NKEY
                    for a in range(4):
                        r = 4 * s + a
                        act.wait_ge(*probT_ps.at(l, r + 1))
                        act.activation(probT[:, r % 2, 0:w], ps[:, 4 + r % 2, 0:w], ACT.Copy)\
                            .then_inc(probT_ready.sem, 1)

                for s in range(10):
                    exps(s)
                    if s:
                        copies(s - 1)
                copies(9)

            act.wait_ge(start_in, 48)
            act.activation(silu_c[:, :, :], silu_c[:, :, :], ACT.Silu).then_inc(cond_ready, 1)
            act.wait_ge(consts_set, 1)
            with act.Fori(0, DEPTH) as l:
                act.wait_ge(*params_in.at(l, 5))
                square_x(l, 0)
                norm_x(l, 0)
                for i in range(HM):
                    empty(l, U_MQ + i, mq[:, i, :], bcol(B_MQ + i))
                for i in range(HM):
                    empty(l, U_MK + i, mk[:, i, :], bcol(B_MK + i))
                act.wait_ge(*lf_abs.at(l, 1))
                act.activation(row_t[0:8, :], row_t[0:8, :], ACT.Exp, scale=-1.0)
                act.drain()
                act.activation(row_t[0:8, :], row_t[0:8, :], ACT.Ln, bias=1.0).then_inc(lf_log.sem, 1)
                act.wait_ge(*acol_ps.at(l, 1))
                act.activation(acol[:, :, :, :].rearrange("p a b c -> p (a b c)"), ps[:, 0, 0:80], ACT.Copy)\
                    .then_inc(acol_ready.sem, 1)
                act.drain()
                mlstm(l)
                act.wait_ge(*h_done.at(l, 16))
                for i in range(HM):
                    act.activation(ml_tmp[:, i, :], y_ml[:, i, :], ACT.Square).then_inc(sq_ready.sem, 1)
                head_roots(l, U_NORM, ml_tmp, 1.0 / P)
                for i in range(KB):
                    empty(l, U_MO + i, sig_mo[:, i, :], bcol(B_MO + i), ACT.Sigmoid)
                for u0, us, b0, dst in ((U_NQ, U_SQ, B_NQ, nq), (U_NK, U_SK, B_NK, nk)):
                    for i in range(KB):
                        if dst is nk:
                            empty(l, u0 + i, dst[:, i, :], bcol(b0 + i))
                        else:
                            empty_queries(l, u0 + i, dst[:, i, :], bcol(b0 + i))
                    act.drain()
                    if dst is nk:
                        act.wait_ge(*head_normed.at(l, HM + KB))
                    for i in range(KB):
                        act.activation(na_tmp[:, i, :], dst[:, i, :], ACT.Square).then_inc(sq_ready.sem, 1)
                    head_roots(l, us, na_tmp, 1.0 / DN)
                attention(l)
                for i in range(KB):
                    empty(l, U_CV + 3 * i, cc_t[:, i, :], bcol(B_CC + i))
                for i in range(3 * KD):
                    if i >= 2:
                        act.wait_ge(*merged_ready.at(l, i - 1))
                    empty(l, U_MG + 2 * i, gate_t[:, i % 2, :], bcol(B_GT + i), ACT.Sigmoid)
                act.wait_ge(*x_mixed.at(l, KD))
                square_x(l, 1)
                norm_x(l, 1)
                act.wait_ge(*logit_shift.at(l, 1))
                act.activation(aff[:, :, :], aff[:, :, :], ACT.Exp).then_inc(logit_exp.sem, 1)
                for n in range(2 * NTILE):
                    t, half = n // 2, n % 2
                    act.wait_ge(*tok_ps.at(l, n + 1))
                    act.activation(h_tok[:, t, half * 512:(half + 1) * 512], ps[:, 4 + n % 4, :], ACT.Copy)\
                        .then_inc(tok_copied.sem, 1)
                with act.Fori(0, NPAIR) as i:
                    n = l * NPAIR + i
                    for j in range(3):
                        act.wait_ge(gather_ps.sem, 3 * n + j + 1)
                        w = 3 if j < 2 else 2
                        act.activation(xg[:, 3 * j:3 * j + w, :, :].rearrange("p a e c -> p (a e c)"),
                                       ps[:, j, 0:w * 2 * CAP], ACT.Copy).then_inc(xg_ready.sem, 1)
                    for e in range(2):
                        m = 2 * n + e
                        for half in range(2):
                            act.wait_ge(up_ps.sem, 2 * m + half + 1)
                            act.activation(silu_t[:, half, :, :].rearrange("p f c -> p (f c)"),
                                           ps[:, 3 + 2 * half, 0:4 * CAP], ACT.Silu).then_inc(silu_ready.sem, 1)
                        for half in range(2):
                            act.wait_ge(down_ps.sem, 2 * m + half + 1)
                            act.activation(y_s[64 * e:64 * e + CAP_S, half * 512:(half + 1) * 512],
                                           ps[0:CAP_S, half, :], ACT.Copy)
                            act.activation(y_p[32 * e:32 * e + CAP_P, half * 512:(half + 1) * 512],
                                           ps[CAP_S:CAP, half, :], ACT.Copy).then_inc(down_copied.sem, 1)
                act.wait_ge(*layer_x.at(l, 1))

        @block.vector
        def _(dve):
            def root_x(l, r):
                dve.wait_ge(*x_root.at(l, r + 1))
                dve.reciprocal(rstd[:, :], rstd[:, :])
                dve.drain()
                for k in range(KD):
                    dve.tensor_tensor(h[:, k, :], x[:, k, :], rstd[:, :], ALU.mult).then_inc(x_normed.sem, 1)

            def rope(l, u0, dst):
                for i in range(HM):
                    dve.wait_ge(*unit_full.at(l, u0 + i + 1))
                    dve.tensor_tensor(rope_tmp, ps[:, bank(u0 + i), :], sinT, ALU.mult).then_inc(dve_emptied.sem, 1)
                    dve.tensor_tensor(dst[:, i, TP:T], dst[:, i, TP:T], cosT, ALU.mult)
                    dve.drain()
                    dve.tensor_tensor(dst[:, i, TP:T], dst[:, i, TP:T], rope_tmp, ALU.add).then_inc(roped.sem, 1)
                    dve.drain()

            def gate_rows(l):
                dve.tensor_scalar(rbias[:, :], rowpar[:, 1:2], rowpar[:, 2:3], None, ALU.add)
                dve.memset(row_zero[0:8, :], 0.0)
                dve.drain()
                dve.wait_ge(*unit_full.at(l, U_G + 1))
                dve.tensor_scalar(cols(row_ig[0:8, :]), ps[0:8, bank(U_G):bank(U_G) + 2, 0:HALF], rowpar[:, 0:1],
                                  None, ALU.add).then_inc(dve_emptied.sem, 1)
                b = bank(U_G + 1)
                dve.wait_ge(*unit_full.at(l, U_G + 2))
                dve.tensor_scalar(cols(row_lf[0:8, :]), ps[0:8, b:b + 2, 0:HALF], rbias[:, :], None, ALU.add)\
                    .then_inc(dve_emptied.sem, 1)
                dve.drain()
                dve.scalar_tensor_tensor(row_t[0:8, :], row_lf[0:8, :], -1.0, row_lf[0:8, :], ALU.mult, ALU.max)\
                    .then_inc(lf_abs.sem, 1)
                dve.wait_ge(*lf_log.at(l, 1))
                dve.scalar_tensor_tensor(row_lf[0:8, :], row_lf[0:8, :], 0.0, row_t[0:8, :], ALU.min, ALU.subtract)
                dve.drain()
                for d in range(2):
                    for g, (lo, hi) in enumerate(SEG):
                        order = slice(lo, hi) if d == 0 else (slice(hi - 1, lo - 1 if lo else None, -1))
                        dve.tensor_tensor_scan(rowB[0:8, d, order], row_lf[0:8, order], row_zero[0:8, order], 0.0,
                                               ALU.add, ALU.add)
                        dve.tensor_tensor_scan(rowM[0:8, d, order], row_lf[0:8, order], row_ig[0:8, order],
                                               rowpar[:, 3:4] if g else 0.0, ALU.add, ALU.max)
                dve.drain()
                for d in range(2):
                    dve.tensor_tensor(rowA[0:8, d, :], row_ig[0:8, :], rowB[0:8, d, :], ALU.subtract)
                dve.drain()
                for d in range(2):
                    last = dve.tensor_tensor(rowB[0:8, d, :], rowB[0:8, d, :], rowM[0:8, d, :], ALU.subtract)
                last.then_inc(rows_ready.sem, 1)

            def mlstm(l):
                def weights(s):
                    g, hd, d = steps[s]
                    lo, hi = SEG[g]
                    dve.wait_ge(*bc_ready.at(l, s + 1))
                    if s >= 2:
                        dve.wait_ge(*nd_ready.at(l, s - 1))
                    if s == 9:
                        dve.wait_ge(*state_out.at(l, 3))
                    w = wmat[:, s % 2, :, :].rearrange("p a b -> p (a b)")
                    if g == 0:
                        dve.tensor_tensor(w[:, 0:P], ps[:, 4, 0:P], tri(d), ALU.add).then_inc(z_ready.sem, 1)
                    else:
                        dve.tensor_tensor(
                            w[:, 0:1920].rearrange("p (i c) -> p i c", c=640)[:, :, 0:P],
                            ps[:, 4, 0:384].rearrange("p (i c) -> p i c", c=P),
                            tri(d)[:, None, :].to_broadcast([P, 3, P]), ALU.add)
                        dve.tensor_tensor(w[:, 1920:2048], ps[:, 4, 384:512], tri(d), ALU.add)\
                            .then_inc(z_ready.sem, 1)
                        dve.wait_ge(*am_ready.at(l, s + 1))
                        dve.tensor_tensor(qi[:, s % 2, :], mq[:, hd, TP:T], qi[:, s % 2, :], ALU.mult)\
                            .then_inc(qi_ready.sem, 1)
                    dve.wait_ge(*st_ready.at(l, s // 2 + 1))
                    for j, (i, t0, t1) in enumerate(stiles(g, d)):
                        dve.wait_ge(*e_ready.at(l, e_before[s] + j + 1))
                        dve.scalar_tensor_tensor(wmat[:, s % 2, i, t0:t1], ps[:, i, t0:t1], ML_SCALE,
                                                 wmat[:, s % 2, i, t0:t1], ALU.mult, ALU.mult)\
                            .then_inc(w_ready.sem, 1)

                def divide(s):
                    g, hd, d = steps[s]
                    lo, hi = SEG[g]
                    n = hi - lo
                    e = emm[:, s % 2, 0:n]
                    dve.wait_ge(*am_ready.at(l, s + 1))
                    dve.wait_ge(*nd_ready.at(l, s + 1))
                    dve.scalar_tensor_tensor(e, ps[:, 7, 0:n], -1.0, e, ALU.mult, ALU.max)
                    dve.drain()
                    dve.tensor_tensor(e, ps[:, 7, 0:n], e, ALU.max)
                    dve.drain()
                    dve.reciprocal(e, e)
                    dve.drain()
                    if d == 0:
                        dve.tensor_tensor(y_ml[:, hd, lo:hi], ps[:, 6, 0:n], e, ALU.mult).then_inc(h_done.sem, 1)
                    else:
                        dve.tensor_tensor(e, ps[:, 6, 0:n], e, ALU.mult)
                        dve.drain()
                        dve.tensor_tensor(y_ml[:, hd, lo:hi], y_ml[:, hd, lo:hi], e, ALU.add)\
                            .then_inc(h_done.sem, 1)

                for s in range(16):
                    if s == 8:
                        divide(7)
                        for c in range(8):
                            hd = c % HM
                            if c >= 2:
                                dve.wait_ge(*state_ps.at(l, c - 1))
                            dve.tensor_scalar(vw[:, c % 2, 0:P], mv[:, 0, hd * P:(hd + 1) * P], wend[:, c:c + 1],
                                              None, ALU.mult)
                            dve.tensor_copy(vw[:, c % 2, P:P + 1], wend[:, c:c + 1]).then_inc(vw_ready.sem, 1)
                    weights(s)
                    if s and s != 8:
                        divide(s - 1)
                divide(15)

            def norm_heads(l, n0, dst, tmp, gain):
                for i in range(KB):
                    dve.wait_ge(*root_ready.at(l, n0 + i + 1))
                    dve.reciprocal(tmp[:, i, :], tmp[:, i, :])
                    dve.drain()
                    dve.scalar_tensor_tensor(dst[:, i, :], dst[:, i, :], gain(i), tmp[:, i, :], ALU.mult, ALU.mult)\
                        .then_inc(head_normed.sem, 1)

            def add_row_bias(l, u, out, at):
                dve.wait_ge(*unit_full.at(l, u + 1))
                return dve.tensor_tensor(out, ps[:, bank(u), :], par[:, Q_BV + at:Q_BV + at + WB], ALU.add)

            def attention(l):
                def maxima(s):
                    n, g = asteps[s]
                    w = TP if n is None else NKEY
                    if s >= 2:
                        dve.wait_ge(*probT_ps.at(l, 4 * (s - 1)))
                    if n is not None:
                        dve.wait_ge(*bias_ready.at(l, s - 1))
                    for a in range(4):
                        dve.wait_ge(*score_ps.at(l, 4 * s + a + 1))
                        dve.sem_inc(dve_passed, 1)
                        add = bias_t[:, 0, a, WINK:NKEY] if n is None else bias_t[:, s % 2, a, :]
                        dve.tensor_tensor_reduce(prob[:, s % 2, a, 0:w], ps[:, a, 0:w], add, 1.0, -3.0e38,
                                                 ALU.add, ALU.max, mx[:, s % 2, a:a + 1])
                    dve.drain()
                    dve.tensor_scalar(mx[:, s % 2, :], mx[:, s % 2, :], -1.0, None, ALU.mult)\
                        .then_inc(score_max.sem, 1)

                def scale(s):
                    w = TP if asteps[s][0] is None else NKEY
                    dve.wait_ge(*prob_exp.at(l, s + 1))
                    dve.reciprocal(rs[:, s % 2, :], rs[:, s % 2, :])
                    dve.drain()
                    for a in range(4):
                        dve.tensor_scalar(prob[:, s % 2, a, 0:w], prob[:, s % 2, a, 0:w], rs[:, s % 2, a:a + 1],
                                          None, ALU.mult).then_inc(prob_ready.sem, 1)

                def copy_out(nb):
                    dve.wait_ge(*att_ps.at(l, nb + 1))
                    src = ps[:, 6 + nb % 2, :].rearrange("p (j q) -> p j q", j=KB)
                    if nb == 0:
                        dve.tensor_copy(y_na[:, :, 0:TP], src).then_inc(att_copied.sem, 1)
                    else:
                        n = nb - 1
                        for j in range(KB):
                            last = dve.tensor_copy(
                                y_na[:, j, TP:T].rearrange("p (r c) -> p r c", c=GRID)[:, :, n * QB:(n + 1) * QB],
                                src[:, j, :].rearrange("p (r c) -> p r c", c=QB))
                        last.then_inc(att_copied.sem, 1)

                for s in range(10):
                    maxima(s)
                    scale(s)
                    if s % 2 == 1 and s >= 3:
                        copy_out(s // 2 - 1)
                copy_out(4)

            def convolution(l):
                for lo in (0, TP + 2):
                    dve.memset(u_pad[:, lo:lo + 1], 0.0)
                dve.memset(u_pad[:, TP + 1:TP + 2], 0.0)
                dve.memset(u_pad[:, T + 3:T + 4], 0.0)
                for i in range(KB):
                    dve.wait_ge(*emptied(l, U_CV + 3 * i))
                    u = U_CV + 3 * i + 1
                    dve.wait_ge(*unit_full.at(l, u + 1))
                    dve.scalar_tensor_tensor(cols(conv_t), pair_ps(u), par[:, Q_BIN + B_CH + i:Q_BIN + B_CH + i + 1],
                                             cols(cc_t[:, i, :]), ALU.add, ALU.mult).then_inc(dve_emptied.sem, 1)
                    dve.drain()
                    dve.tensor_copy(u_pad[:, 1:TP + 1], conv_t[:, 0:TP])
                    dve.tensor_copy(u_pad[:, TP + 3:T + 3], conv_t[:, TP:T])
                    dve.drain()
                    for j in range(3):
                        tap = par[:, Q_CW + 4 * j + i:Q_CW + 4 * j + i + 1]
                        for (lo, hi), at in zip(SEG, (j, j + 2)):
                            src = u_pad[:, lo + at:hi + at]
                            if j == 0:
                                dve.tensor_scalar(conv_t[:, lo:hi], src, tap, None, ALU.mult)
                            else:
                                dve.scalar_tensor_tensor(conv_t[:, lo:hi], src, tap, conv_t[:, lo:hi],
                                                         ALU.mult, ALU.add)
                        dve.drain()
                    u = U_CV + 3 * i + 2
                    dve.wait_ge(*unit_full.at(l, u + 1))
                    dve.scalar_tensor_tensor(cols(y_cv[:, i, :]), pair_ps(u),
                                             par[:, Q_BIN + B_CB + i:Q_BIN + B_CB + i + 1], cols(conv_t),
                                             ALU.add, ALU.mult).then_inc(dve_emptied.sem, 1)
                    dve.drain()
                    dve.sem_inc(conv_done.sem, 1)

            def merge(l):
                for i in range(3 * KD):
                    dt = i % KD
                    dve.wait_ge(*emptied(l, U_MG + 2 * i))
                    dve.wait_ge(*unit_full.at(l, U_MG + 2 * i + 2))
                    out = merged[:, dt, :] if i < KD else prod_t
                    dve.tensor_tensor(cols(out), pair_ps(U_MG + 2 * i + 1), cols(gate_t[:, i % 2, :]), ALU.mult)\
                        .then_inc(dve_emptied.sem, 1)
                    dve.drain()
                    if i >= KD:
                        dve.tensor_tensor(merged[:, dt, :], merged[:, dt, :], prod_t, ALU.add)
                        dve.drain()
                    dve.sem_inc(merged_ready.sem, 1)

            def mix_in(l):
                for k in range(KD):
                    u = U_WO + k
                    b = bank(u)
                    dve.wait_ge(*unit_full.at(l, u + 1))
                    for g, half, lo, hi in ((0, 0, 0, TP), (1, 0, TP, HALF), (1, 1, 0, HALF)):
                        t = half * HALF
                        last = dve.scalar_tensor_tensor(
                            x[:, k, t + lo:t + hi], ps[:, b + half, lo:hi], mod[:, 16 + k, g:g + 1],
                            x[:, k, t + lo:t + hi], ALU.mult, ALU.add)
                    last.then_inc(dve_emptied.sem, 1)
                dve.drain()
                dve.sem_inc(x_mixed.sem, KD)

            def route(l):
                lg = ps[:, 0, 0:NTILE * NE].rearrange("p (t e) -> p t e", e=NE)
                dve.wait_ge(*logit_ps.at(l, 1))
                dve.tensor_reduce(smax, lg, AX.X, ALU.max)
                dve.drain()
                dve.tensor_tensor(aff[:, :, :], lg, smax[:, :, None].to_broadcast([P, NTILE, NE]), ALU.subtract)\
                    .then_inc(logit_shift.sem, 1)
                dve.wait_ge(*logit_exp.at(l, 1))
                dve.tensor_reduce(smax, aff[:, :, :], AX.X, ALU.add)
                dve.drain()
                dve.reciprocal(smax, smax)
                dve.drain()
                dve.tensor_tensor(aff[:, :, :], aff[:, :, :], smax[:, :, None].to_broadcast([P, NTILE, NE]),
                                  ALU.mult).then_inc(aff_ready.sem, 1)
                dve.wait_ge(*affT_ps.at(l, 1))
                dve.tensor_copy(work[0:NE, 0:512], ps[0:NE, 1, :])
                dve.tensor_copy(work[0:NE, 512:T], ps[0:NE, 2, 0:P])
                dve.drain()
                for (lo, hi), cap in zip(SEG, (CAP_P, CAP_S)):
                    for r in range(cap // 8):
                        dve.max(top8[0:NE, :], work[0:NE, lo:hi])
                        dve.drain()
                        dve.match_replace(work[0:NE, lo:hi], top8[0:NE, :], work[0:NE, lo:hi], -1.0)
                        dve.drain()
                dve.tensor_scalar(mask_r[0:NE, :], work[0:NE, :], 0.0, None, ALU.is_lt)
                dve.drain()
                dve.memset(work[0:NE, :], 0.0)
                dve.drain()
                for lo, hi in SEG:
                    dve.tensor_tensor_scan(pos_r[0:NE, lo:hi], mask_r[0:NE, lo:hi], work[0:NE, lo:hi], 0.0,
                                           ALU.add, ALU.add)
                dve.drain()
                dve.tensor_tensor(pos_r[0:NE, :], pos_r[0:NE, :], mask_r[0:NE, :], ALU.mult)
                dve.drain()
                dve.tensor_scalar(pos_r[0:NE, :], pos_r[0:NE, :], -1.0, None, ALU.add).then_inc(pos_ready.sem, 1)
                dve.wait_ge(*posT_ps.at(l, 1))
                dve.tensor_copy(posT[:, :, :].rearrange("p t e -> p (t e)"), ps[:, 3, 0:NTILE * NE])\
                    .then_inc(posT_ready.sem, 1)
                dve.memset(y_p[0:64, :], 0.0)
                dve.drain()

            def experts(l, i):
                n = l * NPAIR + i
                lat = [P, NTILE - 1, 2, CAP_S]
                con = [P, 2, 32]
                pos_s = posT[:, 1:NTILE, bass.ds(2 * i, 2)][:, :, :, None].to_broadcast(lat)
                aff_s = aff[:, 1:NTILE, bass.ds(2 * i, 2)][:, :, :, None].to_broadcast(lat)
                pos_p = posT[:, 0, bass.ds(2 * i, 2)][:, :, None].to_broadcast(con)
                aff_p = aff[:, 0, bass.ds(2 * i, 2)][:, :, None].to_broadcast(con)
                dve.tensor_tensor(pick_s[:, :, :, :], iota[:, None, None, :].to_broadcast(lat), pos_s, ALU.is_equal)
                dve.tensor_tensor(pick_p[:, :, :], iota[:, None, 0:32].to_broadcast(con), pos_p, ALU.is_equal)\
                    .then_inc(pick_ready.sem, 1)
                dve.drain()
                dve.tensor_tensor(gated_s[:, :, :, :], pick_s[:, :, :, :], aff_s, ALU.mult)
                dve.tensor_tensor(gated_p[:, :, :], pick_p[:, :, :], aff_p, ALU.mult).then_inc(gated_ready.sem, 1)
                dve.wait_ge(scat_ps.sem, n + 1)
                dve.tensor_copy(scat_s, ps[:, 7, :])
                dve.tensor_copy(scat_p[0:64, :], ps[0:64, 3, 0:TP]).then_inc(scat_ready.sem, 1)
                for e in range(2):
                    m = 2 * n + e
                    for half in range(2):
                        dve.wait_ge(silu_ready.sem, 2 * m + half + 1)
                        dve.tensor_tensor(act_t[:, e, 4 * half:4 * half + 4, :].rearrange("p f c -> p (f c)"),
                                          ps[:, 4 + 2 * half, 0:4 * CAP],
                                          silu_t[:, half, :, :].rearrange("p f c -> p (f c)"), ALU.mult)\
                            .then_inc(act_ready.sem, 1)
                for dt in range(KD):
                    dve.wait_ge(spread_ps.sem, KD * n + dt + 1)
                    b = 2 if dt % 2 == 0 else 6
                    q = 7 if dt % 2 == 0 else 5
                    dve.scalar_tensor_tensor(x[:, dt, TP:T], ps[:, b, :], mod[:, 40 + dt, 1:2], x[:, dt, TP:T],
                                             ALU.mult, ALU.add)
                    dve.scalar_tensor_tensor(x[:, dt, 0:TP], ps[:, q, 0:TP], mod[:, 40 + dt, 0:1], x[:, dt, 0:TP],
                                             ALU.mult, ALU.add).then_inc(x_added.sem, 1)
                dve.drain()

            dve.memset(eps[:, :], EPS).then_inc(consts_set, 1)
            dve.wait_ge(start_in, 48)
            with dve.Fori(0, DEPTH) as l:
                dve.wait_ge(*params_in.at(l, 5))
                dve.wait_ge(*mod_ps.at(l, 1))
                dve.tensor_tensor(mod[:, :, :], ps[:, 0, 0:96].rearrange("p (a b) -> p a b", b=2),
                                  par[:, Q_ADAB:Q_ADAB + 48][:, :, None].to_broadcast([P, 48, 2]), ALU.add)
                dve.tensor_scalar(gq[:, :], par[:, Q_GQ:Q_GQ + 1], DN ** -0.5, None, ALU.mult)
                dve.drain()
                for a, c, g in ((a1, 8, Q_G1), (a2, 32, Q_G2)):
                    dve.scalar_tensor_tensor(a[:, :, :], mod[:, c:c + 8, :], 1.0,
                                             par[:, g:g + 8][:, :, None].to_broadcast([P, 8, 2]),
                                             ALU.add, ALU.mult).then_inc(scale_ready.sem, 1)
                root_x(l, 0)
                rope(l, U_RQ, mq)
                rope(l, U_RK, mk)
                for t in range(NTILE):
                    add_row_bias(l, U_MV + t, mv[:, t, :], 0).then_inc(dve_emptied.sem, 1)
                gate_rows(l)
                mlstm(l)
                norm_heads(l, 0, y_ml, ml_tmp, lambda i: par[:, Q_OG + i:Q_OG + i + 1])
                for i in range(KB):
                    dve.drain()
                    dve.wait_ge(*emptied(l, U_MO + i))
                    dve.tensor_tensor(y_ml[:, i, :], y_ml[:, i, :], sig_mo[:, i, :], ALU.mult)\
                        .then_inc(yml_ready.sem, 1)
                norm_heads(l, HM, nq, na_tmp, lambda i: gq[:, :])
                norm_heads(l, HM + KB, nk, na_tmp, lambda i: par[:, Q_GK:Q_GK + 1])
                for t in range(NTILE):
                    if t >= 3:
                        dve.wait_ge(*nv_stored[t % 2].at(l, t - 2))
                    out = nvp if t == 0 else nvst[:, t % 2, :]
                    add_row_bias(l, U_NV + t, out, WB).then_inc(dve_emptied.sem, 1)
                    dve.drain()
                    dve.sem_inc(nv_staged.sem, 1)
                for b in range(2):
                    last = dve.memset(bias_t[:, b, :, WINK:NKEY], 0.0)
                dve.drain()
                dve.sem_inc(bias_zeroed.sem, 1)
                attention(l)
                convolution(l)
                merge(l)
                mix_in(l)
                root_x(l, 1)
                route(l)
                with dve.Fori(0, NPAIR) as i:
                    experts(l, i)
                dve.sem_inc(layer_x.sem, 1)


def constants():
    k = np.zeros((P, NCONST), np.float32)
    k[:, K_ID:K_ID + P] = np.eye(P)
    k[:, K_ONE:K_ONE + P] = 1.0
    for b in range(2):
        k[64 * b:64 * b + 64, K_BLK + 64 * b:K_BLK + 64 * b + 64] = 1.0
    half = 32
    freqs = (np.float32(10000.0) ** (-np.arange(half, dtype=np.float32) / np.float32(half))).astype(np.float32)
    t = np.arange(TS)
    for b, pos in enumerate(((t // GRID).astype(np.float32), (t % GRID).astype(np.float32))):
        ang = freqs[:, None] * pos[None, :]
        for s in range(2):
            at = 64 * b + 32 * s
            k[at:at + 32, K_COS:K_COS + TS] = np.cos(ang)
            k[at:at + 32, K_SIN:K_SIN + TS] = np.sin(ang)
        for i in range(half):
            k[64 * b + 32 + i, K_ROT + 64 * b + i] = -1.0
            k[64 * b + i, K_ROT + 64 * b + 32 + i] = 1.0
    s, q = np.arange(P)[:, None], np.arange(P)[None, :]
    k[:, K_TRI:K_TRI + P] = np.where(q >= s, 0.0, -1e30)
    k[:, K_TRI + P:K_TRI + 2 * P] = np.where(q <= s, 0.0, -1e30)
    for n in range(NBLK):
        qcol = n * QB + np.arange(P)[:, None] % QB
        start = np.clip(qcol - 8, 0, GRID - 16)
        kcol = BAND0[n] + np.arange(KBAND)[None, :]
        k[:, K_MASK + n * KBAND:K_MASK + (n + 1) * KBAND] = np.where((kcol >= start) & (kcol < start + 16), 0.0, -1e30)
    k[:, K_IOTA:K_IOTA + CAP_S] = np.arange(CAP_S)
    return k


def kernel(**inputs):
    import numpy as np
    import concourse.bacc as bacc
    from concourse import mybir
    from concourse.bass_utils import run_bass_kernel_spmd as run

    a = {n: np.ascontiguousarray(v) for n, v in inputs.items()}
    f32 = np.float32
    xT = np.concatenate([a["x_prompt"][0].T, a["x_sample"][0].T], axis=1)
    cond = np.stack([a["c_ctx"], a["c"][0]], axis=1)

    def cols(v):
        return v.reshape(DEPTH, -1, P).transpose(0, 2, 1)

    b_in = a["b_in"]
    b_main = np.concatenate([b_in[:, :C_G], b_in[:, C_CB:]], axis=1)
    fm = a["ml_fbias"].reshape(DEPTH, 8)
    m0 = a["state_mlstm_m"][0].reshape(DEPTH, 8)
    twice = lambda v: np.concatenate([v, v], axis=1)[:, :, None]
    prm = np.concatenate([
        cols(a["ada_b"]), cols(a["norm1_g"]), cols(a["norm2_g"]), cols(b_main), cols(a["ml_out_g"]),
        cols(a["cv_w"].reshape(DEPTH, -1)), twice(a["na_q_g"]), twice(a["na_k_g"]),
        np.broadcast_to(m0[:, None, :], (DEPTH, P, 8)),
        a["state_mlstm_n"][0].reshape(DEPTH, 8, P).transpose(0, 2, 1),
        np.broadcast_to(b_in[:, None, C_MV:C_MV + WB], (DEPTH, P, WB)),
        np.broadcast_to(b_in[:, None, C_NV:C_NV + WB], (DEPTH, P, WB))], axis=2)
    rowp = np.stack([b_in[:, C_G:C_G + 8], b_in[:, C_G + 8:C_G + 16], fm, m0], axis=2)
    rpb = np.pad(a["na_rpb"], ((0, 0), (0, 0), (0, 0), (16, 16)))
    r, q = np.arange(P) // QB, np.arange(P) % QB
    dr = np.arange(ROWS)[None, :] - r[:, None] + 7
    biasT = np.stack([
        rpb[:, :, dr[:, :, None],
            (np.arange(KBAND)[None, :] + BAND0[n] - n * QB - q[:, None] + 15 + 16)[:, None, :]]
        for n in range(NBLK)], axis=1)
    biasT = biasT.transpose(0, 1, 3, 2, 4, 5).reshape(DEPTH, NBLK, P, HN, WINK)
    arrays = {
        "xT": xT, "cond": cond, "const": constants(), "prm": prm, "rowp": rowp, "biasT": biasT,
        "ckT": a["cache_ctx_k"][0].reshape(DEPTH, P, WB).transpose(0, 2, 1),
        "cv": a["cache_ctx_v"][0].reshape(DEPTH, P, WB),
        "c0": a["state_mlstm_c"][0].reshape(DEPTH, 8, P, P),
        **{n: a[n] for n in ("ada_w", "w_in", "w_pa", "w_pb", "w_pc", "w_o", "w_router", "w_gate", "w_up", "w_down")},
    }
    nc = bacc.Bacc("TRN2", target_bir_lowering=False, num_devices=1)
    nc.disable_value_cache = True
    aps = []
    arrays = {n: np.ascontiguousarray(v) for n, v in arrays.items()}
    for n, v in arrays.items():
        aps.append(nc.dram_tensor(n, v.shape, mybir.dt.from_np(v.dtype), kind="ExternalInput").ap())
    outs = {"yT": (D, T), "new_k": (DEPTH, WB, TP), "new_v": (DEPTH, TP, WB), "new_cn": (DEPTH, 8, P, P + 1), "new_m": (DEPTH, 8, 1)}
    for n, s in outs.items():
        aps.append(nc.dram_tensor(n, s, mybir.dt.float32, kind="ExternalOutput").ap())
    aps.append(nc.dram_tensor("nv_copy", (TS, WB), mybir.dt.float32, kind="Internal").ap())
    step_program(nc, *aps)
    res = run(nc, [arrays], core_ids=[0]).results[0]
    yT = res["yT"]
    return (yT[:, :TP].T[None], yT[:, TP:].T[None],
            res["new_k"].transpose(0, 2, 1).reshape(1, DEPTH, TP, HN, DN),
            res["new_v"].reshape(1, DEPTH, TP, HN, DN),
            res["new_cn"][..., :P].reshape(1, DEPTH, 2, HM, P, P),
            res["new_cn"][..., P].reshape(1, DEPTH, 2, HM, P),
            res["new_m"].reshape(1, DEPTH, 2, HM))
```

```python
import concourse.bass as bass
from concourse import mybir
from contextlib import ExitStack
import numpy as np

F32 = mybir.dt.float32
F32R = mybir.dt.float32r
ALU = mybir.AluOpType
ACT = mybir.ActivationFunctionType
AX = mybir.AxisListType

P = 128
D = 1024
KD = D // P
DEPTH = 2
TP, TS = 128, 512
T = TP + TS
HALF = T // 2
NTILE = T // P
GRID = 64
ROWS = TS // GRID
HM = 4
HN, DN = 8, 64
WB = 512
KB = WB // P
NBLK, QB, KBAND = 4, 16, 32
NE, FF = 16, 1024
CAP_P, CAP_S = 2 * TP // NE, 2 * TS // NE
CAP = CAP_S + CAP_P
NPAIR = NE // 2
EPS = 1e-6
ML_SCALE = float(P) ** -0.5
BAND0 = [min(max(16 * n - 8, 0), GRID - KBAND) for n in range(NBLK)]
WINK = ROWS * KBAND
NKEY = WINK + P

C_MQ, C_MK, C_MV, C_MO, C_G = 0, 512, 1024, 1536, 2048
C_CB, C_CC, C_CH = 2064, 2576, 3088
C_NQ, C_NK, C_NV, C_GT = 3600, 4112, 4624, 5136
PROJ = C_GT + 3 * D

Q_ADAB, Q_G1, Q_G2, Q_BIN = 0, 48, 56, 64
Q_OG, Q_CW, Q_GQ, Q_GK, Q_M0, Q_N0 = 128, 132, 144, 145, 146, 154
Q_BV = 162
NPRM = Q_BV + 2 * WB
B_MQ, B_MK, B_MO, B_CB, B_CC, B_CH, B_NQ, B_NK, B_GT = 0, 4, 12, 16, 20, 24, 28, 32, 40

K_ID, K_ONE, K_BLK, K_ROT, K_COS, K_SIN = 0, 128, 256, 384, 512, 1024
K_TRI, K_MASK, K_IOTA = 1536, 1792, 1920
NCONST = 1984

NSLOT = 4
CHUNK = 2048
CC = CHUNK // KD
ADA_CHUNKS = 6 * D // CC
(R_MQ, R_MK, R_MV, R_MO, R_NQ, R_NK, R_NV) = range(ADA_CHUNKS, ADA_CHUNKS + 14, 2)
R_CONV = R_NV + 2
R_MERGE = R_CONV + 6
R_O = R_MERGE + 18
R_END = R_O + 4
R_EXP = -(-R_END // NSLOT) * NSLOT
EXP_CHUNKS = 12
PAIR_CHUNKS = 2 * EXP_CHUNKS


def slot_uses(q):
    return sum(1 for c in range(q % NSLOT, q, NSLOT) if c < R_END or c >= R_EXP)


SLOT_LAYER = [slot_uses(R_EXP + NPAIR * PAIR_CHUNKS + s) for s in range(NSLOT)]


class Signal:

    def __init__(self, sem, per_layer, unit=1):
        self.sem, self.per_layer, self.unit = sem, per_layer, unit

    def at(self, l, k):
        return self.sem, (l * self.per_layer + k) * self.unit


def step_program(nc, xT, cond, const, prm, rowp, biasT, ckT, cv, c0, ada_w, w_in, w_pa, w_pb, w_pc,
                 w_o, w_router, w_gate, w_up, w_down, yT, new_k, new_v, new_cn, new_m, nv_dram):
    with ExitStack() as ctx:
        def sb(name, shape, dtype=F32):
            return ctx.enter_context(nc.sbuf_tensor(name, shape, dtype))

        def signal(name, per_layer, unit=1):
            return Signal(ctx.enter_context(nc.semaphore(name)), per_layer, unit)

        def semaphore(name):
            return ctx.enter_context(nc.semaphore(name))

        ring = sb("ring", [P, NSLOT, CHUNK])
        w_hi = sb("w_hi", [P, 2, CHUNK], F32R)
        w_lo = sb("w_lo", [P, 2, CHUNK], F32R)
        x = sb("x", [P, KD, T])
        h = sb("h", [P, KD, T])
        cst = sb("cst", [P, NCONST])
        par = sb("par", [P, NPRM])
        rowpar = sb("rowpar", [8, 4])
        silu_c = sb("silu_c", [P, KD, 2])
        mod = sb("mod", [P, 48, 2])
        a1 = sb("a1", [P, KD, 2])
        a2 = sb("a2", [P, KD, 2])
        eps = sb("eps", [P, 1])
        acol = sb("acol", [P, 2, NTILE, 8])
        wr = sb("wr", [P, KD, NE])
        wg16 = sb("wg16", [P, KD, 16])
        gq = sb("gq", [P, 1])
        rbias = sb("rbias", [8, 1])
        wend = sb("wend", [P, 8])
        mx = sb("mx", [P, 2, 4])
        rs = sb("rs", [P, 2, 4])
        rstd = sb("rstd", [P, T])
        ARENA, FF_WORDS = 21760, 13312
        arena_space = ExitStack()
        arena = arena_space.enter_context(nc.sbuf_tensor("arena", [P, ARENA], F32))
        arena_space.close()
        arena_ff = sb("arena_ff", [P, FF_WORDS])
        xg_hi = sb("xg_hi", [P, KD, 2, CAP], F32R)
        xg_lo = sb("xg_lo", [P, KD, 2, CAP], F32R)
        act_hi = sb("act_hi", [P, 2, KD, CAP], F32R)
        act_lo = sb("act_lo", [P, 2, KD, CAP], F32R)
        ctx.enter_context(nc.sbuf_tensor("arena_rest", [P, ARENA - FF_WORDS - 4 * 2 * KD * CAP], F32))
        ps = ctx.enter_context(nc.psum_tensor("ps", [P, 8, 512], F32))

        def view(at, *shape, store=arena, size=ARENA):
            n = int(np.prod(shape))
            assert at + n <= size
            a = store[:, at:at + n]
            if len(shape) == 1:
                return a
            names = "abcd"[:len(shape)]
            return a.rearrange("p (%s) -> p %s" % (" ".join(names), " ".join(names)),
                               **{c: s for c, s in zip(names, shape)})

        ident = cst[:, K_ID:K_ID + P]
        ones = cst[:, K_ONE:K_ONE + P]
        blkones = cst[:, K_BLK:K_BLK + P]
        rotate = cst[:, K_ROT:K_ROT + P]
        cosT = cst[:, K_COS:K_COS + TS]
        sinT = cst[:, K_SIN:K_SIN + TS]
        iota = cst[:, K_IOTA:K_IOTA + CAP_S]

        def tri(d):
            return cst[:, K_TRI + d * P:K_TRI + (d + 1) * P]

        mod_row = view(0, 2, 512)[0:2, :, :]
        Y_TOP = ARENA - KB * T
        y_ml = view(Y_TOP, KB, T)
        y_na = view(Y_TOP - KB * T, KB, T)
        y_cv = view(Y_TOP - 2 * KB * T, KB, T)
        mq = view(0, HM, T)
        mk = view(2560, HM, T)
        mv = view(5120, NTILE, WB)
        rowA = view(7680, 2, T)
        rowB = view(8960, 2, T)
        rowM = view(10240, 2, T)
        W_AT = 11520
        wmat = view(W_AT, 2, 4, 512)
        row_ig, row_lf, row_t, row_zero = (view(W_AT + T * i, T) for i in range(4))
        rope_tmp = view(W_AT + 2560, TS)
        ktok = view(W_AT + 2048, HM, P)
        vw = view(W_AT + 2560, 2, 129)
        cout = view(W_AT + 2818, 8, 129)
        qi = view(W_AT + 4096, 2, TS)
        emm = view(W_AT + 5120, 2, TS)
        c0s = view(W_AT + 6144, 8, P)
        assert W_AT + 6144 + 1024 <= Y_TOP
        ml_tmp = view(5120, KB, T)
        sig_mo = view(7680, KB, T)
        nq = view(0, KB, T)
        nk = view(2560, KB, T)
        na_tmp = view(10240, KB, T)
        bias_t = view(5120, 2, 4, NKEY)
        prob = view(8192, 2, 4, NKEY)
        vband = view(11264, 2, 2, WB)
        probT = view(13312, 2, NKEY)
        NA_C = 14080
        cks = view(NA_C, KB, P)
        cvs = view(NA_C + 512, WB)
        nvp = view(NA_C + 1024, WB)
        nvst = view(NA_C + 1536, 2, WB)
        assert NA_C + 2560 <= Y_TOP - KB * T
        cc_t = view(5120, KB, T)
        u_pad = view(7680, T + 4)
        conv_t = view(8324, T)
        merged = view(0, KD, T)
        gate_t = view(9728, 2, T)
        prod_t = view(11008, T)
        def ff(at, *shape):
            return view(at, *shape, store=arena_ff, size=FF_WORDS)

        h_tok = ff(0, NTILE, D)
        aff = ff(5120, NTILE, NE)
        posT = ff(5200, NTILE, NE)
        smax = ff(5280, NTILE)
        affT = ff(5312, T)
        work = ff(5952, T)
        mask_r = ff(6592, T)
        pos_r = ff(7232, T)
        top8 = ff(7872, 8)
        pick_s = ff(7936, NTILE - 1, 2, CAP_S)
        pick_p = ff(8448, 2, 32)
        gated_s = ff(8512, NTILE - 1, 2, CAP_S)
        gated_p = ff(9024, 2, 32)
        scat_s = ff(9088, TS)
        scat_p = ff(9600, TP)
        silu_t = ff(9728, 512)
        y_s = ff(10240, D)
        y_p = ff(11264, D)
        act_row = ff(12288, 2, 512)

        slot_landed = [semaphore(f"slot{s}_landed") for s in range(NSLOT)]
        slot_used = [semaphore(f"slot{s}_used") for s in range(NSLOT)]
        start_in = semaphore("start_in")
        cond_ready = semaphore("cond_ready")
        consts_set = semaphore("consts_set")
        params_in = signal("params_in", 5, 16)
        mod_row_ps = signal("mod_row_ps", ADA_CHUNKS // 2)
        mod_row_copied = signal("mod_row_copied", ADA_CHUNKS // 2)
        mod_ps = signal("mod_ps", 1)
        mod_ready = signal("mod_ready", 1)
        scale_ready = signal("scale_ready", 2)
        x_sq = signal("x_sq", 2 * KD)
        x_ss = signal("x_ss", 2)
        x_root = signal("x_root", 2)
        x_normed = signal("x_normed", 2 * KD)
        h_ready = signal("h_ready", 2 * KD)
        layer_x = signal("layer_x", 1)
        unit_full = signal("unit_full", 1)
        act_emptied = signal("act_emptied", 1)
        dve_emptied = signal("dve_emptied", 1)
        rows_ready = signal("rows_ready", 1)
        lf_abs = signal("lf_abs", 1)
        lf_log = signal("lf_log", 1)
        acol_ps = signal("acol_ps", 1)
        acol_ready = signal("acol_ready", 1)
        roped = signal("roped", 2 * HM)
        st_ready = signal("st_ready", 2 * HM)
        bc_ready = signal("bc_ready", 16)
        am_ready = signal("am_ready", 16)
        z_ready = signal("z_ready", 16)
        e_ready = signal("e_ready", 40)
        w_ready = signal("w_ready", 40)
        qi_ready = signal("qi_ready", 8)
        nd_ready = signal("nd_ready", 16)
        h_done = signal("h_done", 16)
        ktok_ps = signal("ktok_ps", 1)
        ktok_ready = signal("ktok_ready", 1)
        vw_ready = signal("vw_ready", 8)
        state_ps = signal("state_ps", 8)
        state_copied = signal("state_copied", 8)
        state_out = signal("state_out", 3, 16)
        sq_ready = signal("sq_ready", 12)
        root_ready = signal("root_ready", 12)
        head_normed = signal("head_normed", 12)
        mo_ready = signal("mo_ready", KB)
        yml_ready = signal("yml_ready", KB)
        nv_staged = signal("nv_staged", NTILE)
        nv_stored = [signal("nv_even_stored", 3, 16), signal("nv_odd_stored", 2, 16)]
        newk_out = signal("newk_out", 1, 16)
        bias_zeroed = signal("bias_zeroed", 1)
        ctx_in = signal("ctx_in", 2, 16)
        band_in = [signal(f"band_in{b}", 4, 16) for b in range(2)]
        bias_in = [signal(f"bias_in{b}", 4, 16) for b in range(2)]
        bias_ready = signal("bias_ready", 8)
        score_ps = signal("score_ps", 40)
        score_max = signal("score_max", 10)
        prob_exp = signal("prob_exp", 10)
        prob_ready = signal("prob_ready", 40)
        probT_ps = signal("probT_ps", 40)
        probT_ready = signal("probT_ready", 40)
        att_ps = signal("att_ps", 5)
        att_copied = signal("att_copied", 5)
        cc_ready = signal("cc_ready", KB)
        conv_done = signal("conv_done", KB)
        gate_ready = signal("gate_ready", 24)
        merged_ready = signal("merged_ready", 24)
        x_mixed = signal("x_mixed", KD)
        tok_ps = signal("tok_ps", 10)
        tok_copied = signal("tok_copied", 10)
        logit_ps = signal("logit_ps", 1)
        logit_shift = signal("logit_shift", 1)
        logit_exp = signal("logit_exp", 1)
        aff_ready = signal("aff_ready", 1)
        affT_ps = signal("affT_ps", 1)
        pos_ready = signal("pos_ready", 1)
        posT_ps = signal("posT_ps", 1)
        posT_ready = signal("posT_ready", 1)
        pick_ready = signal("pick_ready", NPAIR)
        gated_ready = signal("gated_ready", NPAIR)
        scat_ps = signal("scat_ps", NPAIR)
        scat_ready = signal("scat_ready", NPAIR)
        gather_ps = signal("gather_ps", 3 * NPAIR)
        xg_ready = signal("xg_ready", 3 * NPAIR)
        up_ps = signal("up_ps", 2 * NE)
        silu_ready = signal("silu_ready", 2 * NE)
        act_ready = signal("act_ready", 2 * NE)
        down_ps = signal("down_ps", 2 * NE)
        down_copied = signal("down_copied", 2 * NE)
        actT_ps = signal("actT_ps", 2 * NE)
        actT_hi = signal("actT_hi", 2 * NE)
        actT_ready = signal("actT_ready", 2 * NE)
        xg_hi_ready = signal("xg_hi_ready", 3 * NPAIR)
        hi_ready = semaphore("hi_ready")
        hi_used = [semaphore(f"hi{b}_used") for b in range(2)]
        lo_used = [semaphore(f"lo{b}_used") for b in range(2)]
        context_spread = signal("context_spread", NPAIR)
        context_added = signal("context_added", NPAIR)
        spread_ps = signal("spread_ps", KD * NPAIR)
        x_added = signal("x_added", KD * NPAIR)
        stored = semaphore("stored")
        pe_passed = semaphore("pe_passed")
        dve_passed = semaphore("dve_passed")
        pool_passed = semaphore("pool_passed")

        units = []

        def unit(kind, count):
            at = len(units)
            units.extend([kind] * count)
            return at

        U_MQ, U_RQ = unit("act", HM), unit("dve", HM)
        U_MK, U_RK = unit("act", HM), unit("dve", HM)
        U_MV = unit("dve", NTILE)
        U_G = unit("dve", 2)
        U_NORM = unit("act", HM)
        U_MO = unit("act", KB)
        U_NQ, U_SQ = unit("act", KB), unit("act", KB)
        U_NK, U_SK = unit("act", KB), unit("act", KB)
        U_NV = unit("dve", NTILE)
        U_CV = unit("cv", 3 * KB)
        U_MG = unit("mg", 2 * 3 * KD)
        U_WO = unit("dve", KD)
        for i in range(KB):
            units[U_CV + 3 * i:U_CV + 3 * i + 3] = ["act", "dve", "dve"]
        for i in range(3 * KD):
            units[U_MG + 2 * i:U_MG + 2 * i + 2] = ["act", "dve"]
        act_before = [sum(1 for k in units[:u] if k == "act") for u in range(len(units) + 1)]
        dve_before = [sum(1 for k in units[:u] if k == "dve") for u in range(len(units) + 1)]
        unit_full.per_layer = len(units)
        act_emptied.per_layer = act_before[-1]
        dve_emptied.per_layer = dve_before[-1]

        def bank(u):
            return 2 * (u % 4)

        def emptied(l, u):
            if units[u] == "act":
                return act_emptied.at(l, act_before[u] + 1)
            return dve_emptied.at(l, dve_before[u] + 1)

        def pair_ps(u):
            b = bank(u)
            return ps[:, b:b + 2, 0:HALF]

        def cols(a):
            return a.rearrange("p (a b) -> p a b", a=2)

        SEG = [(0, TP), (TP, T)]
        steps = [(g, hd, d) for g in range(2) for hd in range(HM) for d in range(2)]
        e_before = [0]
        for g, _, _ in steps:
            e_before.append(e_before[-1] + (4 if g else 1))

        def stiles(g, d):
            if g == 0:
                return [(0, 0, P)]
            if d == 0:
                return [(i, i * P, TS) for i in range(4)]
            return [(i, 0, (i + 1) * P) for i in (3, 2, 1, 0)]

        asteps = [(None, 0), (None, 1)] + [(n, g) for n in range(NBLK) for g in range(2)]

        expert_chunks = [(w, kh, nh) for nh in range(2) for w in (w_gate, w_up) for kh in range(2)] + \
                        [(w_down, kh, nh) for kh in range(2) for nh in range(2)]

        block = ctx.enter_context(nc.Block())

        @block.sync
        def _(sp):
            def load(l, q, src, i=None, j=None):
                s = (q if i is None else j) % NSLOT
                before = l * SLOT_LAYER[s] + slot_uses(q)
                if i is not None:
                    before = before + i * (PAIR_CHUNKS // NSLOT)
                sp.wait_ge(slot_used[s], before + 1)
                n = src.shape[2]
                dst = ring[:, s, :].rearrange("p (k n) -> p k n", n=n)
                sp.dma_start(dst, src).then_inc(slot_landed[s], 16)

            def rows_of(w, c, n=CC):
                return w.rearrange("(k p) n -> p k n", p=P)[:, :, c:c + n]

            with sp.Fori(0, DEPTH) as l:
                ada_l = ada_w[l, :, :]
                win_l = w_in[l, :, :]
                for q in range(ADA_CHUNKS):
                    load(l, q, rows_of(ada_l, CC * q))
                for q, c in ((R_MQ, C_MQ), (R_MK, C_MK), (R_MV, C_MV), (R_MO, C_MO), (R_NQ, C_NQ),
                             (R_NK, C_NK), (R_NV, C_NV)):
                    for j in range(2):
                        load(l, q + j, rows_of(win_l, c + CC * j))
                for j in range(2):
                    for b, c in enumerate((C_CC, C_CH, C_CB)):
                        load(l, R_CONV + 3 * j + b, rows_of(win_l, c + CC * j))
                for b, w in enumerate((w_pa, w_pb, w_pc)):
                    for j in range(2):
                        load(l, R_MERGE + 6 * b + 3 * j, rows_of(w[l, :, :], 512 * j, 512))
                        for g in range(2):
                            load(l, R_MERGE + 6 * b + 3 * j + 1 + g,
                                 rows_of(win_l, C_GT + b * D + CC * (2 * j + g)))
                for j in range(4):
                    load(l, R_O + j, rows_of(w_o[l, :, :], CC * j))
                with sp.Fori(0, NPAIR) as i:
                    for e in range(2):
                        for j, (w, kh, nh) in enumerate(expert_chunks):
                            load(l, R_EXP + EXP_CHUNKS * e + j,
                                 rows_of(w[l, 2 * i + e, 512 * kh:512 * (kh + 1), :], 512 * nh, 512),
                                 i, EXP_CHUNKS * e + j)

        @block.gpsimd
        def _(pool):
            pool.dma_start(x[:, :, :], xT.rearrange("(k p) t -> p k t", p=P)).then_inc(start_in, 16)
            pool.dma_start(cst[:, :], const).then_inc(start_in, 16)
            pool.dma_start(silu_c[:, :, :], cond.rearrange("(k p) c -> p k c", p=P)).then_inc(start_in, 16)
            with pool.Fori(0, DEPTH) as l:
                pool.dma_start(par[:, :], prm[l, :, :]).then_inc(params_in.sem, 16)
                pool.dma_start(rowpar[:, :], rowp[l, :, :]).then_inc(params_in.sem, 16)
                pool.dma_start(wr[:, :, :], w_router[l, :, :].rearrange("(k p) e -> p k e", p=P))\
                    .then_inc(params_in.sem, 16)
                pool.dma_start(wg16[:, :, :], w_in[l, :, :].rearrange("(k p) n -> p k n", p=P)[:, :, C_G:C_G + 16])\
                    .then_inc(params_in.sem, 16)
                pool.dma_start(c0s[:, :, :], c0[l, :, :, :].rearrange("g d v -> d g v")).then_inc(params_in.sem, 16)
                pool.wait_ge(*rows_ready.at(l, 1))
                pool.sem_inc(pool_passed, 1)
                pool.dma_start(new_m[l, 0:HM, :], rowM[0:HM, 0, TP - 1:TP]).then_inc(state_out.sem, 16)
                pool.dma_start(new_m[l, HM:8, :], rowM[HM:8, 1, 0:1]).then_inc(state_out.sem, 16)
                pool.wait_ge(*state_copied.at(l, 8))
                pool.sem_inc(pool_passed, 1)
                pool.dma_start(new_cn[l, :, :, :].rearrange("g d v -> d g v"), cout).then_inc(state_out.sem, 16)
                pool.wait_ge(*h_done.at(l, 16))
                pool.sem_inc(pool_passed, 1)
                pool.dma_start(cks[:, :, :], ckT[l, :, :].rearrange("(j p) t -> p j t", p=P)).then_inc(ctx_in.sem, 16)
                pool.dma_start(cvs, cv[l, :, :]).then_inc(ctx_in.sem, 16)
                for t in range(NTILE):
                    pool.wait_ge(*nv_staged.at(l, t + 1))
                    pool.sem_inc(pool_passed, 1)
                    if t == 0:
                        pool.wait_ge(*head_normed.at(l, 12))
                        pool.sem_inc(pool_passed, 1)
                        pool.dma_start(new_k[l, :, :].rearrange("(j p) t -> p j t", p=P), nk[:, :, 0:TP])\
                            .then_inc(newk_out.sem, 16)
                        pool.dma_start(new_v[l, :, :], nvp).then_inc(nv_stored[0].sem, 16)
                    else:
                        pool.dma_start(nv_dram[(t - 1) * P:t * P, :], nvst[:, t % 2, :])\
                            .then_inc(nv_stored[t % 2].sem, 16)
                pool.wait_ge(*nv_stored[0].at(l, 3))
                pool.wait_ge(*nv_stored[1].at(l, 2))
                pool.wait_ge(*bias_zeroed.at(l, 1))
                pool.sem_inc(pool_passed, 1)
                nv_grid = nv_dram.rearrange("(g i c) f -> g i c f", g=2, c=GRID)

                def band_load(n):
                    for g in range(2):
                        pool.dma_start(vband[:, n % 2, g, :], nv_grid[g, :, BAND0[n]:BAND0[n] + KBAND, :])\
                            .then_inc(band_in[n % 2].sem, 16)

                def bias_load(s):
                    n, g = asteps[s + 2]
                    pool.dma_start(bias_t[:, s % 2, :, 0:WINK], biasT[l, n, :, 4 * g:4 * g + 4, :])\
                        .then_inc(bias_in[s % 2].sem, 16)

                band_load(0)
                band_load(1)
                bias_load(0)
                bias_load(1)
                for s in range(8):
                    n, g = asteps[s + 2]
                    pool.wait_ge(*bias_in[s % 2].at(l, s // 2 + 1))
                    pool.tensor_tensor(
                        bias_t[:, s % 2, :, 0:WINK].rearrange("p a (i j) -> p a i j", j=KBAND),
                        bias_t[:, s % 2, :, 0:WINK].rearrange("p a (i j) -> p a i j", j=KBAND),
                        cst[:, K_MASK + n * KBAND:K_MASK + (n + 1) * KBAND][:, None, None, :]
                        .to_broadcast([P, 4, ROWS, KBAND]), ALU.add).then_inc(bias_ready.sem, 1)
                    if 1 <= s <= 6:
                        pool.wait_ge(*score_max.at(l, s + 2))
                        pool.sem_inc(pool_passed, 1)
                        bias_load(s + 1)
                    if s in (3, 5):
                        pool.wait_ge(*att_ps.at(l, (s - 1) // 2 + 1))
                        pool.sem_inc(pool_passed, 1)
                        band_load((s - 1) // 2 + 1)
                pool.wait_ge(*newk_out.at(l, 1))
                pool.wait_ge(*layer_x.at(l, 1))
            pool.dma_start(yT.rearrange("(k p) t -> p k t", p=P), x[:, :, :]).then_inc(stored, 16)
            pool.wait_ge(stored, 16)
            pool.wait_ge(*state_out.at(DEPTH - 1, 3))
            pool.wait_ge(*nv_stored[0].at(DEPTH - 1, 3))
            pool.wait_ge(*newk_out.at(DEPTH - 1, 1))

        @block.tensor
        def _(pe):
            def chunk(l, q, n, i=None, j=None):
                s = (q if i is None else j) % NSLOT
                before = l * SLOT_LAYER[s] + slot_uses(q)
                if i is not None:
                    before = before + i * (PAIR_CHUNKS // NSLOT)
                pe.wait_ge(slot_landed[s], (before + 1) * 16)
                return s, ring[:, s, :].rearrange("p (k n) -> p k n", n=n)

            def free_unit(l, u):
                if u >= 4:
                    pe.wait_ge(*emptied(l, u - 4))

            def tile_unit(l, u, weights, acts, nk):
                free_unit(l, u)
                for half in range(2):
                    for k in range(nk):
                        last = pe.matmul(ps[:, bank(u) + half, 0:HALF], weights(k),
                                         acts(k)[:, half * HALF:(half + 1) * HALF],
                                         start=(k == 0), stop=(k == nk - 1))
                return last.then_inc(unit_full.sem, 1)

            def project(l, q, u0):
                for j in range(2):
                    s, w = chunk(l, q + j, CC)
                    for f in range(2):
                        last = tile_unit(l, u0 + 2 * j + f, lambda k: w[:, k, f * P:(f + 1) * P],
                                         lambda k: h[:, k, :], KD)
                    release(s)

            def release(s):
                pe.drain()
                pe.sem_inc(slot_used[s], 1)

            def project_tokens(l, q, u0):
                two = [chunk(l, q + j, CC) for j in range(2)]
                for t in range(NTILE):
                    free_unit(l, u0 + t)
                    for j, (s, w) in enumerate(two):
                        for k in range(KD):
                            last = pe.matmul(ps[:, bank(u0 + t), j * CC:(j + 1) * CC], h[:, k, t * P:(t + 1) * P],
                                             w[:, k, :], start=(k == 0), stop=(k == KD - 1))
                    last.then_inc(unit_full.sem, 1)
                for s, _ in two:
                    release(s)

            def rope_rows(l, u0, src, first):
                for i in range(HM):
                    free_unit(l, u0 + i)
                    pe.wait_ge(*emptied(l, u0 - HM + i))
                    pe.matmul(ps[:, bank(u0 + i), :], rotate, src[:, i, TP:T], start=True, stop=True)\
                        .then_inc(unit_full.sem, 1)

            def head_sums(l, u0, n0, lhs, tmp):
                for i in range(KB):
                    pe.wait_ge(*sq_ready.at(l, n0 + i + 1))
                    tile_unit(l, u0 + i, lambda k: lhs, lambda k: tmp[:, i, :], 1)

            def modulation(l):
                def turn(r):
                    pe.wait_ge(*mod_row_copied.at(l, r + 1))
                    pe.sem_inc(pe_passed, 1)
                    for f in range(4):
                        last = pe.transpose(ps[:, 0, 2 * (4 * r + f):2 * (4 * r + f) + 2],
                                            mod_row[:, r % 2, f * P:(f + 1) * P], ident[0:2, 0:2])
                    return last

                for q in range(ADA_CHUNKS):
                    s, w = chunk(l, q, CC)
                    r = q // 2
                    if q % 2 == 0 and r >= 2:
                        pe.wait_ge(*mod_row_copied.at(l, r - 1))
                    for k in range(KD):
                        last = pe.matmul(ps[0:2, 4 + r % 2, (q % 2) * CC:(q % 2 + 1) * CC], silu_c[:, k, :],
                                         w[:, k, :], start=(k == 0), stop=(k == KD - 1))
                    last.then_inc(slot_used[s], 1)
                    if q % 2:
                        pe.drain()
                        pe.sem_inc(mod_row_ps.sem, 1)
                        if r:
                            turn(r - 1)
                turn(ADA_CHUNKS // 2 - 1).then_inc(mod_ps.sem, 1)

            def x_sums(l, r):
                for k in range(KD):
                    pe.wait_ge(*x_sq.at(l, r * KD + k + 1))
                    for half in range(2):
                        last = pe.matmul(ps[:, 2 + half, 0:HALF], ones, h[:, k, half * HALF:(half + 1) * HALF],
                                         start=(k == 0), stop=(k == KD - 1))
                last.then_inc(x_ss.sem, 1)

            def mlstm(l):
                def scores(s):
                    g, hd, d = steps[s]
                    n = g * HM + hd
                    if s:
                        pe.wait_ge(*w_ready.at(l, e_before[s]))
                    lo, hi = SEG[g]
                    for i in range((hi - lo) // P):
                        last = pe.matmul(ps[:, i, 0:hi - lo], mk[:, hd, lo + i * P:lo + (i + 1) * P],
                                         mq[:, hd, lo:hi], start=True, stop=True)
                    last.then_inc(st_ready.sem, 1)

                def broadcasts(s):
                    g, hd, d = steps[s]
                    lo, hi = SEG[g]
                    if s:
                        pe.wait_ge(*w_ready.at(l, e_before[s]))
                        pe.wait_ge(*am_ready.at(l, s))
                    pick = ident[0:8, d * HM + hd:d * HM + hd + 1].to_broadcast([8, P])
                    pe.matmul(ps[:, 4, 0:hi - lo], pick, rowB[0:8, d, lo:hi], start=True, stop=True)
                    pe.matmul(ps[:, 5, 0:hi - lo], pick, rowM[0:8, d, lo:hi], start=True, stop=True)\
                        .then_inc(bc_ready.sem, 1)

                def sums(s):
                    g, hd, d = steps[s]
                    lo, hi = SEG[g]
                    tiles = stiles(g, d)
                    if s:
                        pe.wait_ge(*h_done.at(l, s))
                    for j, (i, t0, t1) in enumerate(tiles):
                        pe.wait_ge(*w_ready.at(l, e_before[s] + j + 1))
                        w = wmat[:, s % 2, i, t0:t1]
                        end = g == 0
                        pe.matmul(ps[:, 6, t0:t1], mv[:, lo // P + i, hd * P:(hd + 1) * P], w,
                                  start=(j == 0), stop=end)
                        last = pe.matmul(ps[:, 7, t0:t1], ones, w, start=(j == 0), stop=end)
                    if g:
                        pe.wait_ge(*qi_ready.at(l, s - 8 + 1))
                        pe.matmul(ps[:, 6, :], c0s[:, d * HM + hd, :], qi[:, s % 2, :], start=False, stop=True)
                        last = pe.matmul(ps[:, 7, :],
                                         par[:, Q_N0 + d * HM + hd:Q_N0 + d * HM + hd + 1].to_broadcast([P, P]),
                                         qi[:, s % 2, :], start=False, stop=True)
                    last.then_inc(nd_ready.sem, 1)

                def final_states():
                    pe.wait_ge(*w_ready.at(l, e_before[8]))
                    for hd in range(HM):
                        last = pe.transpose(ps[:, 0, hd * P:(hd + 1) * P], mk[:, hd, 0:TP], ident)
                    last.then_inc(ktok_ps.sem, 1)
                    pe.wait_ge(*ktok_ready.at(l, 1))
                    for g in range(8):
                        hd = g % HM
                        pe.wait_ge(*vw_ready.at(l, g + 1))
                        if g >= 2:
                            pe.wait_ge(*state_copied.at(l, g - 1))
                        pe.matmul(ps[:, 1 + g % 2, 0:129], ktok[:, hd, :], vw[:, g % 2, :], start=True, stop=True)\
                            .then_inc(state_ps.sem, 1)
                    pe.wait_ge(*state_copied.at(l, 8))

                for s in range(16):
                    if s == 8:
                        sums(7)
                        final_states()
                    if steps[s][2] == 0:
                        scores(s)
                    broadcasts(s)
                    if s and s != 8:
                        sums(s - 1)
                sums(15)

            def attention(l):
                def scores(s):
                    n, g = asteps[s]
                    for a in range(4):
                        hd = 4 * g + a
                        lo = DN * (hd % 2)
                        j = hd // 2
                        if s:
                            pe.wait_ge(*score_max.at(l, s))
                        if n is None:
                            last = pe.matmul(ps[:, a, 0:P], nq[lo:lo + DN, j, 0:TP], nk[lo:lo + DN, j, 0:TP],
                                             start=True, stop=True)
                        else:
                            kg = nk[lo:lo + DN, j, TP:T].rearrange("p (r c) -> p r c", c=GRID)
                            qblk = nq[lo:lo + DN, j, TP + n * P:TP + (n + 1) * P]
                            pe.matmul(ps[:, a, 0:WINK], qblk, kg[:, :, BAND0[n]:BAND0[n] + KBAND],
                                      start=True, stop=True)
                            last = pe.matmul(ps[:, a, WINK:NKEY], qblk, cks[lo:lo + DN, j, :],
                                             start=True, stop=True)
                        last.then_inc(score_ps.sem, 1)

                def outputs(s):
                    n, g = asteps[s]
                    nb = s // 2
                    nt = 1 if n is None else 3

                    def turn(a):
                        r = 4 * s + a
                        pe.wait_ge(*prob_ready.at(l, r + 1))
                        if r >= 2:
                            pe.wait_ge(*probT_ready.at(l, r - 1))
                        for i in range(nt):
                            last = pe.transpose(ps[:, 4 + r % 2, i * P:(i + 1) * P],
                                                prob[:, s % 2, a, i * P:(i + 1) * P], ident)
                        last.then_inc(probT_ps.sem, 1)

                    def weigh(a):
                        r = 4 * s + a
                        hd = 4 * g + a
                        lo = DN * (hd % 2)
                        pe.wait_ge(*probT_ready.at(l, r + 1))
                        for i in range(nt):
                            if n is None:
                                v = nvp[:, hd * DN:(hd + 1) * DN]
                            elif i < 2:
                                v = vband[:, n % 2, i, hd * DN:(hd + 1) * DN]
                            else:
                                v = cvs[:, hd * DN:(hd + 1) * DN]
                            last = pe.matmul(ps[lo:lo + DN, 6 + nb % 2, (hd // 2) * P:(hd // 2 + 1) * P], v,
                                             probT[:, r % 2, i * P:(i + 1) * P],
                                             start=(i == 0), stop=(i == nt - 1))
                        return last

                    if g == 0 and nb >= 2:
                        pe.wait_ge(*att_copied.at(l, nb - 1))
                    if n is not None and g == 0:
                        pe.wait_ge(*band_in[n % 2].at(l, 2 * (n // 2) + 2))
                    turn(0)
                    for a in range(4):
                        if a < 3:
                            turn(a + 1)
                        last = weigh(a)
                    if g == 1:
                        last.then_inc(att_ps.sem, 1)

                for s in range(10):
                    if s == 2:
                        pe.wait_ge(*ctx_in.at(l, 2))
                    scores(s)
                    if s:
                        outputs(s - 1)
                outputs(9)

            def convolution(l):
                for j in range(2):
                    slots = [chunk(l, R_CONV + 3 * j + b, CC) for b in range(3)]
                    for f in range(2):
                        for b, (s, w) in enumerate(slots):
                            tile_unit(l, U_CV + 3 * (2 * j + f) + b, lambda k: w[:, k, f * P:(f + 1) * P],
                                      lambda k: h[:, k, :], KD)
                    pe.drain()
                    for s, _ in slots:
                        pe.sem_inc(slot_used[s], 1)

            def merge(l):
                for b, y in enumerate((y_ml, y_cv, y_na)):
                    if b == 0:
                        pe.wait_ge(*yml_ready.at(l, KB))
                    if b == 1:
                        pe.wait_ge(*conv_done.at(l, KB))
                    if b == 2:
                        pe.wait_ge(*att_copied.at(l, 5))
                    for j in range(2):
                        sp, wp = chunk(l, R_MERGE + 6 * b + 3 * j, 512)
                        for g in range(2):
                            sg, wgt = chunk(l, R_MERGE + 6 * b + 3 * j + 1 + g, CC)
                            for f in range(2):
                                dt = 4 * j + 2 * g + f
                                u = U_MG + 2 * (b * KD + dt)
                                tile_unit(l, u, lambda k: wgt[:, k, f * P:(f + 1) * P], lambda k: h[:, k, :], KD)
                                tile_unit(l, u + 1, lambda k: wp[:, k, dt % 4 * P:(dt % 4 + 1) * P],
                                          lambda k: y[:, k, :], KB)
                            release(sg)
                        release(sp)

            def mix_out(l):
                pe.wait_ge(*merged_ready.at(l, 24))
                for j in range(4):
                    s, w = chunk(l, R_O + j, CC)
                    for f in range(2):
                        tile_unit(l, U_WO + 2 * j + f, lambda k: w[:, k, f * P:(f + 1) * P],
                                  lambda k: merged[:, k, :], KD)
                    release(s)

            def route(l):
                for t in range(NTILE):
                    for k in range(KD):
                        last = pe.matmul(ps[:, 0, t * NE:(t + 1) * NE], h[:, k, t * P:(t + 1) * P], wr[:, k, :],
                                         start=(k == 0), stop=(k == KD - 1))
                last.then_inc(logit_ps.sem, 1)
                for n in range(2 * NTILE):
                    t, half = n // 2, n % 2
                    if n >= 4:
                        pe.wait_ge(*tok_copied.at(l, n - 3))
                    for k in range(4):
                        last = pe.transpose(ps[:, 4 + n % 4, k * P:(k + 1) * P],
                                            h[:, 4 * half + k, t * P:(t + 1) * P], ident)
                    last.then_inc(tok_ps.sem, 1)
                pe.wait_ge(*aff_ready.at(l, 1))
                for t in range(NTILE):
                    last = pe.transpose(ps[0:NE, 1 + t // 4, (t % 4) * P:(t % 4 + 1) * P], aff[:, t, :], ident)
                last.then_inc(affT_ps.sem, 1)
                pe.wait_ge(*pos_ready.at(l, 1))
                pe.sem_inc(pe_passed, 1)
                for t in range(NTILE):
                    last = pe.transpose(ps[:, 3, t * NE:(t + 1) * NE], pos_r[0:NE, t * P:(t + 1) * P],
                                        ident[0:NE, 0:NE])
                last.then_inc(posT_ps.sem, 1)

            def gather(n, j):
                if j == 0:
                    pe.wait_ge(pick_ready.sem, n + 1)
                for dt in range(3 * j, min(3 * j + 3, KD)):
                    out = ps[:, 2 + j, (dt % 3) * 2 * CAP:(dt % 3 + 1) * 2 * CAP]\
                        .rearrange("p (e c) -> p e c", e=2)
                    for t in range(1, NTILE):
                        pe.matmul(out[:, :, 0:CAP_S], h_tok[:, t, dt * P:(dt + 1) * P],
                                  pick_s[:, t - 1, :, :], start=(t == 1), stop=(t == NTILE - 1))
                    last = pe.matmul(out[:, :, CAP_S:CAP], h_tok[:, 0, dt * P:(dt + 1) * P],
                                     pick_p[:, :, 0:CAP_P], start=True, stop=True)
                last.then_inc(gather_ps.sem, 1)

            def turn_scatter(n):
                pe.wait_ge(gated_ready.sem, n + 1)
                for t in range(NTILE - 1):
                    pe.transpose(ps[:, 2, t * P:(t + 1) * P],
                                 gated_s[:, t, :, :].rearrange("p e c -> p (e c)"), ident)
                pe.transpose(ps[0:64, 3, 0:TP], gated_p[:, :, :].rearrange("p e c -> p (e c)"), ident)\
                    .then_inc(scat_ps.sem, 1)

            def spread_context(n):
                pe.wait_ge(down_copied.sem, 4 * n + 4)
                for dt in range(KD):
                    last = pe.matmul(ps[:, 2 if dt < 4 else 7, dt % 4 * TP:(dt % 4 + 1) * TP],
                                     y_p[0:64, dt * P:(dt + 1) * P], scat_p[0:64, :], start=True, stop=True)
                last.then_inc(context_spread.sem, 1)

            def spread(n, dt):
                if dt >= 2:
                    pe.wait_ge(x_added.sem, KD * n + dt - 1)
                pe.matmul(ps[:, dt % 2, :], y_s[:, dt * P:(dt + 1) * P], scat_s, start=True, stop=True)\
                    .then_inc(spread_ps.sem, 1)

            def expert(l, i, e, first, last_pair):
                n = l * NPAIR + i
                m = n * 2 + e

                def turn_act(half):
                    pe.wait_ge(act_ready.sem, 2 * m + half + 1)
                    for f in range(4):
                        last = pe.transpose(ps[:, 7, f * CAP:(f + 1) * CAP],
                                            act_row[0:CAP, half, f * P:(f + 1) * P], ident[0:CAP, 0:CAP])
                    last.then_inc(actT_ps.sem, 1)

                for c, (w, kh, nh) in enumerate(expert_chunks):
                    q = EXP_CHUNKS * e + c
                    s = q % NSLOT
                    if c == 0 and e == 1:
                        pe.wait_ge(scat_ready.sem, n + 1)
                    if c == 8:
                        pe.wait_ge(actT_ready.sem, 2 * m + 1)
                        if e == 0 and not first:
                            pe.wait_ge(x_added.sem, KD * n)
                    if c == 10:
                        pe.wait_ge(actT_ready.sem, 2 * m + 2)
                    if c in (8, 9) and not (first and e == 0):
                        pe.wait_ge(down_copied.sem, 2 * m - 1 + nh)
                    if c < 8:
                        b = 3 + 2 * nh + (w is w_up)
                        a_hi, a_lo = xg_hi[:, :, e, :], xg_lo[:, :, e, :]
                    else:
                        b = nh
                        a_hi, a_lo = act_hi[:, e, :, :], act_lo[:, e, :, :]
                    hi = w_hi[:, q % 2, :].rearrange("p (k n) -> p k n", k=4)
                    lo = w_lo[:, q % 2, :].rearrange("p (k n) -> p k n", k=4)
                    pe.wait_ge(hi_ready, n * PAIR_CHUNKS + q + 1)
                    for k in range(4):
                        pe.matmul(ps[0:CAP, b, :], a_hi[:, 4 * kh + k, :], hi[:, k, :],
                                  start=(kh == 0 and k == 0), stop=False)
                    pe.wait_ge(slot_used[s], l * SLOT_LAYER[s] + slot_uses(R_EXP + q) + 1
                               + i * (PAIR_CHUNKS // NSLOT) + 1)
                    for k in range(4):
                        last = pe.matmul(ps[0:CAP, b, :], a_lo[:, 4 * kh + k, :], hi[:, k, :],
                                         start=False, stop=False)
                    last.then_inc(hi_used[q % 2], 1)
                    for k in range(4):
                        last = pe.matmul(ps[0:CAP, b, :], a_hi[:, 4 * kh + k, :], lo[:, k, :],
                                         start=False, stop=(kh == 1 and k == 3))
                    last.then_inc(lo_used[q % 2], 1)
                    if c in (3, 7):
                        pe.drain()
                        pe.sem_inc(up_ps.sem, 1)
                    if c in (10, 11):
                        pe.drain()
                        pe.sem_inc(down_ps.sem, 1)
                    if e == 0 and not first:
                        if c == 1:
                            spread_context(n - 1)
                        if 2 <= c <= 5:
                            spread(n - 1, 2 * c - 4)
                            spread(n - 1, 2 * c - 3)
                    if c == 5:
                        if e == 0 and not first:
                            pe.wait_ge(context_added.sem, n)
                        turn_act(0)
                    if c == 9:
                        turn_act(1)
                    if e == 0 and c == 9:
                        turn_scatter(n)
                    if e == 1 and not last_pair and 7 <= c <= 9:
                        gather(n + 1, c - 7)

            def pair(l, i, first=False, last_pair=False):
                pe.wait_ge(xg_ready.sem, 3 * (l * NPAIR + i) + 3)
                for e in range(2):
                    expert(l, i, e, first, last_pair)

            for s in range(NSLOT):
                pe.sem_inc(slot_used[s], 1)
            for b in range(2):
                pe.sem_inc(hi_used[b], 1)
                pe.sem_inc(lo_used[b], 1)
            pe.wait_ge(cond_ready, 1)
            with pe.Fori(0, DEPTH) as l:
                modulation(l)
                x_sums(l, 0)
                pe.wait_ge(*h_ready.at(l, KD))
                project(l, R_MQ, U_MQ)
                rope_rows(l, U_RQ, mq, 0)
                project(l, R_MK, U_MK)
                rope_rows(l, U_RK, mk, HM)
                project_tokens(l, R_MV, U_MV)
                for j in range(2):
                    u = U_G + j
                    free_unit(l, u)
                    for half in range(2):
                        for k in range(KD):
                            last = pe.matmul(ps[0:8, bank(u) + half, 0:HALF], wg16[:, k, 8 * j:8 * j + 8],
                                             h[:, k, half * HALF:(half + 1) * HALF],
                                             start=(k == 0), stop=(k == KD - 1))
                    last.then_inc(unit_full.sem, 1)
                pe.wait_ge(*rows_ready.at(l, 1))
                pe.wait_ge(*roped.at(l, 2 * HM))
                pe.sem_inc(pe_passed, 1)
                for d in range(2):
                    for t in range(NTILE):
                        last = pe.transpose(ps[:, 0, (d * NTILE + t) * 8:(d * NTILE + t + 1) * 8],
                                            rowA[0:8, d, t * P:(t + 1) * P], ident[0:8, 0:8])
                last.then_inc(acol_ps.sem, 1)
                pe.wait_ge(*acol_ready.at(l, 1))
                mlstm(l)
                pe.wait_ge(*h_done.at(l, 16))
                head_sums(l, U_NORM, 0, ones, ml_tmp)
                project(l, R_MO, U_MO)
                project(l, R_NQ, U_NQ)
                head_sums(l, U_SQ, HM, blkones, na_tmp)
                project(l, R_NK, U_NK)
                head_sums(l, U_SK, HM + KB, blkones, na_tmp)
                project_tokens(l, R_NV, U_NV)
                pe.wait_ge(*head_normed.at(l, 12))
                pe.wait_ge(*emptied(l, U_NV + NTILE - 1))
                attention(l)
                pe.wait_ge(*att_copied.at(l, 5))
                convolution(l)
                merge(l)
                mix_out(l)
                pe.wait_ge(*x_mixed.at(l, KD))
                x_sums(l, 1)
                pe.wait_ge(*h_ready.at(l, 2 * KD))
                route(l)
                pe.wait_ge(*tok_copied.at(l, 10))
                pe.wait_ge(*posT_ready.at(l, 1))
                for j in range(3):
                    gather(l * NPAIR, j)
                pair(l, 0, first=True)
                with pe.Fori(1, NPAIR - 1) as i:
                    pair(l, i)
                pair(l, NPAIR - 1, last_pair=True)
                spread_context(l * NPAIR + NPAIR - 1)
                for dt in range(KD):
                    spread(l * NPAIR + NPAIR - 1, dt)
                pe.wait_ge(x_added.sem, (l + 1) * KD * NPAIR)
                pe.wait_ge(context_added.sem, (l + 1) * NPAIR)

        @block.scalar
        def _(act):
            def gathered_hi(n, j):
                w = 3 if j < 2 else 2
                act.wait_ge(gather_ps.sem, 3 * n + j + 1)
                act.activation(xg_hi[:, 3 * j:3 * j + w, :, :].rearrange("p a e c -> p (a e c)"),
                               ps[:, 2 + j, 0:w * 2 * CAP], ACT.Copy).then_inc(xg_hi_ready.sem, 1)

            def outputs(m, e, half):
                act.wait_ge(down_ps.sem, 2 * m + half + 1)
                act.activation(y_s[64 * e:64 * e + CAP_S, half * 512:(half + 1) * 512],
                               ps[0:CAP_S, half, :], ACT.Copy)
                act.activation(y_p[32 * e:32 * e + CAP_P, half * 512:(half + 1) * 512],
                               ps[CAP_S:CAP, half, :], ACT.Copy).then_inc(down_copied.sem, 1)

            def pair(l, i, first=False, last_pair=False):
                n = l * NPAIR + i
                for e in range(2):
                    m = 2 * n + e
                    for c in range(EXP_CHUNKS):
                        q = EXP_CHUNKS * e + c
                        s = q % NSLOT
                        act.wait_ge(slot_landed[s], (l * SLOT_LAYER[s] + slot_uses(R_EXP + q)
                                                     + i * (PAIR_CHUNKS // NSLOT) + 1) * 16)
                        act.wait_ge(hi_used[q % 2], n * (PAIR_CHUNKS // 2) + q // 2 + 1)
                        act.activation(w_hi[:, q % 2, :], ring[:, s, :], ACT.Copy).then_inc(hi_ready, 1)
                        if c < 2 and not (first and e == 0):
                            outputs(m - 1, 1 - e, c)
                        if c in (5, 9):
                            half = (c - 5) // 4
                            act.wait_ge(up_ps.sem, 2 * m + half + 1)
                            act.activation(silu_t[0:CAP, :], ps[0:CAP, 3 + 2 * half, :], ACT.Silu)\
                                .then_inc(silu_ready.sem, 1)
                        if c in (7, 10):
                            half = (c - 7) // 3
                            act.wait_ge(actT_ps.sem, 2 * m + half + 1)
                            act.activation(act_hi[:, e, 4 * half:4 * half + 4, :].rearrange("p f c -> p (f c)"),
                                           ps[:, 7, 0:4 * CAP], ACT.Copy).then_inc(actT_hi.sem, 1)
                        if e == 1 and not last_pair and c >= 9:
                            gathered_hi(n + 1, c - 9)

            def square_x(l, r):
                for k in range(KD):
                    act.activation(h[:, k, :], x[:, k, :], ACT.Square).then_inc(x_sq.sem, 1)

            def norm_x(l, r):
                act.wait_ge(*x_ss.at(l, r + 1))
                act.activation(cols(rstd[:, :]), ps[:, 2:4, 0:HALF], ACT.Sqrt, bias=eps[:, :], scale=1.0 / D)\
                    .then_inc(x_root.sem, 1)
                act.wait_ge(*scale_ready.at(l, 2))
                a, b0 = (a1, 0) if r == 0 else (a2, 24)
                for k in range(KD):
                    act.wait_ge(*x_normed.at(l, r * KD + k + 1))
                    for g, (lo, hi) in enumerate(SEG):
                        last = act.activation(h[:, k, lo:hi], h[:, k, lo:hi], ACT.Identity,
                                              bias=mod[:, b0 + k, g:g + 1], scale=a[:, k, g:g + 1])
                    last.then_inc(h_ready.sem, 1)

            def empty(l, u, out, bias, func=ACT.Identity, scale=1.0):
                act.wait_ge(*unit_full.at(l, u + 1))
                return act.activation(cols(out), pair_ps(u), func, bias=bias, scale=scale)\
                    .then_inc(act_emptied.sem, 1)

            def empty_queries(l, u, out, bias):
                act.wait_ge(*unit_full.at(l, u + 1))
                b = bank(u)
                act.activation(out[:, 0:TP], ps[:, b, 0:TP], ACT.Identity, bias=bias)
                blocks = out[:, TP:T].rearrange("p (n r c) -> p r n c", n=NBLK, r=ROWS)
                cut = (HALF - TP) // GRID
                for r0, r1, src in ((0, cut, ps[:, b, TP:HALF]), (cut, ROWS, ps[:, b + 1, 0:HALF])):
                    src = src.rearrange("p (r n c) -> p r n c", n=NBLK, c=QB)
                    for r in range(r0, r1):
                        last = act.activation(blocks[:, r, :, :], src[:, r - r0, :, :], ACT.Identity, bias=bias)
                last.then_inc(act_emptied.sem, 1)

            def bcol(i):
                return par[:, Q_BIN + i:Q_BIN + i + 1]

            def head_roots(l, u0, tmp, scale):
                for i in range(KB):
                    empty(l, u0 + i, tmp[:, i, :], eps[:, :], ACT.Sqrt, scale)
                    act.drain()
                    act.sem_inc(root_ready.sem, 1)

            def mlstm(l):
                for s, (g, hd, d) in enumerate(steps):
                    if s == 8:
                        act.wait_ge(*ktok_ps.at(l, 1))
                        act.activation(ktok, ps[:, 0, :].rearrange("p (a b) -> p a b", a=HM), ACT.Copy,
                                       scale=ML_SCALE).then_inc(ktok_ready.sem, 1)
                        for c in range(8):
                            act.wait_ge(*state_ps.at(l, c + 1))
                            act.activation(cout[:, c, :], ps[:, 1 + c % 2, 0:129], ACT.Copy)\
                                .then_inc(state_copied.sem, 1)
                    if s == 9:
                        act.wait_ge(*state_out.at(l, 3))
                    lo, hi = SEG[g]
                    n = hi - lo
                    act.wait_ge(*bc_ready.at(l, s + 1))
                    act.wait_ge(*z_ready.at(l, s + 1))
                    if s >= 2:
                        act.wait_ge(*nd_ready.at(l, s - 1))
                        act.wait_ge(*h_done.at(l, s - 1))
                    if g:
                        act.activation(qi[:, s % 2, :], ps[:, 4, :], ACT.Exp,
                                       bias=par[:, Q_M0 + d * HM + hd:Q_M0 + d * HM + hd + 1])
                    else:
                        end = TP - 1 if d == 0 else 0
                        act.activation(wend[:, d * HM + hd:d * HM + hd + 1], ps[:, 4, end:end + 1], ACT.Exp,
                                       bias=acol[:, d, 0, d * HM + hd:d * HM + hd + 1])
                    act.activation(emm[:, s % 2, 0:n], ps[:, 5, 0:n], ACT.Exp, scale=-1.0).then_inc(am_ready.sem, 1)
                    for i, t0, t1 in stiles(g, d):
                        bias = acol[:, d, lo // P + i, d * HM + hd:d * HM + hd + 1]
                        dg = i * P
                        last = act.activation(wmat[:, s % 2, i, dg:dg + P], wmat[:, s % 2, i, dg:dg + P], ACT.Exp,
                                              bias=bias)
                        a, b = (dg + P, t1) if d == 0 else (t0, dg)
                        if b > a:
                            last = act.activation(wmat[:, s % 2, i, a:b], ps[:, 4, a:b], ACT.Exp, bias=bias)
                        last.then_inc(e_ready.sem, 1)

            def attention(l):
                def exps(s):
                    n, g = asteps[s]
                    w = TP if n is None else NKEY
                    act.wait_ge(*score_max.at(l, s + 1))
                    for a in range(4):
                        last = act.activation(prob[:, s % 2, a, 0:w], prob[:, s % 2, a, 0:w], ACT.Exp,
                                              bias=mx[:, s % 2, a:a + 1], accum_out=rs[:, s % 2, a:a + 1])
                    last.then_inc(prob_exp.sem, 1)

                def copies(s):
                    w = TP if asteps[s][0] is None else NKEY
                    for a in range(4):
                        r = 4 * s + a
                        act.wait_ge(*probT_ps.at(l, r + 1))
                        act.activation(probT[:, r % 2, 0:w], ps[:, 4 + r % 2, 0:w], ACT.Copy)\
                            .then_inc(probT_ready.sem, 1)

                for s in range(10):
                    exps(s)
                    if s:
                        copies(s - 1)
                copies(9)

            act.wait_ge(start_in, 48)
            act.activation(silu_c[:, :, :], silu_c[:, :, :], ACT.Silu).then_inc(cond_ready, 1)
            act.wait_ge(consts_set, 1)
            with act.Fori(0, DEPTH) as l:
                act.wait_ge(*params_in.at(l, 5))
                for r in range(ADA_CHUNKS // 2):
                    act.wait_ge(*mod_row_ps.at(l, r + 1))
                    act.activation(mod_row[:, r % 2, :], ps[0:2, 4 + r % 2, :], ACT.Copy)\
                        .then_inc(mod_row_copied.sem, 1)
                square_x(l, 0)
                norm_x(l, 0)
                for i in range(HM):
                    empty(l, U_MQ + i, mq[:, i, :], bcol(B_MQ + i))
                for i in range(HM):
                    empty(l, U_MK + i, mk[:, i, :], bcol(B_MK + i))
                act.wait_ge(*lf_abs.at(l, 1))
                act.activation(row_t[0:8, :], row_t[0:8, :], ACT.Exp, scale=-1.0)
                act.drain()
                act.activation(row_t[0:8, :], row_t[0:8, :], ACT.Ln, bias=1.0).then_inc(lf_log.sem, 1)
                act.wait_ge(*acol_ps.at(l, 1))
                act.activation(acol[:, :, :, :].rearrange("p a b c -> p (a b c)"), ps[:, 0, 0:80], ACT.Copy)\
                    .then_inc(acol_ready.sem, 1)
                act.drain()
                mlstm(l)
                act.wait_ge(*h_done.at(l, 16))
                for i in range(HM):
                    act.activation(ml_tmp[:, i, :], y_ml[:, i, :], ACT.Square).then_inc(sq_ready.sem, 1)
                head_roots(l, U_NORM, ml_tmp, 1.0 / P)
                for i in range(KB):
                    empty(l, U_MO + i, sig_mo[:, i, :], bcol(B_MO + i), ACT.Sigmoid)
                for u0, us, b0, dst in ((U_NQ, U_SQ, B_NQ, nq), (U_NK, U_SK, B_NK, nk)):
                    for i in range(KB):
                        if dst is nk:
                            empty(l, u0 + i, dst[:, i, :], bcol(b0 + i))
                        else:
                            empty_queries(l, u0 + i, dst[:, i, :], bcol(b0 + i))
                    act.drain()
                    if dst is nk:
                        act.wait_ge(*head_normed.at(l, HM + KB))
                    for i in range(KB):
                        act.activation(na_tmp[:, i, :], dst[:, i, :], ACT.Square).then_inc(sq_ready.sem, 1)
                    head_roots(l, us, na_tmp, 1.0 / DN)
                attention(l)
                for i in range(KB):
                    empty(l, U_CV + 3 * i, cc_t[:, i, :], bcol(B_CC + i))
                for i in range(3 * KD):
                    if i >= 2:
                        act.wait_ge(*merged_ready.at(l, i - 1))
                    empty(l, U_MG + 2 * i, gate_t[:, i % 2, :], bcol(B_GT + i), ACT.Sigmoid)
                act.wait_ge(*x_mixed.at(l, KD))
                square_x(l, 1)
                norm_x(l, 1)
                act.wait_ge(*logit_shift.at(l, 1))
                act.activation(aff[:, :, :], aff[:, :, :], ACT.Exp).then_inc(logit_exp.sem, 1)
                for n in range(2 * NTILE):
                    t, half = n // 2, n % 2
                    act.wait_ge(*tok_ps.at(l, n + 1))
                    act.activation(h_tok[:, t, half * 512:(half + 1) * 512], ps[:, 4 + n % 4, :], ACT.Copy)\
                        .then_inc(tok_copied.sem, 1)
                for j in range(3):
                    gathered_hi(l * NPAIR, j)
                pair(l, 0, first=True)
                with act.Fori(1, NPAIR - 1) as i:
                    pair(l, i)
                pair(l, NPAIR - 1, last_pair=True)
                for half in range(2):
                    outputs(2 * NPAIR * (l + 1) - 1, 1, half)
                act.wait_ge(*layer_x.at(l, 1))

        @block.vector
        def _(dve):
            def root_x(l, r):
                dve.wait_ge(*x_root.at(l, r + 1))
                dve.reciprocal(rstd[:, :], rstd[:, :])
                dve.drain()
                for k in range(KD):
                    dve.tensor_tensor(h[:, k, :], x[:, k, :], rstd[:, :], ALU.mult).then_inc(x_normed.sem, 1)

            def rope(l, u0, dst):
                for i in range(HM):
                    dve.wait_ge(*unit_full.at(l, u0 + i + 1))
                    dve.tensor_tensor(rope_tmp, ps[:, bank(u0 + i), :], sinT, ALU.mult).then_inc(dve_emptied.sem, 1)
                    dve.tensor_tensor(dst[:, i, TP:T], dst[:, i, TP:T], cosT, ALU.mult)
                    dve.drain()
                    dve.tensor_tensor(dst[:, i, TP:T], dst[:, i, TP:T], rope_tmp, ALU.add).then_inc(roped.sem, 1)
                    dve.drain()

            def gate_rows(l):
                dve.tensor_scalar(rbias[:, :], rowpar[:, 1:2], rowpar[:, 2:3], None, ALU.add)
                dve.memset(row_zero[0:8, :], 0.0)
                dve.drain()
                dve.wait_ge(*unit_full.at(l, U_G + 1))
                dve.tensor_scalar(cols(row_ig[0:8, :]), ps[0:8, bank(U_G):bank(U_G) + 2, 0:HALF], rowpar[:, 0:1],
                                  None, ALU.add).then_inc(dve_emptied.sem, 1)
                b = bank(U_G + 1)
                dve.wait_ge(*unit_full.at(l, U_G + 2))
                dve.tensor_scalar(cols(row_lf[0:8, :]), ps[0:8, b:b + 2, 0:HALF], rbias[:, :], None, ALU.add)\
                    .then_inc(dve_emptied.sem, 1)
                dve.drain()
                dve.scalar_tensor_tensor(row_t[0:8, :], row_lf[0:8, :], -1.0, row_lf[0:8, :], ALU.mult, ALU.max)\
                    .then_inc(lf_abs.sem, 1)
                dve.wait_ge(*lf_log.at(l, 1))
                dve.scalar_tensor_tensor(row_lf[0:8, :], row_lf[0:8, :], 0.0, row_t[0:8, :], ALU.min, ALU.subtract)
                dve.drain()
                for d in range(2):
                    for g, (lo, hi) in enumerate(SEG):
                        order = slice(lo, hi) if d == 0 else (slice(hi - 1, lo - 1 if lo else None, -1))
                        dve.tensor_tensor_scan(rowB[0:8, d, order], row_lf[0:8, order], row_zero[0:8, order], 0.0,
                                               ALU.add, ALU.add)
                        dve.tensor_tensor_scan(rowM[0:8, d, order], row_lf[0:8, order], row_ig[0:8, order],
                                               rowpar[:, 3:4] if g else 0.0, ALU.add, ALU.max)
                dve.drain()
                for d in range(2):
                    dve.tensor_tensor(rowA[0:8, d, :], row_ig[0:8, :], rowB[0:8, d, :], ALU.subtract)
                dve.drain()
                for d in range(2):
                    last = dve.tensor_tensor(rowB[0:8, d, :], rowB[0:8, d, :], rowM[0:8, d, :], ALU.subtract)
                last.then_inc(rows_ready.sem, 1)

            def mlstm(l):
                def weights(s):
                    g, hd, d = steps[s]
                    lo, hi = SEG[g]
                    dve.wait_ge(*bc_ready.at(l, s + 1))
                    if s >= 2:
                        dve.wait_ge(*nd_ready.at(l, s - 1))
                    if s == 9:
                        dve.wait_ge(*state_out.at(l, 3))
                    w = wmat[:, s % 2, :, :].rearrange("p a b -> p (a b)")
                    if g == 0:
                        dve.tensor_tensor(w[:, 0:P], ps[:, 4, 0:P], tri(d), ALU.add).then_inc(z_ready.sem, 1)
                    else:
                        dve.tensor_tensor(
                            w[:, 0:1920].rearrange("p (i c) -> p i c", c=640)[:, :, 0:P],
                            ps[:, 4, 0:384].rearrange("p (i c) -> p i c", c=P),
                            tri(d)[:, None, :].to_broadcast([P, 3, P]), ALU.add)
                        dve.tensor_tensor(w[:, 1920:2048], ps[:, 4, 384:512], tri(d), ALU.add)\
                            .then_inc(z_ready.sem, 1)
                        dve.wait_ge(*am_ready.at(l, s + 1))
                        dve.tensor_tensor(qi[:, s % 2, :], mq[:, hd, TP:T], qi[:, s % 2, :], ALU.mult)\
                            .then_inc(qi_ready.sem, 1)
                    dve.wait_ge(*st_ready.at(l, s // 2 + 1))
                    for j, (i, t0, t1) in enumerate(stiles(g, d)):
                        dve.wait_ge(*e_ready.at(l, e_before[s] + j + 1))
                        dve.scalar_tensor_tensor(wmat[:, s % 2, i, t0:t1], ps[:, i, t0:t1], ML_SCALE,
                                                 wmat[:, s % 2, i, t0:t1], ALU.mult, ALU.mult)\
                            .then_inc(w_ready.sem, 1)

                def divide(s):
                    g, hd, d = steps[s]
                    lo, hi = SEG[g]
                    n = hi - lo
                    e = emm[:, s % 2, 0:n]
                    dve.wait_ge(*am_ready.at(l, s + 1))
                    dve.wait_ge(*nd_ready.at(l, s + 1))
                    dve.scalar_tensor_tensor(e, ps[:, 7, 0:n], -1.0, e, ALU.mult, ALU.max)
                    dve.drain()
                    dve.tensor_tensor(e, ps[:, 7, 0:n], e, ALU.max)
                    dve.drain()
                    dve.reciprocal(e, e)
                    dve.drain()
                    if d == 0:
                        dve.tensor_tensor(y_ml[:, hd, lo:hi], ps[:, 6, 0:n], e, ALU.mult).then_inc(h_done.sem, 1)
                    else:
                        dve.tensor_tensor(e, ps[:, 6, 0:n], e, ALU.mult)
                        dve.drain()
                        dve.tensor_tensor(y_ml[:, hd, lo:hi], y_ml[:, hd, lo:hi], e, ALU.add)\
                            .then_inc(h_done.sem, 1)

                for s in range(16):
                    if s == 8:
                        divide(7)
                        for c in range(8):
                            hd = c % HM
                            if c >= 2:
                                dve.wait_ge(*state_ps.at(l, c - 1))
                            dve.tensor_scalar(vw[:, c % 2, 0:P], mv[:, 0, hd * P:(hd + 1) * P], wend[:, c:c + 1],
                                              None, ALU.mult)
                            dve.tensor_copy(vw[:, c % 2, P:P + 1], wend[:, c:c + 1]).then_inc(vw_ready.sem, 1)
                    weights(s)
                    if s and s != 8:
                        divide(s - 1)
                divide(15)

            def norm_heads(l, n0, dst, tmp, gain):
                for i in range(KB):
                    dve.wait_ge(*root_ready.at(l, n0 + i + 1))
                    dve.reciprocal(tmp[:, i, :], tmp[:, i, :])
                    dve.drain()
                    dve.scalar_tensor_tensor(dst[:, i, :], dst[:, i, :], gain(i), tmp[:, i, :], ALU.mult, ALU.mult)\
                        .then_inc(head_normed.sem, 1)

            def add_row_bias(l, u, out, at):
                dve.wait_ge(*unit_full.at(l, u + 1))
                return dve.tensor_tensor(out, ps[:, bank(u), :], par[:, Q_BV + at:Q_BV + at + WB], ALU.add)

            def attention(l):
                def maxima(s):
                    n, g = asteps[s]
                    w = TP if n is None else NKEY
                    if s >= 2:
                        dve.wait_ge(*probT_ps.at(l, 4 * (s - 1)))
                    if n is not None:
                        dve.wait_ge(*bias_ready.at(l, s - 1))
                    for a in range(4):
                        dve.wait_ge(*score_ps.at(l, 4 * s + a + 1))
                        dve.sem_inc(dve_passed, 1)
                        add = bias_t[:, 0, a, WINK:NKEY] if n is None else bias_t[:, s % 2, a, :]
                        dve.tensor_tensor_reduce(prob[:, s % 2, a, 0:w], ps[:, a, 0:w], add, 1.0, -3.0e38,
                                                 ALU.add, ALU.max, mx[:, s % 2, a:a + 1])
                    dve.drain()
                    dve.tensor_scalar(mx[:, s % 2, :], mx[:, s % 2, :], -1.0, None, ALU.mult)\
                        .then_inc(score_max.sem, 1)

                def scale(s):
                    w = TP if asteps[s][0] is None else NKEY
                    dve.wait_ge(*prob_exp.at(l, s + 1))
                    dve.reciprocal(rs[:, s % 2, :], rs[:, s % 2, :])
                    dve.drain()
                    for a in range(4):
                        dve.tensor_scalar(prob[:, s % 2, a, 0:w], prob[:, s % 2, a, 0:w], rs[:, s % 2, a:a + 1],
                                          None, ALU.mult).then_inc(prob_ready.sem, 1)

                def copy_out(nb):
                    dve.wait_ge(*att_ps.at(l, nb + 1))
                    src = ps[:, 6 + nb % 2, :].rearrange("p (j q) -> p j q", j=KB)
                    if nb == 0:
                        dve.tensor_copy(y_na[:, :, 0:TP], src).then_inc(att_copied.sem, 1)
                    else:
                        n = nb - 1
                        for j in range(KB):
                            last = dve.tensor_copy(
                                y_na[:, j, TP:T].rearrange("p (r c) -> p r c", c=GRID)[:, :, n * QB:(n + 1) * QB],
                                src[:, j, :].rearrange("p (r c) -> p r c", c=QB))
                        last.then_inc(att_copied.sem, 1)

                for s in range(10):
                    maxima(s)
                    scale(s)
                    if s % 2 == 1 and s >= 3:
                        copy_out(s // 2 - 1)
                copy_out(4)

            def convolution(l):
                for lo in (0, TP + 2):
                    dve.memset(u_pad[:, lo:lo + 1], 0.0)
                dve.memset(u_pad[:, TP + 1:TP + 2], 0.0)
                dve.memset(u_pad[:, T + 3:T + 4], 0.0)
                for i in range(KB):
                    dve.wait_ge(*emptied(l, U_CV + 3 * i))
                    u = U_CV + 3 * i + 1
                    dve.wait_ge(*unit_full.at(l, u + 1))
                    dve.scalar_tensor_tensor(cols(conv_t), pair_ps(u), par[:, Q_BIN + B_CH + i:Q_BIN + B_CH + i + 1],
                                             cols(cc_t[:, i, :]), ALU.add, ALU.mult).then_inc(dve_emptied.sem, 1)
                    dve.drain()
                    dve.tensor_copy(u_pad[:, 1:TP + 1], conv_t[:, 0:TP])
                    dve.tensor_copy(u_pad[:, TP + 3:T + 3], conv_t[:, TP:T])
                    dve.drain()
                    for j in range(3):
                        tap = par[:, Q_CW + 4 * j + i:Q_CW + 4 * j + i + 1]
                        for (lo, hi), at in zip(SEG, (j, j + 2)):
                            src = u_pad[:, lo + at:hi + at]
                            if j == 0:
                                dve.tensor_scalar(conv_t[:, lo:hi], src, tap, None, ALU.mult)
                            else:
                                dve.scalar_tensor_tensor(conv_t[:, lo:hi], src, tap, conv_t[:, lo:hi],
                                                         ALU.mult, ALU.add)
                        dve.drain()
                    u = U_CV + 3 * i + 2
                    dve.wait_ge(*unit_full.at(l, u + 1))
                    dve.scalar_tensor_tensor(cols(y_cv[:, i, :]), pair_ps(u),
                                             par[:, Q_BIN + B_CB + i:Q_BIN + B_CB + i + 1], cols(conv_t),
                                             ALU.add, ALU.mult).then_inc(dve_emptied.sem, 1)
                    dve.drain()
                    dve.sem_inc(conv_done.sem, 1)

            def merge(l):
                for i in range(3 * KD):
                    dt = i % KD
                    dve.wait_ge(*emptied(l, U_MG + 2 * i))
                    dve.wait_ge(*unit_full.at(l, U_MG + 2 * i + 2))
                    out = merged[:, dt, :] if i < KD else prod_t
                    dve.tensor_tensor(cols(out), pair_ps(U_MG + 2 * i + 1), cols(gate_t[:, i % 2, :]), ALU.mult)\
                        .then_inc(dve_emptied.sem, 1)
                    dve.drain()
                    if i >= KD:
                        dve.tensor_tensor(merged[:, dt, :], merged[:, dt, :], prod_t, ALU.add)
                        dve.drain()
                    dve.sem_inc(merged_ready.sem, 1)

            def mix_in(l):
                for k in range(KD):
                    u = U_WO + k
                    b = bank(u)
                    dve.wait_ge(*unit_full.at(l, u + 1))
                    for g, half, lo, hi in ((0, 0, 0, TP), (1, 0, TP, HALF), (1, 1, 0, HALF)):
                        t = half * HALF
                        last = dve.scalar_tensor_tensor(
                            x[:, k, t + lo:t + hi], ps[:, b + half, lo:hi], mod[:, 16 + k, g:g + 1],
                            x[:, k, t + lo:t + hi], ALU.mult, ALU.add)
                    last.then_inc(dve_emptied.sem, 1)
                dve.drain()
                dve.sem_inc(x_mixed.sem, KD)

            def route(l):
                lg = ps[:, 0, 0:NTILE * NE].rearrange("p (t e) -> p t e", e=NE)
                dve.wait_ge(*logit_ps.at(l, 1))
                dve.tensor_reduce(smax, lg, AX.X, ALU.max)
                dve.drain()
                dve.tensor_tensor(aff[:, :, :], lg, smax[:, :, None].to_broadcast([P, NTILE, NE]), ALU.subtract)\
                    .then_inc(logit_shift.sem, 1)
                dve.wait_ge(*logit_exp.at(l, 1))
                dve.tensor_reduce(smax, aff[:, :, :], AX.X, ALU.add)
                dve.drain()
                dve.reciprocal(smax, smax)
                dve.drain()
                dve.tensor_tensor(aff[:, :, :], aff[:, :, :], smax[:, :, None].to_broadcast([P, NTILE, NE]),
                                  ALU.mult).then_inc(aff_ready.sem, 1)
                dve.wait_ge(*affT_ps.at(l, 1))
                dve.tensor_copy(work[0:NE, 0:512], ps[0:NE, 1, :])
                dve.tensor_copy(work[0:NE, 512:T], ps[0:NE, 2, 0:P])
                dve.drain()
                for (lo, hi), cap in zip(SEG, (CAP_P, CAP_S)):
                    for r in range(cap // 8):
                        dve.max(top8[0:NE, :], work[0:NE, lo:hi])
                        dve.drain()
                        dve.match_replace(work[0:NE, lo:hi], top8[0:NE, :], work[0:NE, lo:hi], -1.0)
                        dve.drain()
                dve.tensor_scalar(mask_r[0:NE, :], work[0:NE, :], 0.0, None, ALU.is_lt)
                dve.drain()
                dve.memset(work[0:NE, :], 0.0)
                dve.drain()
                for lo, hi in SEG:
                    dve.tensor_tensor_scan(pos_r[0:NE, lo:hi], mask_r[0:NE, lo:hi], work[0:NE, lo:hi], 0.0,
                                           ALU.add, ALU.add)
                dve.drain()
                dve.tensor_tensor(pos_r[0:NE, :], pos_r[0:NE, :], mask_r[0:NE, :], ALU.mult)
                dve.drain()
                dve.tensor_scalar(pos_r[0:NE, :], pos_r[0:NE, :], -1.0, None, ALU.add).then_inc(pos_ready.sem, 1)
                dve.wait_ge(*posT_ps.at(l, 1))
                dve.tensor_copy(posT[:, :, :].rearrange("p t e -> p (t e)"), ps[:, 3, 0:NTILE * NE])\
                    .then_inc(posT_ready.sem, 1)
                dve.memset(y_p[0:64, :], 0.0)
                dve.drain()

            def picks(n, first_expert):
                lat = [P, NTILE - 1, 2, CAP_S]
                con = [P, 2, 32]
                two = bass.ds(first_expert, 2)
                pos_s = posT[:, 1:NTILE, two][:, :, :, None].to_broadcast(lat)
                aff_s = aff[:, 1:NTILE, two][:, :, :, None].to_broadcast(lat)
                pos_p = posT[:, 0, two][:, :, None].to_broadcast(con)
                aff_p = aff[:, 0, two][:, :, None].to_broadcast(con)
                dve.tensor_tensor(pick_s[:, :, :, :], iota[:, None, None, :].to_broadcast(lat), pos_s, ALU.is_equal)
                dve.tensor_tensor(pick_p[:, :, :], iota[:, None, 0:32].to_broadcast(con), pos_p, ALU.is_equal)\
                    .then_inc(pick_ready.sem, 1)
                dve.drain()
                dve.tensor_tensor(gated_s[:, :, :, :], pick_s[:, :, :, :], aff_s, ALU.mult)
                dve.tensor_tensor(gated_p[:, :, :], pick_p[:, :, :], aff_p, ALU.mult).then_inc(gated_ready.sem, 1)

            def gathered_lo(n, j):
                w = 3 if j < 2 else 2
                at = slice(3 * j, 3 * j + w)
                dve.wait_ge(xg_hi_ready.sem, 3 * n + j + 1)
                dve.tensor_tensor(xg_lo[:, at, :, :].rearrange("p a e c -> p (a e c)"),
                                  ps[:, 2 + j, 0:w * 2 * CAP],
                                  xg_hi[:, at, :, :].rearrange("p a e c -> p (a e c)").bitcast(F32),
                                  ALU.subtract).then_inc(xg_ready.sem, 1)

            def add_context(n):
                dve.wait_ge(context_spread.sem, n + 1)
                for dt in range(KD):
                    last = dve.scalar_tensor_tensor(
                        x[:, dt, 0:TP], ps[:, 2 if dt < 4 else 7, dt % 4 * TP:(dt % 4 + 1) * TP],
                        mod[:, 40 + dt, 0:1], x[:, dt, 0:TP], ALU.mult, ALU.add)
                last.then_inc(context_added.sem, 1)

            def add_latent(n, dt):
                dve.wait_ge(spread_ps.sem, KD * n + dt + 1)
                dve.scalar_tensor_tensor(x[:, dt, TP:T], ps[:, dt % 2, :], mod[:, 40 + dt, 1:2], x[:, dt, TP:T],
                                         ALU.mult, ALU.add).then_inc(x_added.sem, 1)

            def pair(l, i, first=False, last_pair=False):
                n = l * NPAIR + i
                for e in range(2):
                    m = 2 * n + e
                    for c in range(EXP_CHUNKS):
                        q = EXP_CHUNKS * e + c
                        if e == 0 and not first:
                            if c == 3:
                                add_context(n - 1)
                            if 4 <= c <= 7:
                                add_latent(n - 1, 2 * c - 8)
                                add_latent(n - 1, 2 * c - 7)
                        if e == 0 and c == 11:
                            dve.wait_ge(scat_ps.sem, n + 1)
                            dve.tensor_copy(scat_s, ps[:, 2, :])
                            dve.tensor_copy(scat_p[0:64, :], ps[0:64, 3, 0:TP]).then_inc(scat_ready.sem, 1)
                        dve.wait_ge(hi_ready, n * PAIR_CHUNKS + q + 1)
                        dve.wait_ge(lo_used[q % 2], n * (PAIR_CHUNKS // 2) + q // 2 + 1)
                        dve.tensor_tensor(w_lo[:, q % 2, :], ring[:, q % NSLOT, :], w_hi[:, q % 2, :].bitcast(F32),
                                          ALU.subtract).then_inc(slot_used[q % NSLOT], 1)
                        if e == 1 and not last_pair and c == 3:
                            picks(n + 1, 2 * i + 2)
                        if c in (5, 9):
                            half = (c - 5) // 4
                            dve.wait_ge(silu_ready.sem, 2 * m + half + 1)
                            dve.tensor_tensor(act_row[0:CAP, half, :], ps[0:CAP, 4 + 2 * half, :], silu_t[0:CAP, :],
                                              ALU.mult).then_inc(act_ready.sem, 1)
                        if c in (7, 10):
                            half = (c - 7) // 3
                            dve.wait_ge(actT_hi.sem, 2 * m + half + 1)
                            at = slice(4 * half, 4 * half + 4)
                            dve.tensor_tensor(act_lo[:, e, at, :].rearrange("p f c -> p (f c)"),
                                              ps[:, 7, 0:4 * CAP],
                                              act_hi[:, e, at, :].rearrange("p f c -> p (f c)").bitcast(F32),
                                              ALU.subtract).then_inc(actT_ready.sem, 1)
                        if e == 1 and not last_pair and c >= 9:
                            gathered_lo(n + 1, c - 9)

            dve.memset(eps[:, :], EPS).then_inc(consts_set, 1)
            dve.wait_ge(start_in, 48)
            with dve.Fori(0, DEPTH) as l:
                dve.wait_ge(*params_in.at(l, 5))
                dve.wait_ge(*mod_ps.at(l, 1))
                dve.tensor_tensor(mod[:, :, :], ps[:, 0, 0:96].rearrange("p (a b) -> p a b", b=2),
                                  par[:, Q_ADAB:Q_ADAB + 48][:, :, None].to_broadcast([P, 48, 2]), ALU.add)
                dve.tensor_scalar(gq[:, :], par[:, Q_GQ:Q_GQ + 1], DN ** -0.5, None, ALU.mult)
                dve.drain()
                for a, c, g in ((a1, 8, Q_G1), (a2, 32, Q_G2)):
                    dve.scalar_tensor_tensor(a[:, :, :], mod[:, c:c + 8, :], 1.0,
                                             par[:, g:g + 8][:, :, None].to_broadcast([P, 8, 2]),
                                             ALU.add, ALU.mult).then_inc(scale_ready.sem, 1)
                root_x(l, 0)
                rope(l, U_RQ, mq)
                rope(l, U_RK, mk)
                for t in range(NTILE):
                    add_row_bias(l, U_MV + t, mv[:, t, :], 0).then_inc(dve_emptied.sem, 1)
                gate_rows(l)
                mlstm(l)
                norm_heads(l, 0, y_ml, ml_tmp, lambda i: par[:, Q_OG + i:Q_OG + i + 1])
                for i in range(KB):
                    dve.drain()
                    dve.wait_ge(*emptied(l, U_MO + i))
                    dve.tensor_tensor(y_ml[:, i, :], y_ml[:, i, :], sig_mo[:, i, :], ALU.mult)\
                        .then_inc(yml_ready.sem, 1)
                norm_heads(l, HM, nq, na_tmp, lambda i: gq[:, :])
                norm_heads(l, HM + KB, nk, na_tmp, lambda i: par[:, Q_GK:Q_GK + 1])
                for t in range(NTILE):
                    if t >= 3:
                        dve.wait_ge(*nv_stored[t % 2].at(l, t - 2))
                    out = nvp if t == 0 else nvst[:, t % 2, :]
                    add_row_bias(l, U_NV + t, out, WB).then_inc(dve_emptied.sem, 1)
                    dve.drain()
                    dve.sem_inc(nv_staged.sem, 1)
                for b in range(2):
                    last = dve.memset(bias_t[:, b, :, WINK:NKEY], 0.0)
                dve.drain()
                dve.sem_inc(bias_zeroed.sem, 1)
                attention(l)
                convolution(l)
                merge(l)
                mix_in(l)
                root_x(l, 1)
                route(l)
                picks(l * NPAIR, 0)
                for j in range(3):
                    gathered_lo(l * NPAIR, j)
                pair(l, 0, first=True)
                with dve.Fori(1, NPAIR - 1) as i:
                    pair(l, i)
                pair(l, NPAIR - 1, last_pair=True)
                add_context(l * NPAIR + NPAIR - 1)
                for dt in range(KD):
                    add_latent(l * NPAIR + NPAIR - 1, dt)
                dve.drain()
                dve.sem_inc(layer_x.sem, 1)


def constants():
    k = np.zeros((P, NCONST), np.float32)
    k[:, K_ID:K_ID + P] = np.eye(P)
    k[:, K_ONE:K_ONE + P] = 1.0
    for b in range(2):
        k[64 * b:64 * b + 64, K_BLK + 64 * b:K_BLK + 64 * b + 64] = 1.0
    half = 32
    freqs = (np.float32(10000.0) ** (-np.arange(half, dtype=np.float32) / np.float32(half))).astype(np.float32)
    t = np.arange(TS)
    for b, pos in enumerate(((t // GRID).astype(np.float32), (t % GRID).astype(np.float32))):
        ang = freqs[:, None] * pos[None, :]
        for s in range(2):
            at = 64 * b + 32 * s
            k[at:at + 32, K_COS:K_COS + TS] = np.cos(ang)
            k[at:at + 32, K_SIN:K_SIN + TS] = np.sin(ang)
        for i in range(half):
            k[64 * b + 32 + i, K_ROT + 64 * b + i] = -1.0
            k[64 * b + i, K_ROT + 64 * b + 32 + i] = 1.0
    s, q = np.arange(P)[:, None], np.arange(P)[None, :]
    k[:, K_TRI:K_TRI + P] = np.where(q >= s, 0.0, -1e30)
    k[:, K_TRI + P:K_TRI + 2 * P] = np.where(q <= s, 0.0, -1e30)
    for n in range(NBLK):
        qcol = n * QB + np.arange(P)[:, None] % QB
        start = np.clip(qcol - 8, 0, GRID - 16)
        kcol = BAND0[n] + np.arange(KBAND)[None, :]
        k[:, K_MASK + n * KBAND:K_MASK + (n + 1) * KBAND] = np.where((kcol >= start) & (kcol < start + 16), 0.0, -1e30)
    k[:, K_IOTA:K_IOTA + CAP_S] = np.arange(CAP_S)
    return k


def kernel(**inputs):
    import numpy as np
    import concourse.bacc as bacc
    from concourse import mybir
    from concourse.bass_utils import run_bass_kernel_spmd as run

    a = {n: np.ascontiguousarray(v) for n, v in inputs.items()}
    f32 = np.float32
    xT = np.concatenate([a["x_prompt"][0].T, a["x_sample"][0].T], axis=1)
    cond = np.stack([a["c_ctx"], a["c"][0]], axis=1)

    def cols(v):
        return v.reshape(DEPTH, -1, P).transpose(0, 2, 1)

    b_in = a["b_in"]
    b_main = np.concatenate([b_in[:, :C_G], b_in[:, C_CB:]], axis=1)
    fm = a["ml_fbias"].reshape(DEPTH, 8)
    m0 = a["state_mlstm_m"][0].reshape(DEPTH, 8)
    twice = lambda v: np.concatenate([v, v], axis=1)[:, :, None]
    prm = np.concatenate([
        cols(a["ada_b"]), cols(a["norm1_g"]), cols(a["norm2_g"]), cols(b_main), cols(a["ml_out_g"]),
        cols(a["cv_w"].reshape(DEPTH, -1)), twice(a["na_q_g"]), twice(a["na_k_g"]),
        np.broadcast_to(m0[:, None, :], (DEPTH, P, 8)),
        a["state_mlstm_n"][0].reshape(DEPTH, 8, P).transpose(0, 2, 1),
        np.broadcast_to(b_in[:, None, C_MV:C_MV + WB], (DEPTH, P, WB)),
        np.broadcast_to(b_in[:, None, C_NV:C_NV + WB], (DEPTH, P, WB))], axis=2)
    rowp = np.stack([b_in[:, C_G:C_G + 8], b_in[:, C_G + 8:C_G + 16], fm, m0], axis=2)
    rpb = np.pad(a["na_rpb"], ((0, 0), (0, 0), (0, 0), (16, 16)))
    r, q = np.arange(P) // QB, np.arange(P) % QB
    dr = np.arange(ROWS)[None, :] - r[:, None] + 7
    biasT = np.stack([
        rpb[:, :, dr[:, :, None],
            (np.arange(KBAND)[None, :] + BAND0[n] - n * QB - q[:, None] + 15 + 16)[:, None, :]]
        for n in range(NBLK)], axis=1)
    biasT = biasT.transpose(0, 1, 3, 2, 4, 5).reshape(DEPTH, NBLK, P, HN, WINK)
    arrays = {
        "xT": xT, "cond": cond, "const": constants(), "prm": prm, "rowp": rowp, "biasT": biasT,
        "ckT": a["cache_ctx_k"][0].reshape(DEPTH, P, WB).transpose(0, 2, 1),
        "cv": a["cache_ctx_v"][0].reshape(DEPTH, P, WB),
        "c0": a["state_mlstm_c"][0].reshape(DEPTH, 8, P, P),
        **{n: a[n] for n in ("ada_w", "w_in", "w_pa", "w_pb", "w_pc", "w_o", "w_router", "w_gate", "w_up", "w_down")},
    }
    nc = bacc.Bacc("TRN2", target_bir_lowering=False, num_devices=1)
    nc.disable_value_cache = True
    aps = []
    arrays = {n: np.ascontiguousarray(v) for n, v in arrays.items()}
    for n, v in arrays.items():
        aps.append(nc.dram_tensor(n, v.shape, mybir.dt.from_np(v.dtype), kind="ExternalInput").ap())
    outs = {"yT": (D, T), "new_k": (DEPTH, WB, TP), "new_v": (DEPTH, TP, WB), "new_cn": (DEPTH, 8, P, P + 1), "new_m": (DEPTH, 8, 1)}
    for n, s in outs.items():
        aps.append(nc.dram_tensor(n, s, mybir.dt.float32, kind="ExternalOutput").ap())
    aps.append(nc.dram_tensor("nv_copy", (TS, WB), mybir.dt.float32, kind="Internal").ap())
    step_program(nc, *aps)
    res = run(nc, [arrays], core_ids=[0]).results[0]
    yT = res["yT"]
    return (yT[:, :TP].T[None], yT[:, TP:].T[None],
            res["new_k"].transpose(0, 2, 1).reshape(1, DEPTH, TP, HN, DN),
            res["new_v"].reshape(1, DEPTH, TP, HN, DN),
            res["new_cn"][..., :P].reshape(1, DEPTH, 2, HM, P, P),
            res["new_cn"][..., P].reshape(1, DEPTH, 2, HM, P),
            res["new_m"].reshape(1, DEPTH, 2, HM))
```

```python
import concourse.bass as bass
from concourse import mybir
from contextlib import ExitStack
import numpy as np

F32 = mybir.dt.float32
F32R = mybir.dt.float32r
ALU = mybir.AluOpType
ACT = mybir.ActivationFunctionType
AX = mybir.AxisListType

P = 128
D = 1024
KD = D // P
DEPTH = 2
TP, TS = 128, 512
T = TP + TS
HALF = T // 2
NTILE = T // P
GRID = 64
ROWS = TS // GRID
HM = 4
HN, DN = 8, 64
WB = 512
KB = WB // P
NBLK, QB, KBAND = 4, 16, 32
NE, FF = 16, 1024
CAP_P, CAP_S = 2 * TP // NE, 2 * TS // NE
CAP = CAP_S + CAP_P
NPAIR = NE // 2
EPS = 1e-6
ML_SCALE = float(P) ** -0.5
BAND0 = [min(max(16 * n - 8, 0), GRID - KBAND) for n in range(NBLK)]
WINK = ROWS * KBAND
NKEY = WINK + P

C_MQ, C_MK, C_MV, C_MO, C_G = 0, 512, 1024, 1536, 2048
C_CB, C_CC, C_CH = 2064, 2576, 3088
C_NQ, C_NK, C_NV, C_GT = 3600, 4112, 4624, 5136
PROJ = C_GT + 3 * D

Q_ADAB, Q_G1, Q_G2, Q_BIN = 0, 48, 56, 64
Q_OG, Q_CW, Q_GQ, Q_GK, Q_M0, Q_N0 = 128, 132, 144, 145, 146, 154
Q_BV = 162
NPRM = Q_BV + 2 * WB
B_MQ, B_MK, B_MO, B_CB, B_CC, B_CH, B_NQ, B_NK, B_GT = 0, 4, 12, 16, 20, 24, 28, 32, 40

K_ID, K_ONE, K_BLK, K_ROT, K_COS, K_SIN = 0, 128, 256, 384, 512, 1024
K_TRI, K_MASK, K_IOTA = 1536, 1792, 1920
NCONST = 1984

NSLOT = 4
CHUNK = 2048
CC = CHUNK // KD
ADA_CHUNKS = 6 * D // CC
GC = P
(R_MQ, R_G, R_MK, R_MV, R_MO, R_NQ, R_NK, R_NV) = range(ADA_CHUNKS, ADA_CHUNKS + 16, 2)
R_CONV = R_NV + 2
R_MERGE = R_CONV + 6
R_O = R_MERGE + 18
R_END = R_O + 4
R_EXP = -(-R_END // NSLOT) * NSLOT
EXP_CHUNKS = 12
PAIR_CHUNKS = 2 * EXP_CHUNKS
SPLITS = list(range(R_MQ, R_MERGE)) + [R_MERGE + 3 * (g // 2) + 2 * (g % 2) for g in range(12)] \
    + list(range(R_O, R_O + 4))
MIX_SPLITS = len(SPLITS)
SPLIT_LAYER = MIX_SPLITS + NPAIR * PAIR_CHUNKS
assert MIX_SPLITS % 2 == 0


def slot_uses(q):
    return sum(1 for c in range(q % NSLOT, q, NSLOT) if c < R_END or c >= R_EXP)


SLOT_LAYER = [slot_uses(R_EXP + NPAIR * PAIR_CHUNKS + s) for s in range(NSLOT)]


class Signal:

    def __init__(self, sem, per_layer, unit=1):
        self.sem, self.per_layer, self.unit = sem, per_layer, unit

    def at(self, l, k):
        return self.sem, (l * self.per_layer + k) * self.unit


def step_program(nc, xT, cond, const, prm, rowp, biasT, ckT, cv, c0, ada_w, w_in, w_pa, w_pb, w_pc,
                 w_o, w_router, w_gate, w_up, w_down, yT, new_k, new_v, new_cn, new_m, nv_dram, x_dram):
    with ExitStack() as ctx:
        def sb(name, shape, dtype=F32):
            return ctx.enter_context(nc.sbuf_tensor(name, shape, dtype))

        def signal(name, per_layer, unit=1):
            return Signal(ctx.enter_context(nc.semaphore(name)), per_layer, unit)

        def semaphore(name):
            return ctx.enter_context(nc.semaphore(name))

        ring = sb("ring", [P, NSLOT, CHUNK])
        w_hi = sb("w_hi", [P, 2, CHUNK], F32R)
        w_lo = sb("w_lo", [P, 2, CHUNK], F32R)
        with nc.sbuf_tensor("x", [P, KD, T], F32) as x:
            pass
        h_hi = sb("h_hi", [P, KD, T], F32R)
        with nc.sbuf_tensor("h", [P, KD, T], F32) as h:
            pass
        h_lo = sb("h_lo", [P, KD, T], F32R)
        cst = sb("cst", [P, NCONST])
        par = sb("par", [P, NPRM])
        rowpar = sb("rowpar", [8, 4])
        silu_c = sb("silu_c", [P, KD, 2])
        mod = sb("mod", [P, 48, 2])
        a1 = sb("a1", [P, KD, 2])
        a2 = sb("a2", [P, KD, 2])
        eps = sb("eps", [P, 1])
        acol = sb("acol", [P, 2, NTILE, 8])
        wr = sb("wr", [P, KD, NE])
        gq = sb("gq", [P, 1])
        rbias = sb("rbias", [8, 1])
        wend = sb("wend", [P, 8])
        mx = sb("mx", [P, 2, 4])
        rs = sb("rs", [P, 2, 4])
        rstd = sb("rstd", [P, T])
        ARENA, FF_WORDS = 21760, 13312
        arena_space = ExitStack()
        arena = arena_space.enter_context(nc.sbuf_tensor("arena", [P, ARENA], F32))
        arena_space.close()
        M_HI = 11520
        with ExitStack() as overlay:
            merged_lo = overlay.enter_context(nc.sbuf_tensor("merged_lo", [P, KD, T], F32R))
            overlay.enter_context(nc.sbuf_tensor("overlay_gap", [P, M_HI - KD * T], F32))
            merged_hi = overlay.enter_context(nc.sbuf_tensor("merged_hi", [P, KD, T], F32R))
        arena_ff = sb("arena_ff", [P, FF_WORDS])
        xg_hi = sb("xg_hi", [P, KD, 2, CAP], F32R)
        xg_lo = sb("xg_lo", [P, KD, 2, CAP], F32R)
        act_hi = sb("act_hi", [P, 2, KD, CAP], F32R)
        act_lo = sb("act_lo", [P, 2, KD, CAP], F32R)
        ctx.enter_context(nc.sbuf_tensor("arena_rest", [P, ARENA - FF_WORDS - 4 * 2 * KD * CAP], F32))
        ps = ctx.enter_context(nc.psum_tensor("ps", [P, 8, 512], F32))

        def view(at, *shape, store=arena, size=ARENA):
            n = int(np.prod(shape))
            assert at + n <= size
            a = store[:, at:at + n]
            if len(shape) == 1:
                return a
            names = "abcd"[:len(shape)]
            return a.rearrange("p (%s) -> p %s" % (" ".join(names), " ".join(names)),
                               **{c: s for c, s in zip(names, shape)})

        ident = cst[:, K_ID:K_ID + P]
        ones = cst[:, K_ONE:K_ONE + P]
        blkones = cst[:, K_BLK:K_BLK + P]
        rotate = cst[:, K_ROT:K_ROT + P]
        cosT = cst[:, K_COS:K_COS + TS]
        sinT = cst[:, K_SIN:K_SIN + TS]
        iota = cst[:, K_IOTA:K_IOTA + CAP_S]

        def tri(d):
            return cst[:, K_TRI + d * P:K_TRI + (d + 1) * P]

        mod_row = view(0, 2, 512)[0:2, :, :]
        Y_TOP = ARENA - KB * T
        y_ml = view(Y_TOP, KB, T)
        y_na = view(Y_TOP - KB * T, KB, T)
        y_cv = view(Y_TOP - 2 * KB * T, KB, T)
        mq = view(0, HM, T)
        mk = view(2560, HM, T)
        mv = view(5120, NTILE, WB)
        rowA = view(7680, 2, T)
        rowB = view(8960, 2, T)
        rowM = view(10240, 2, T)
        W_AT = 11520
        wmat = view(W_AT, 2, 4, 512)
        row_ig, row_lf, row_t, row_zero = (view(W_AT + T * i, T) for i in range(4))
        rope_tmp = view(W_AT + 2560, TS)
        ktok = view(W_AT + 2048, HM, P)
        vw = view(W_AT + 2560, 2, 129)
        cout = view(W_AT + 2818, 8, 129)
        qi = view(W_AT + 4096, 2, TS)
        emm = view(W_AT + 5120, 2, TS)
        c0s = view(W_AT + 6144, 8, P)
        num = view(W_AT + 7168, TS)
        assert W_AT + 7168 + TS <= Y_TOP
        ml_tmp = view(5120, KB, T)
        sig_mo = view(7680, KB, T)
        nq = view(0, KB, T)
        nk = view(2560, KB, T)
        na_tmp = view(10240, KB, T)
        bias_t = view(5120, 2, 4, NKEY)
        prob = view(8192, 2, 4, NKEY)
        vband = view(11264, 2, 2, WB)
        probT = view(13312, 2, NKEY)
        NA_C = 14080
        cks = view(NA_C, KB, P)
        cvs = view(NA_C + 512, WB)
        nvp = view(NA_C + 1024, WB)
        nvst = view(NA_C + 1536, 2, WB)
        assert NA_C + 2560 <= Y_TOP - KB * T
        cc_t = view(5120, KB, T)
        u_pad = view(7680, T + 4)
        conv_t = view(8324, 2, T)
        merged = view(0, KD, T)
        gate_t = view(9728, 2, T)
        prod_t = view(5120, T)
        assert 9728 + 2 * T <= M_HI and M_HI + KD * T <= Y_TOP - KB * T
        def ff(at, *shape):
            return view(at, *shape, store=arena_ff, size=FF_WORDS)

        h_tok = ff(0, NTILE, D)
        aff = ff(5120, NTILE, NE)
        posT = ff(5200, NTILE, NE)
        smax = ff(5280, NTILE)
        affT = ff(5312, T)
        work = ff(5952, T)
        mask_r = ff(6592, T)
        pos_r = ff(7232, T)
        top8 = ff(7872, 8)
        pick_s = ff(7936, NTILE - 1, 2, CAP_S)
        pick_p = ff(8448, 2, 32)
        gated_s = ff(8512, NTILE - 1, 2, CAP_S)
        gated_p = ff(9024, 2, 32)
        scat_s = ff(9088, TS)
        scat_p = ff(9600, TP)
        silu_t = ff(9728, 512)
        y_s = ff(10240, D)
        y_p = ff(11264, D)
        act_row = ff(12288, 2, 512)

        slot_landed = [semaphore(f"slot{s}_landed") for s in range(NSLOT)]
        slot_used = [semaphore(f"slot{s}_used") for s in range(NSLOT)]
        start_in = semaphore("start_in")
        cond_ready = semaphore("cond_ready")
        consts_set = semaphore("consts_set")
        params_in = signal("params_in", 4, 16)
        mod_row_ps = signal("mod_row_ps", ADA_CHUNKS // 2)
        mod_row_copied = signal("mod_row_copied", ADA_CHUNKS // 2)
        mod_ps = signal("mod_ps", 1)
        mod_ready = signal("mod_ready", 1)
        scale_ready = signal("scale_ready", 2)
        x_sq = signal("x_sq", 2 * KD)
        x_ss = signal("x_ss", 2)
        x_root = signal("x_root", 2)
        x_normed = signal("x_normed", 2 * KD)
        h_ready = signal("h_ready", 2 * KD)
        h_split = signal("h_split", KD)
        x_saved = signal("x_saved", 1, 16)
        x_back = signal("x_back", 1, 16)
        layer_x = signal("layer_x", 1)
        unit_full = signal("unit_full", 1)
        act_emptied = signal("act_emptied", 1)
        dve_emptied = signal("dve_emptied", 1)
        rows_ready = signal("rows_ready", 1)
        lf_abs = signal("lf_abs", 1)
        lf_log = signal("lf_log", 1)
        acol_ps = signal("acol_ps", 1)
        acol_ready = signal("acol_ready", 1)
        roped = signal("roped", 2 * HM)
        st_ready = signal("st_ready", 2 * HM)
        bc_ready = signal("bc_ready", 16)
        am_ready = signal("am_ready", 16)
        qe_ready = signal("qe_ready", 16)
        z_ready = signal("z_ready", 16)
        e_ready = signal("e_ready", 40)
        w_ready = signal("w_ready", 40)
        qi_ready = signal("qi_ready", 8)
        nd_ready = signal("nd_ready", 16)
        h_done = signal("h_done", 16)
        num_copied = signal("num_copied", 16)
        den_read = signal("den_read", 16)
        ktok_ps = signal("ktok_ps", 1)
        ktok_ready = signal("ktok_ready", 1)
        vw_ready = signal("vw_ready", 8)
        state_ps = signal("state_ps", 8)
        state_copied = signal("state_copied", 8)
        state_out = signal("state_out", 3, 16)
        sq_ready = signal("sq_ready", 12)
        root_ready = signal("root_ready", 12)
        head_normed = signal("head_normed", 12)
        mo_ready = signal("mo_ready", KB)
        yml_ready = signal("yml_ready", KB)
        nv_staged = signal("nv_staged", NTILE)
        nv_stored = [signal("nv_even_stored", 3, 16), signal("nv_odd_stored", 2, 16)]
        newk_out = signal("newk_out", 1, 16)
        bias_zeroed = signal("bias_zeroed", 1)
        ctx_in = signal("ctx_in", 2, 16)
        band_in = [signal(f"band_in{b}", 4, 16) for b in range(2)]
        bias_in = [signal(f"bias_in{b}", 4, 16) for b in range(2)]
        bias_ready = signal("bias_ready", 8)
        score_ps = signal("score_ps", 40)
        score_max = signal("score_max", 10)
        prob_exp = signal("prob_exp", 40)
        prob_ready = signal("prob_ready", 40)
        probT_ps = signal("probT_ps", 40)
        probT_ready = signal("probT_ready", 40)
        att_ps = signal("att_ps", 5)
        att_copied = signal("att_copied", 5)
        cc_ready = signal("cc_ready", KB)
        conv_done = signal("conv_done", KB)
        gate_ready = signal("gate_ready", 24)
        merged_ready = signal("merged_ready", 24)
        x_mixed = signal("x_mixed", KD)
        tok_ps = signal("tok_ps", 10)
        tok_copied = signal("tok_copied", 10)
        logit_ps = signal("logit_ps", 1)
        logit_shift = signal("logit_shift", 1)
        logit_exp = signal("logit_exp", 1)
        aff_ready = signal("aff_ready", 1)
        affT_ps = signal("affT_ps", 1)
        pos_ready = signal("pos_ready", 1)
        posT_ps = signal("posT_ps", 1)
        posT_ready = signal("posT_ready", 1)
        pick_ready = signal("pick_ready", NPAIR)
        gated_ready = signal("gated_ready", NPAIR)
        scat_ps = signal("scat_ps", NPAIR)
        scat_ready = signal("scat_ready", NPAIR)
        gather_ps = signal("gather_ps", 3 * NPAIR)
        xg_ready = signal("xg_ready", 3 * NPAIR)
        up_ps = signal("up_ps", 2 * NE)
        silu_ready = signal("silu_ready", 2 * NE)
        act_ready = signal("act_ready", 2 * NE)
        down_ps = signal("down_ps", 2 * NE)
        down_copied = signal("down_copied", 2 * NE)
        actT_ps = signal("actT_ps", 2 * NE)
        actT_hi = signal("actT_hi", 2 * NE)
        actT_ready = signal("actT_ready", 2 * NE)
        xg_hi_ready = signal("xg_hi_ready", 3 * NPAIR)
        hi_ready = semaphore("hi_ready")
        hi_used = [semaphore(f"hi{b}_used") for b in range(2)]
        lo_used = [semaphore(f"lo{b}_used") for b in range(2)]
        context_spread = signal("context_spread", NPAIR)
        context_added = signal("context_added", NPAIR)
        spread_ps = signal("spread_ps", KD * NPAIR)
        x_added = signal("x_added", KD * NPAIR)
        stored = semaphore("stored")
        pe_passed = semaphore("pe_passed")
        dve_passed = semaphore("dve_passed")
        pool_passed = semaphore("pool_passed")

        units = []

        def unit(kind, count):
            at = len(units)
            units.extend([kind] * count)
            return at

        U_MQ, U_RQ = unit("act", HM), unit("dve", HM)
        U_G = unit("dve", 2)
        U_MK, U_RK = unit("act", HM), unit("dve", HM)
        U_MV = unit("dve", NTILE)
        U_MO = unit("act", KB)
        U_NORM = unit("act", HM)
        U_NQ, U_NK = unit("act", KB), [unit("act", 2)]
        U_SQ = unit("act", KB)
        U_NK.append(unit("act", 2))
        U_SK = unit("act", KB)
        U_NV = unit("dve", NTILE)
        U_CV = unit("cv", 3 * KB)
        U_MG = unit("mg", 2 * 3 * KD)
        U_WO = unit("dve", KD)
        for j in range(2):
            units[U_CV + 6 * j:U_CV + 6 * j + 6] = ["act"] * 2 + ["dve"] * 4

        def u_conv(i, b):
            return U_CV + 6 * (i // 2) + 2 * b + i % 2

        for i in range(3 * KD):
            units[U_MG + 2 * i:U_MG + 2 * i + 2] = ["act", "dve"]
        act_before = [sum(1 for k in units[:u] if k == "act") for u in range(len(units) + 1)]
        dve_before = [sum(1 for k in units[:u] if k == "dve") for u in range(len(units) + 1)]
        unit_full.per_layer = len(units)
        act_emptied.per_layer = act_before[-1]
        dve_emptied.per_layer = dve_before[-1]

        def bank(u):
            return 2 * (u % 4)

        def emptied(l, u):
            if units[u] == "act":
                return act_emptied.at(l, act_before[u] + 1)
            return dve_emptied.at(l, dve_before[u] + 1)

        def pair_ps(u):
            b = bank(u)
            return ps[:, b:b + 2, 0:HALF]

        def cols(a):
            return a.rearrange("p (a b) -> p a b", a=2)

        SEG = [(0, TP), (TP, T)]
        steps = [(g, hd, d) for g in range(2) for hd in range(HM) for d in range(2)]
        e_before = [0]
        for g, _, _ in steps:
            e_before.append(e_before[-1] + (4 if g else 1))

        def stiles(g, d):
            if g == 0:
                return [(0, 0, P)]
            if d == 0:
                return [(i, i * P, TS) for i in range(4)]
            return [(i, 0, (i + 1) * P) for i in (3, 2, 1, 0)]

        asteps = [(None, 0), (None, 1)] + [(n, g) for n in range(NBLK) for g in range(2)]

        expert_chunks = [(w, kh, nh) for nh in range(2) for w in (w_gate, w_up) for kh in range(2)] + \
                        [(w_down, kh, nh) for kh in range(2) for nh in range(2)]

        block = ctx.enter_context(nc.Block())

        @block.sync
        def _(sp):
            def load(l, q, src, i=None, j=None):
                s = (q if i is None else j) % NSLOT
                before = l * SLOT_LAYER[s] + slot_uses(q)
                if i is not None:
                    before = before + i * (PAIR_CHUNKS // NSLOT)
                sp.wait_ge(slot_used[s], before + 1)
                n = src.shape[2]
                dst = ring[:, s, 0:src.shape[1] * n].rearrange("p (k n) -> p k n", n=n)
                sp.dma_start(dst, src).then_inc(slot_landed[s], 16)

            def rows_of(w, c, n=CC):
                return w.rearrange("(k p) n -> p k n", p=P)[:, :, c:c + n]

            with sp.Fori(0, DEPTH) as l:
                ada_l = ada_w[l, :, :]
                win_l = w_in[l, :, :]
                for q in range(ADA_CHUNKS):
                    load(l, q, rows_of(ada_l, CC * q))
                for j in range(2):
                    load(l, R_MQ + j, rows_of(win_l, C_MQ + CC * j))
                for j in range(2):
                    load(l, R_G + j, rows_of(win_l, C_G + 8 * j, GC))
                for q, c in ((R_MK, C_MK), (R_MV, C_MV), (R_MO, C_MO), (R_NQ, C_NQ),
                             (R_NK, C_NK), (R_NV, C_NV)):
                    for j in range(2):
                        load(l, q + j, rows_of(win_l, c + CC * j))
                for j in range(2):
                    for b, c in enumerate((C_CC, C_CH, C_CB)):
                        load(l, R_CONV + 3 * j + b, rows_of(win_l, c + CC * j))
                for b, w in enumerate((w_pa, w_pb, w_pc)):
                    for j in range(2):
                        first = R_MERGE + 6 * b + 3 * j
                        load(l, first, rows_of(win_l, C_GT + b * D + CC * 2 * j))
                        load(l, first + 1, rows_of(w[l, :, :], 512 * j, 512))
                        load(l, first + 2, rows_of(win_l, C_GT + b * D + CC * (2 * j + 1)))
                for j in range(4):
                    load(l, R_O + j, rows_of(w_o[l, :, :], CC * j))
                with sp.Fori(0, NPAIR) as i:
                    for e in range(2):
                        for j, (w, kh, nh) in enumerate(expert_chunks):
                            load(l, R_EXP + EXP_CHUNKS * e + j,
                                 rows_of(w[l, 2 * i + e, 512 * kh:512 * (kh + 1), :], 512 * nh, 512),
                                 i, EXP_CHUNKS * e + j)

        @block.gpsimd
        def _(pool):
            def split(l, q0, count=2):
                first = SPLITS.index(q0)
                for si in range(first, first + count):
                    q, b = SPLITS[si], si % 2
                    s = q % NSLOT
                    n = KD * GC if R_G <= q < R_G + 2 else CHUNK
                    pool.wait_ge(slot_landed[s], (l * SLOT_LAYER[s] + slot_uses(q) + 1) * 16)
                    pool.wait_ge(hi_used[b], l * (SPLIT_LAYER // 2) + si // 2 + 1)
                    pool.wait_ge(lo_used[b], l * (SPLIT_LAYER // 2) + si // 2 + 1)
                    pool.sem_inc(pool_passed, 1)
                    pool.tensor_copy(w_hi[:, b, 0:n], ring[:, s, 0:n]).then_inc(hi_ready, 1)
                    pool.drain()
                    pool.tensor_tensor(w_lo[:, b, 0:n], ring[:, s, 0:n], w_hi[:, b, 0:n].bitcast(F32),
                                       ALU.subtract).then_inc(slot_used[s], 1)

            pool.dma_start(x[:, :, :], xT.rearrange("(k p) t -> p k t", p=P)).then_inc(start_in, 16)
            pool.dma_start(cst[:, :], const).then_inc(start_in, 16)
            pool.dma_start(silu_c[:, :, :], cond.rearrange("(k p) c -> p k c", p=P)).then_inc(start_in, 16)
            pool.wait_ge(start_in, 48)
            pool.sem_inc(pool_passed, 1)
            with pool.Fori(0, DEPTH) as l:
                pool.dma_start(x_dram, x[:, :, :]).then_inc(x_saved.sem, 16)
                pool.dma_start(par[:, :], prm[l, :, :]).then_inc(params_in.sem, 16)
                pool.dma_start(rowpar[:, :], rowp[l, :, :]).then_inc(params_in.sem, 16)
                pool.dma_start(wr[:, :, :], w_router[l, :, :].rearrange("(k p) e -> p k e", p=P))\
                    .then_inc(params_in.sem, 16)
                pool.dma_start(c0s[:, :, :], c0[l, :, :, :].rearrange("g d v -> d g v")).then_inc(params_in.sem, 16)
                split(l, R_MQ)
                split(l, R_G)
                split(l, R_MK)
                split(l, R_MV)
                pool.wait_ge(*rows_ready.at(l, 1))
                pool.sem_inc(pool_passed, 1)
                pool.dma_start(new_m[l, 0:HM, :], rowM[0:HM, 0, TP - 1:TP]).then_inc(state_out.sem, 16)
                pool.dma_start(new_m[l, HM:8, :], rowM[HM:8, 1, 0:1]).then_inc(state_out.sem, 16)
                split(l, R_MO)
                pool.wait_ge(*state_copied.at(l, 8))
                pool.sem_inc(pool_passed, 1)
                pool.dma_start(new_cn[l, :, :, :].rearrange("g d v -> d g v"), cout).then_inc(state_out.sem, 16)
                pool.wait_ge(*h_done.at(l, 16))
                pool.sem_inc(pool_passed, 1)
                pool.dma_start(cks[:, :, :], ckT[l, :, :].rearrange("(j p) t -> p j t", p=P)).then_inc(ctx_in.sem, 16)
                pool.dma_start(cvs, cv[l, :, :]).then_inc(ctx_in.sem, 16)
                split(l, R_NQ)
                split(l, R_NK)
                split(l, R_NV)
                for t in range(NTILE):
                    pool.wait_ge(*nv_staged.at(l, t + 1))
                    pool.sem_inc(pool_passed, 1)
                    if t == 0:
                        pool.wait_ge(*head_normed.at(l, 12))
                        pool.sem_inc(pool_passed, 1)
                        pool.dma_start(new_k[l, :, :].rearrange("(j p) t -> p j t", p=P), nk[:, :, 0:TP])\
                            .then_inc(newk_out.sem, 16)
                        pool.dma_start(new_v[l, :, :], nvp).then_inc(nv_stored[0].sem, 16)
                    else:
                        pool.dma_start(nv_dram[(t - 1) * P:t * P, :], nvst[:, t % 2, :])\
                            .then_inc(nv_stored[t % 2].sem, 16)
                pool.wait_ge(*nv_stored[0].at(l, 3))
                pool.wait_ge(*nv_stored[1].at(l, 2))
                pool.wait_ge(*bias_zeroed.at(l, 1))
                pool.sem_inc(pool_passed, 1)
                nv_grid = nv_dram.rearrange("(g i c) f -> g i c f", g=2, c=GRID)

                def band_load(n):
                    for g in range(2):
                        pool.dma_start(vband[:, n % 2, g, :], nv_grid[g, :, BAND0[n]:BAND0[n] + KBAND, :])\
                            .then_inc(band_in[n % 2].sem, 16)

                def bias_load(s):
                    n, g = asteps[s + 2]
                    pool.dma_start(bias_t[:, s % 2, :, 0:WINK], biasT[l, n, :, 4 * g:4 * g + 4, :])\
                        .then_inc(bias_in[s % 2].sem, 16)

                band_load(0)
                band_load(1)
                bias_load(0)
                bias_load(1)
                for s in range(8):
                    n, g = asteps[s + 2]
                    pool.wait_ge(*bias_in[s % 2].at(l, s // 2 + 1))
                    pool.tensor_tensor(
                        bias_t[:, s % 2, :, 0:WINK].rearrange("p a (i j) -> p a i j", j=KBAND),
                        bias_t[:, s % 2, :, 0:WINK].rearrange("p a (i j) -> p a i j", j=KBAND),
                        cst[:, K_MASK + n * KBAND:K_MASK + (n + 1) * KBAND][:, None, None, :]
                        .to_broadcast([P, 4, ROWS, KBAND]), ALU.add).then_inc(bias_ready.sem, 1)
                    if 1 <= s <= 6:
                        pool.wait_ge(*score_max.at(l, s + 2))
                        pool.sem_inc(pool_passed, 1)
                        bias_load(s + 1)
                    if s in (3, 5):
                        pool.wait_ge(*att_ps.at(l, (s - 1) // 2 + 1))
                        pool.sem_inc(pool_passed, 1)
                        band_load((s - 1) // 2 + 1)
                    if s == 1:
                        split(l, R_CONV)
                split(l, R_CONV + 2, SPLITS.index(R_O) + 2 - SPLITS.index(R_CONV + 2))
                pool.wait_ge(*unit_full.at(l, U_WO))
                pool.wait_ge(*x_saved.at(l, 1))
                pool.sem_inc(pool_passed, 1)
                pool.dma_start(x[:, :, :], x_dram).then_inc(x_back.sem, 16)
                split(l, R_O + 2)
                pool.wait_ge(*newk_out.at(l, 1))
                pool.wait_ge(*layer_x.at(l, 1))
            pool.dma_start(yT.rearrange("(k p) t -> p k t", p=P), x[:, :, :]).then_inc(stored, 16)
            pool.wait_ge(stored, 16)
            pool.wait_ge(*state_out.at(DEPTH - 1, 3))
            pool.wait_ge(*nv_stored[0].at(DEPTH - 1, 3))
            pool.wait_ge(*newk_out.at(DEPTH - 1, 1))

        @block.tensor
        def _(pe):
            def chunk(l, q, n, i=None, j=None):
                s = (q if i is None else j) % NSLOT
                before = l * SLOT_LAYER[s] + slot_uses(q)
                if i is not None:
                    before = before + i * (PAIR_CHUNKS // NSLOT)
                pe.wait_ge(slot_landed[s], (before + 1) * 16)
                return s, ring[:, s, :].rearrange("p (k n) -> p k n", n=n)

            def free_unit(l, u):
                if u >= 4:
                    pe.wait_ge(*emptied(l, u - 4))

            def tile_unit(l, u, weights, acts, nk):
                free_unit(l, u)
                for half in range(2):
                    for k in range(nk):
                        last = pe.matmul(ps[:, bank(u) + half, 0:HALF], weights(k),
                                         acts(k)[:, half * HALF:(half + 1) * HALF],
                                         start=(k == 0), stop=(k == nk - 1))
                return last.then_inc(unit_full.sem, 1)

            def split_chunk(l, q, n=CC):
                si = SPLITS.index(q)
                s = q % NSLOT
                pe.wait_ge(hi_ready, l * SPLIT_LAYER + si + 1)
                pe.wait_ge(slot_used[s], l * SLOT_LAYER[s] + slot_uses(q) + 2)
                return (si % 2,) + tuple(w[:, si % 2, 0:KD * n].rearrange("p (k n) -> p k n", n=n)
                                         for w in (w_hi, w_lo))

            def leave(b):
                pe.drain()
                pe.sem_inc(hi_used[b], 1)
                pe.sem_inc(lo_used[b], 1)

            def split_unit(l, u, hi, lo, f0, fresh=False, acts=(h_hi, h_lo)):
                free_unit(l, u)
                for half in range(2):
                    at = slice(half * HALF, (half + 1) * HALF)
                    for k in range(KD):
                        if fresh and half == 0:
                            pe.wait_ge(*h_split.at(l, k + 1))
                        for part, (w, a) in enumerate(((hi, acts[0]), (hi, acts[1]), (lo, acts[0]))):
                            last = pe.matmul(ps[:, bank(u) + half, 0:HALF], w[:, k, f0:f0 + P], a[:, k, at],
                                             start=(k == 0 and part == 0), stop=(k == KD - 1 and part == 2))
                return last.then_inc(unit_full.sem, 1)

            def project(l, q, us, fresh=False):
                for j in range(len(us) // 2):
                    b, hi, lo = split_chunk(l, q + j)
                    for f in range(2):
                        split_unit(l, us[2 * j + f], hi, lo, f * P, fresh=fresh and j == 0 and f == 0)
                    leave(b)

            def release(s):
                pe.drain()
                pe.sem_inc(slot_used[s], 1)

            def project_tokens(l, q, u0):
                two = {}
                for t, j in [(t, 0) for t in range(4)] + [(t, 1) for t in range(4)] + [(4, 0), (4, 1)]:
                    if j == 0:
                        free_unit(l, u0 + t)
                    if j not in two:
                        two[j] = split_chunk(l, q + j)
                    _, hi, lo = two[j]
                    at = slice(t * P, (t + 1) * P)
                    for k in range(KD):
                        for part, (a, w) in enumerate(((h_hi, hi), (h_lo, hi), (h_hi, lo))):
                            last = pe.matmul(ps[:, bank(u0 + t), j * CC:(j + 1) * CC], a[:, k, at], w[:, k, :],
                                             start=(k == 0 and part == 0), stop=(k == KD - 1 and part == 2))
                    if j == 1:
                        last.then_inc(unit_full.sem, 1)
                for b, _, _ in two.values():
                    leave(b)

            def rope_rows(l, u0, src, first):
                for i in range(HM):
                    free_unit(l, u0 + i)
                    pe.wait_ge(*emptied(l, u0 - HM + i))
                    pe.matmul(ps[:, bank(u0 + i), :], rotate, src[:, i, TP:T], start=True, stop=True)\
                        .then_inc(unit_full.sem, 1)

            def head_sums(l, u0, n0, lhs, tmp):
                for i in range(KB):
                    pe.wait_ge(*sq_ready.at(l, n0 + i + 1))
                    tile_unit(l, u0 + i, lambda k: lhs, lambda k: tmp[:, i, :], 1)

            def modulation(l):
                def turn(r):
                    pe.wait_ge(*mod_row_copied.at(l, r + 1))
                    pe.sem_inc(pe_passed, 1)
                    for f in range(4):
                        last = pe.transpose(ps[:, 0, 2 * (4 * r + f):2 * (4 * r + f) + 2],
                                            mod_row[:, r % 2, f * P:(f + 1) * P], ident[0:2, 0:2])
                    return last

                for q in range(ADA_CHUNKS):
                    s, w = chunk(l, q, CC)
                    r = q // 2
                    if q % 2 == 0 and r >= 2:
                        pe.wait_ge(*mod_row_copied.at(l, r - 1))
                    for k in range(KD):
                        last = pe.matmul(ps[0:2, 4 + r % 2, (q % 2) * CC:(q % 2 + 1) * CC], silu_c[:, k, :],
                                         w[:, k, :], start=(k == 0), stop=(k == KD - 1))
                    last.then_inc(slot_used[s], 1)
                    if q % 2:
                        pe.drain()
                        pe.sem_inc(mod_row_ps.sem, 1)
                        if r:
                            turn(r - 1)
                        if r == 6:
                            x_sums(l, 0)
                turn(ADA_CHUNKS // 2 - 1).then_inc(mod_ps.sem, 1)

            def x_sums(l, r):
                for k in range(KD):
                    pe.wait_ge(*x_sq.at(l, r * KD + k + 1))
                    for half in range(2):
                        last = pe.matmul(ps[:, 2 + half, 0:HALF], ones, h[:, k, half * HALF:(half + 1) * HALF],
                                         start=(k == 0), stop=(k == KD - 1))
                last.then_inc(x_ss.sem, 1)

            def mlstm(l):
                def scores(s):
                    g, hd, d = steps[s]
                    n = g * HM + hd
                    if s:
                        pe.wait_ge(*w_ready.at(l, e_before[s]))
                    lo, hi = SEG[g]
                    for i in range((hi - lo) // P):
                        last = pe.matmul(ps[:, i, 0:hi - lo], mk[:, hd, lo + i * P:lo + (i + 1) * P],
                                         mq[:, hd, lo:hi], start=True, stop=True)
                    last.then_inc(st_ready.sem, 1)

                def broadcasts(s):
                    g, hd, d = steps[s]
                    lo, hi = SEG[g]
                    if s:
                        pe.wait_ge(*w_ready.at(l, e_before[s]))
                        pe.wait_ge(*am_ready.at(l, s))
                    pick = ident[0:8, d * HM + hd:d * HM + hd + 1].to_broadcast([8, P])
                    pe.matmul(ps[:, 4, 0:hi - lo], pick, rowB[0:8, d, lo:hi], start=True, stop=True)
                    pe.matmul(ps[:, 5, 0:hi - lo], pick, rowM[0:8, d, lo:hi], start=True, stop=True)\
                        .then_inc(bc_ready.sem, 1)

                def sums(s):
                    g, hd, d = steps[s]
                    lo, hi = SEG[g]
                    tiles = stiles(g, d)
                    if s:
                        pe.wait_ge(*num_copied.at(l, s))
                        pe.wait_ge(*den_read.at(l, s))
                    for j, (i, t0, t1) in enumerate(tiles):
                        pe.wait_ge(*w_ready.at(l, e_before[s] + j + 1))
                        w = wmat[:, s % 2, i, t0:t1]
                        end = g == 0
                        pe.matmul(ps[:, 6, t0:t1], mv[:, lo // P + i, hd * P:(hd + 1) * P], w,
                                  start=(j == 0), stop=end)
                        last = pe.matmul(ps[:, 7, t0:t1], ones, w, start=(j == 0), stop=end)
                    if g:
                        pe.wait_ge(*qi_ready.at(l, s - 8 + 1))
                        pe.matmul(ps[:, 6, :], c0s[:, d * HM + hd, :], qi[:, s % 2, :], start=False, stop=True)
                        last = pe.matmul(ps[:, 7, :],
                                         par[:, Q_N0 + d * HM + hd:Q_N0 + d * HM + hd + 1].to_broadcast([P, P]),
                                         qi[:, s % 2, :], start=False, stop=True)
                    last.then_inc(nd_ready.sem, 1)

                def final_states():
                    pe.wait_ge(*w_ready.at(l, e_before[8]))
                    for hd in range(HM):
                        last = pe.transpose(ps[:, 0, hd * P:(hd + 1) * P], mk[:, hd, 0:TP], ident)
                    last.then_inc(ktok_ps.sem, 1)
                    pe.wait_ge(*ktok_ready.at(l, 1))
                    for g in range(8):
                        hd = g % HM
                        pe.wait_ge(*vw_ready.at(l, g + 1))
                        if g >= 2:
                            pe.wait_ge(*state_copied.at(l, g - 1))
                        pe.matmul(ps[:, 1 + g % 2, 0:129], ktok[:, hd, :], vw[:, g % 2, :], start=True, stop=True)\
                            .then_inc(state_ps.sem, 1)
                    pe.wait_ge(*state_copied.at(l, 8))

                for s in range(16):
                    if s == 8:
                        sums(7)
                        final_states()
                    if steps[s][2] == 0:
                        scores(s)
                    broadcasts(s)
                    if s and s != 8:
                        sums(s - 1)
                sums(15)

            def attention(l):
                def scores(s):
                    n, g = asteps[s]
                    for a in range(4):
                        hd = 4 * g + a
                        lo = DN * (hd % 2)
                        j = hd // 2
                        if s:
                            pe.wait_ge(*score_max.at(l, s))
                        if n is None:
                            last = pe.matmul(ps[:, a, 0:P], nq[lo:lo + DN, j, 0:TP], nk[lo:lo + DN, j, 0:TP],
                                             start=True, stop=True)
                        else:
                            kg = nk[lo:lo + DN, j, TP:T].rearrange("p (r c) -> p r c", c=GRID)
                            qblk = nq[lo:lo + DN, j, TP + n * P:TP + (n + 1) * P]
                            pe.matmul(ps[:, a, 0:WINK], qblk, kg[:, :, BAND0[n]:BAND0[n] + KBAND],
                                      start=True, stop=True)
                            last = pe.matmul(ps[:, a, WINK:NKEY], qblk, cks[lo:lo + DN, j, :],
                                             start=True, stop=True)
                        last.then_inc(score_ps.sem, 1)

                def outputs(s):
                    n, g = asteps[s]
                    nb = s // 2
                    nt = 1 if n is None else 3

                    def turn(a):
                        r = 4 * s + a
                        pe.wait_ge(*prob_ready.at(l, r + 1))
                        if r >= 2:
                            pe.wait_ge(*probT_ready.at(l, r - 1))
                        for i in range(nt):
                            last = pe.transpose(ps[:, 4 + r % 2, i * P:(i + 1) * P],
                                                prob[:, s % 2, a, i * P:(i + 1) * P], ident)
                        last.then_inc(probT_ps.sem, 1)

                    def weigh(a):
                        r = 4 * s + a
                        hd = 4 * g + a
                        lo = DN * (hd % 2)
                        pe.wait_ge(*probT_ready.at(l, r + 1))
                        for i in range(nt):
                            if n is None:
                                v = nvp[:, hd * DN:(hd + 1) * DN]
                            elif i < 2:
                                v = vband[:, n % 2, i, hd * DN:(hd + 1) * DN]
                            else:
                                v = cvs[:, hd * DN:(hd + 1) * DN]
                            last = pe.matmul(ps[lo:lo + DN, 6 + nb % 2, (hd // 2) * P:(hd // 2 + 1) * P], v,
                                             probT[:, r % 2, i * P:(i + 1) * P],
                                             start=(i == 0), stop=(i == nt - 1))
                        return last

                    if g == 0 and nb >= 2:
                        pe.wait_ge(*att_copied.at(l, nb - 1))
                    if n is not None and g == 0:
                        pe.wait_ge(*band_in[n % 2].at(l, 2 * (n // 2) + 2))
                    turn(0)
                    for a in range(4):
                        if a < 3:
                            turn(a + 1)
                        last = weigh(a)
                    if g == 1:
                        last.then_inc(att_ps.sem, 1)

                for s in range(10):
                    if s == 2:
                        pe.wait_ge(*ctx_in.at(l, 2))
                    scores(s)
                    if s:
                        outputs(s - 1)
                outputs(9)

            def convolution(l):
                for j in range(2):
                    project(l, R_CONV + 3 * j, [U_CV + 6 * j + v for v in range(6)])

            def merge(l):
                for b, y in enumerate((y_ml, y_cv, y_na)):
                    if b == 0:
                        pe.wait_ge(*yml_ready.at(l, KB))
                    if b == 1:
                        pe.wait_ge(*conv_done.at(l, KB))
                    if b == 2:
                        pe.wait_ge(*att_copied.at(l, 5))
                    for j in range(2):
                        for g in range(2):
                            half, hi, lo = split_chunk(l, R_MERGE + 6 * b + 3 * j + 2 * g)
                            for f in range(2):
                                dt = 4 * j + 2 * g + f
                                u = U_MG + 2 * (b * KD + dt)
                                split_unit(l, u, hi, lo, f * P)
                                if dt % 4 == 0:
                                    sp, wp = chunk(l, R_MERGE + 6 * b + 3 * j + 1, 512)
                                tile_unit(l, u + 1, lambda k: wp[:, k, dt % 4 * P:(dt % 4 + 1) * P],
                                          lambda k: y[:, k, :], KB)
                            leave(half)
                        release(sp)

            def mix_out(l):
                pe.wait_ge(*merged_ready.at(l, 24))
                for j in range(4):
                    b, hi, lo = split_chunk(l, R_O + j)
                    for f in range(2):
                        split_unit(l, U_WO + 2 * j + f, hi, lo, f * P, acts=(merged_hi, merged_lo))
                    leave(b)

            def route(l):
                for t in range(NTILE):
                    for k in range(KD):
                        last = pe.matmul(ps[:, 0, t * NE:(t + 1) * NE], h[:, k, t * P:(t + 1) * P], wr[:, k, :],
                                         start=(k == 0), stop=(k == KD - 1))
                last.then_inc(logit_ps.sem, 1)
                for n in range(2 * NTILE):
                    t, half = n // 2, n % 2
                    if n >= 4:
                        pe.wait_ge(*tok_copied.at(l, n - 3))
                    for k in range(4):
                        last = pe.transpose(ps[:, 4 + n % 4, k * P:(k + 1) * P],
                                            h[:, 4 * half + k, t * P:(t + 1) * P], ident)
                    last.then_inc(tok_ps.sem, 1)
                pe.wait_ge(*aff_ready.at(l, 1))
                for t in range(NTILE):
                    last = pe.transpose(ps[0:NE, 1 + t // 4, (t % 4) * P:(t % 4 + 1) * P], aff[:, t, :], ident)
                last.then_inc(affT_ps.sem, 1)
                pe.wait_ge(*pos_ready.at(l, 1))
                pe.sem_inc(pe_passed, 1)
                for t in range(NTILE):
                    last = pe.transpose(ps[:, 3, t * NE:(t + 1) * NE], pos_r[0:NE, t * P:(t + 1) * P],
                                        ident[0:NE, 0:NE])
                last.then_inc(posT_ps.sem, 1)

            def gather(n, j):
                if j == 0:
                    pe.wait_ge(pick_ready.sem, n + 1)
                for dt in range(3 * j, min(3 * j + 3, KD)):
                    out = ps[:, 2 + j, (dt % 3) * 2 * CAP:(dt % 3 + 1) * 2 * CAP]\
                        .rearrange("p (e c) -> p e c", e=2)
                    for t in range(1, NTILE):
                        pe.matmul(out[:, :, 0:CAP_S], h_tok[:, t, dt * P:(dt + 1) * P],
                                  pick_s[:, t - 1, :, :], start=(t == 1), stop=(t == NTILE - 1))
                    last = pe.matmul(out[:, :, CAP_S:CAP], h_tok[:, 0, dt * P:(dt + 1) * P],
                                     pick_p[:, :, 0:CAP_P], start=True, stop=True)
                last.then_inc(gather_ps.sem, 1)

            def turn_scatter(n):
                pe.wait_ge(gated_ready.sem, n + 1)
                for t in range(NTILE - 1):
                    pe.transpose(ps[:, 2, t * P:(t + 1) * P],
                                 gated_s[:, t, :, :].rearrange("p e c -> p (e c)"), ident)
                pe.transpose(ps[0:64, 3, 0:TP], gated_p[:, :, :].rearrange("p e c -> p (e c)"), ident)\
                    .then_inc(scat_ps.sem, 1)

            def spread_context(n):
                pe.wait_ge(down_copied.sem, 4 * n + 4)
                for dt in range(KD):
                    last = pe.matmul(ps[:, 2 if dt < 4 else 7, dt % 4 * TP:(dt % 4 + 1) * TP],
                                     y_p[0:64, dt * P:(dt + 1) * P], scat_p[0:64, :], start=True, stop=True)
                last.then_inc(context_spread.sem, 1)

            def spread(n, dt):
                if dt >= 2:
                    pe.wait_ge(x_added.sem, KD * n + dt - 1)
                pe.matmul(ps[:, dt % 2, :], y_s[:, dt * P:(dt + 1) * P], scat_s, start=True, stop=True)\
                    .then_inc(spread_ps.sem, 1)

            def expert(l, i, e, first, last_pair):
                n = l * NPAIR + i
                m = n * 2 + e

                def turn_act(half):
                    pe.wait_ge(act_ready.sem, 2 * m + half + 1)
                    for f in range(4):
                        last = pe.transpose(ps[:, 7, f * CAP:(f + 1) * CAP],
                                            act_row[0:CAP, half, f * P:(f + 1) * P], ident[0:CAP, 0:CAP])
                    last.then_inc(actT_ps.sem, 1)

                for c, (w, kh, nh) in enumerate(expert_chunks):
                    q = EXP_CHUNKS * e + c
                    s = q % NSLOT
                    if c == 0 and e == 1:
                        pe.wait_ge(scat_ready.sem, n + 1)
                    if c == 8:
                        pe.wait_ge(actT_ready.sem, 2 * m + 1)
                        if e == 0 and not first:
                            pe.wait_ge(x_added.sem, KD * n)
                    if c == 10:
                        pe.wait_ge(actT_ready.sem, 2 * m + 2)
                    if c in (8, 9) and not (first and e == 0):
                        pe.wait_ge(down_copied.sem, 2 * m - 1 + nh)
                    if c < 8:
                        b = 3 + 2 * nh + (w is w_up)
                        a_hi, a_lo = xg_hi[:, :, e, :], xg_lo[:, :, e, :]
                    else:
                        b = nh
                        a_hi, a_lo = act_hi[:, e, :, :], act_lo[:, e, :, :]
                    hi = w_hi[:, q % 2, :].rearrange("p (k n) -> p k n", k=4)
                    lo = w_lo[:, q % 2, :].rearrange("p (k n) -> p k n", k=4)
                    pe.wait_ge(hi_ready, l * SPLIT_LAYER + MIX_SPLITS + i * PAIR_CHUNKS + q + 1)
                    for k in range(4):
                        pe.matmul(ps[0:CAP, b, :], a_hi[:, 4 * kh + k, :], hi[:, k, :],
                                  start=(kh == 0 and k == 0), stop=False)
                    pe.wait_ge(slot_used[s], l * SLOT_LAYER[s] + slot_uses(R_EXP + q) + 1
                               + i * (PAIR_CHUNKS // NSLOT) + 1)
                    for k in range(4):
                        last = pe.matmul(ps[0:CAP, b, :], a_lo[:, 4 * kh + k, :], hi[:, k, :],
                                         start=False, stop=False)
                    last.then_inc(hi_used[q % 2], 1)
                    for k in range(4):
                        last = pe.matmul(ps[0:CAP, b, :], a_hi[:, 4 * kh + k, :], lo[:, k, :],
                                         start=False, stop=(kh == 1 and k == 3))
                    last.then_inc(lo_used[q % 2], 1)
                    if c in (3, 7):
                        pe.drain()
                        pe.sem_inc(up_ps.sem, 1)
                    if c in (10, 11):
                        pe.drain()
                        pe.sem_inc(down_ps.sem, 1)
                    if e == 0 and not first:
                        if c == 1:
                            spread_context(n - 1)
                        if 2 <= c <= 5:
                            spread(n - 1, 2 * c - 4)
                            spread(n - 1, 2 * c - 3)
                    if c == 5:
                        if e == 0 and not first:
                            pe.wait_ge(context_added.sem, n)
                        turn_act(0)
                    if c == 9:
                        turn_act(1)
                    if e == 0 and c == 9:
                        turn_scatter(n)
                    if e == 1 and not last_pair and 7 <= c <= 9:
                        gather(n + 1, c - 7)

            def pair(l, i, first=False, last_pair=False):
                pe.wait_ge(xg_ready.sem, 3 * (l * NPAIR + i) + 3)
                for e in range(2):
                    expert(l, i, e, first, last_pair)

            for s in range(NSLOT):
                pe.sem_inc(slot_used[s], 1)
            for b in range(2):
                pe.sem_inc(hi_used[b], 1)
                pe.sem_inc(lo_used[b], 1)
            pe.wait_ge(cond_ready, 1)
            with pe.Fori(0, DEPTH) as l:
                modulation(l)
                project(l, R_MQ, range(U_MQ, U_MQ + KB), fresh=True)
                rope_rows(l, U_RQ, mq, 0)
                for j in range(2):
                    b, hi, lo = split_chunk(l, R_G + j, GC)
                    split_unit(l, U_G + j, hi, lo, 0)
                    leave(b)
                project(l, R_MK, range(U_MK, U_MK + KB))
                rope_rows(l, U_RK, mk, HM)
                project_tokens(l, R_MV, U_MV)
                pe.wait_ge(*rows_ready.at(l, 1))
                pe.wait_ge(*emptied(l, U_MV + NTILE - 1))
                pe.wait_ge(*roped.at(l, 2 * HM))
                pe.sem_inc(pe_passed, 1)
                for d in range(2):
                    for t in range(NTILE):
                        last = pe.transpose(ps[:, 0, (d * NTILE + t) * 8:(d * NTILE + t + 1) * 8],
                                            rowA[0:8, d, t * P:(t + 1) * P], ident[0:8, 0:8])
                last.then_inc(acol_ps.sem, 1)
                pe.wait_ge(*acol_ready.at(l, 1))
                mlstm(l)
                pe.wait_ge(*num_copied.at(l, 16))
                pe.wait_ge(*den_read.at(l, 16))
                project(l, R_MO, range(U_MO, U_MO + KB))
                head_sums(l, U_NORM, 0, ones, ml_tmp)
                project(l, R_NQ, range(U_NQ, U_NQ + KB))
                project(l, R_NK, range(U_NK[0], U_NK[0] + 2))
                head_sums(l, U_SQ, HM, blkones, na_tmp)
                project(l, R_NK + 1, range(U_NK[1], U_NK[1] + 2))
                head_sums(l, U_SK, HM + KB, blkones, ml_tmp)
                project_tokens(l, R_NV, U_NV)
                pe.wait_ge(*head_normed.at(l, 12))
                pe.wait_ge(*emptied(l, U_NV + NTILE - 1))
                attention(l)
                pe.wait_ge(*att_copied.at(l, 5))
                convolution(l)
                merge(l)
                mix_out(l)
                pe.wait_ge(*x_mixed.at(l, KD))
                x_sums(l, 1)
                pe.wait_ge(*h_ready.at(l, 2 * KD))
                route(l)
                pe.wait_ge(*tok_copied.at(l, 10))
                pe.wait_ge(*posT_ready.at(l, 1))
                for j in range(3):
                    gather(l * NPAIR, j)
                pair(l, 0, first=True)
                with pe.Fori(1, NPAIR - 1) as i:
                    pair(l, i)
                pair(l, NPAIR - 1, last_pair=True)
                spread_context(l * NPAIR + NPAIR - 1)
                for dt in range(KD):
                    spread(l * NPAIR + NPAIR - 1, dt)
                pe.wait_ge(x_added.sem, (l + 1) * KD * NPAIR)
                pe.wait_ge(context_added.sem, (l + 1) * NPAIR)

        @block.scalar
        def _(act):
            def gathered_hi(n, j):
                w = 3 if j < 2 else 2
                act.wait_ge(gather_ps.sem, 3 * n + j + 1)
                act.activation(xg_hi[:, 3 * j:3 * j + w, :, :].rearrange("p a e c -> p (a e c)"),
                               ps[:, 2 + j, 0:w * 2 * CAP], ACT.Copy).then_inc(xg_hi_ready.sem, 1)

            def outputs(m, e, half):
                act.wait_ge(down_ps.sem, 2 * m + half + 1)
                act.activation(y_s[64 * e:64 * e + CAP_S, half * 512:(half + 1) * 512],
                               ps[0:CAP_S, half, :], ACT.Copy)
                act.activation(y_p[32 * e:32 * e + CAP_P, half * 512:(half + 1) * 512],
                               ps[CAP_S:CAP, half, :], ACT.Copy).then_inc(down_copied.sem, 1)

            def pair(l, i, first=False, last_pair=False):
                n = l * NPAIR + i
                for e in range(2):
                    m = 2 * n + e
                    for c in range(EXP_CHUNKS):
                        q = EXP_CHUNKS * e + c
                        s = q % NSLOT
                        act.wait_ge(slot_landed[s], (l * SLOT_LAYER[s] + slot_uses(R_EXP + q)
                                                     + i * (PAIR_CHUNKS // NSLOT) + 1) * 16)
                        act.wait_ge(hi_used[q % 2], l * (SPLIT_LAYER // 2) + MIX_SPLITS // 2
                                    + i * (PAIR_CHUNKS // 2) + q // 2 + 1)
                        act.activation(w_hi[:, q % 2, :], ring[:, s, :], ACT.Copy).then_inc(hi_ready, 1)
                        if c < 2 and not (first and e == 0):
                            outputs(m - 1, 1 - e, c)
                        if c in (5, 9):
                            half = (c - 5) // 4
                            act.wait_ge(up_ps.sem, 2 * m + half + 1)
                            act.activation(silu_t[0:CAP, :], ps[0:CAP, 3 + 2 * half, :], ACT.Silu)\
                                .then_inc(silu_ready.sem, 1)
                        if c in (7, 10):
                            half = (c - 7) // 3
                            act.wait_ge(actT_ps.sem, 2 * m + half + 1)
                            act.activation(act_hi[:, e, 4 * half:4 * half + 4, :].rearrange("p f c -> p (f c)"),
                                           ps[:, 7, 0:4 * CAP], ACT.Copy).then_inc(actT_hi.sem, 1)
                        if e == 1 and not last_pair and c >= 9:
                            gathered_hi(n + 1, c - 9)

            def square_x(l, r):
                for k in range(KD):
                    act.activation(h[:, k, :], x[:, k, :], ACT.Square).then_inc(x_sq.sem, 1)

            def root_mean(l, r):
                act.wait_ge(*x_ss.at(l, r + 1))
                act.activation(cols(rstd[:, :]), ps[:, 2:4, 0:HALF], ACT.Sqrt, bias=eps[:, :], scale=1.0 / D)\
                    .then_inc(x_root.sem, 1)

            def norm_x(l, r):
                act.wait_ge(*scale_ready.at(l, 2))
                a, b0 = (a1, 0) if r == 0 else (a2, 24)
                for k in range(KD):
                    act.wait_ge(*x_normed.at(l, r * KD + k + 1))
                    for g, (lo, hi) in enumerate(SEG):
                        last = act.activation(h[:, k, lo:hi], h[:, k, lo:hi], ACT.Identity,
                                              bias=mod[:, b0 + k, g:g + 1], scale=a[:, k, g:g + 1])
                    if r == 0:
                        act.drain()
                        if k == 0:
                            act.wait_ge(*x_saved.at(l, 1))
                        last = act.activation(h_hi[:, k, :], h[:, k, :], ACT.Copy)
                    last.then_inc(h_ready.sem, 1)

            def empty(l, u, out, bias, func=ACT.Identity, scale=1.0):
                act.wait_ge(*unit_full.at(l, u + 1))
                return act.activation(cols(out), pair_ps(u), func, bias=bias, scale=scale)\
                    .then_inc(act_emptied.sem, 1)

            def empty_queries(l, u, out, bias):
                act.wait_ge(*unit_full.at(l, u + 1))
                b = bank(u)
                act.activation(out[:, 0:TP], ps[:, b, 0:TP], ACT.Identity, bias=bias)
                blocks = out[:, TP:T].rearrange("p (n r c) -> p r n c", n=NBLK, r=ROWS)
                cut = (HALF - TP) // GRID
                for r0, r1, src in ((0, cut, ps[:, b, TP:HALF]), (cut, ROWS, ps[:, b + 1, 0:HALF])):
                    src = src.rearrange("p (r n c) -> p r n c", n=NBLK, c=QB)
                    for r in range(r0, r1):
                        last = act.activation(blocks[:, r, :, :], src[:, r - r0, :, :], ACT.Identity, bias=bias)
                last.then_inc(act_emptied.sem, 1)

            def bcol(i):
                return par[:, Q_BIN + i:Q_BIN + i + 1]

            def head_roots(l, u0, tmp, scale):
                for i in range(KB):
                    empty(l, u0 + i, tmp[:, i, :], eps[:, :], ACT.Sqrt, scale)
                    act.drain()
                    act.sem_inc(root_ready.sem, 1)

            def mlstm(l):
                def copy_num(s):
                    n = TS if steps[s][0] else TP
                    act.wait_ge(*nd_ready.at(l, s + 1))
                    if s:
                        act.wait_ge(*h_done.at(l, s))
                    act.activation(num[:, 0:n], ps[:, 6, 0:n], ACT.Copy).then_inc(num_copied.sem, 1)

                for s, (g, hd, d) in enumerate(steps):
                    if s == 8:
                        copy_num(7)
                        act.wait_ge(*ktok_ps.at(l, 1))
                        act.activation(ktok, ps[:, 0, :].rearrange("p (a b) -> p a b", a=HM), ACT.Copy,
                                       scale=ML_SCALE).then_inc(ktok_ready.sem, 1)
                        for c in range(8):
                            act.wait_ge(*state_ps.at(l, c + 1))
                            act.activation(cout[:, c, :], ps[:, 1 + c % 2, 0:129], ACT.Copy)\
                                .then_inc(state_copied.sem, 1)
                    if s == 9:
                        act.wait_ge(*state_out.at(l, 3))
                    lo, hi = SEG[g]
                    n = hi - lo
                    act.wait_ge(*bc_ready.at(l, s + 1))
                    act.wait_ge(*z_ready.at(l, s + 1))
                    if s >= 2:
                        act.wait_ge(*nd_ready.at(l, s - 1))
                    if g:
                        act.activation(qi[:, s % 2, :], ps[:, 4, :], ACT.Exp,
                                       bias=par[:, Q_M0 + d * HM + hd:Q_M0 + d * HM + hd + 1])\
                            .then_inc(qe_ready.sem, 1)
                    else:
                        end = TP - 1 if d == 0 else 0
                        act.activation(wend[:, d * HM + hd:d * HM + hd + 1], ps[:, 4, end:end + 1], ACT.Exp,
                                       bias=acol[:, d, 0, d * HM + hd:d * HM + hd + 1])\
                            .then_inc(qe_ready.sem, 1)
                    for i, t0, t1 in stiles(g, d):
                        bias = acol[:, d, lo // P + i, d * HM + hd:d * HM + hd + 1]
                        dg = i * P
                        last = act.activation(wmat[:, s % 2, i, dg:dg + P], wmat[:, s % 2, i, dg:dg + P], ACT.Exp,
                                              bias=bias)
                        a, b = (dg + P, t1) if d == 0 else (t0, dg)
                        if b > a:
                            last = act.activation(wmat[:, s % 2, i, a:b], ps[:, 4, a:b], ACT.Exp, bias=bias)
                        last.then_inc(e_ready.sem, 1)
                    if s >= 2:
                        act.wait_ge(*h_done.at(l, s - 1))
                    act.activation(emm[:, s % 2, 0:n], ps[:, 5, 0:n], ACT.Exp, scale=-1.0).then_inc(am_ready.sem, 1)
                    if s and s != 8:
                        copy_num(s - 1)
                copy_num(15)

            def attention(l):
                def exp(s, a):
                    w = TP if asteps[s][0] is None else NKEY
                    if a == 0:
                        act.wait_ge(*score_max.at(l, s + 1))
                    act.activation(prob[:, s % 2, a, 0:w], prob[:, s % 2, a, 0:w], ACT.Exp,
                                   bias=mx[:, s % 2, a:a + 1], accum_out=rs[:, s % 2, a:a + 1])\
                        .then_inc(prob_exp.sem, 1)

                def copy(s, a):
                    w = TP if asteps[s][0] is None else NKEY
                    r = 4 * s + a
                    act.wait_ge(*probT_ps.at(l, r + 1))
                    act.activation(probT[:, r % 2, 0:w], ps[:, 4 + r % 2, 0:w], ACT.Copy)\
                        .then_inc(probT_ready.sem, 1)

                for s in range(11):
                    for a in range(4):
                        if s < 10:
                            exp(s, a)
                        if s:
                            copy(s - 1, a)

            act.wait_ge(start_in, 48)
            act.activation(silu_c[:, :, :], silu_c[:, :, :], ACT.Silu).then_inc(cond_ready, 1)
            act.wait_ge(consts_set, 1)
            with act.Fori(0, DEPTH) as l:
                for r in range(ADA_CHUNKS // 2):
                    if r == 4:
                        act.wait_ge(*params_in.at(l, 4))
                        square_x(l, 0)
                    if r == 7:
                        root_mean(l, 0)
                    act.wait_ge(*mod_row_ps.at(l, r + 1))
                    act.activation(mod_row[:, r % 2, :], ps[0:2, 4 + r % 2, :], ACT.Copy)\
                        .then_inc(mod_row_copied.sem, 1)
                norm_x(l, 0)
                for i in range(HM):
                    empty(l, U_MQ + i, mq[:, i, :], bcol(B_MQ + i))
                act.wait_ge(*lf_abs.at(l, 1))
                act.activation(row_t[0:8, :], row_t[0:8, :], ACT.Exp, scale=-1.0)
                act.drain()
                act.activation(row_t[0:8, :], row_t[0:8, :], ACT.Ln, bias=1.0).then_inc(lf_log.sem, 1)
                for i in range(HM):
                    empty(l, U_MK + i, mk[:, i, :], bcol(B_MK + i))
                act.wait_ge(*acol_ps.at(l, 1))
                act.activation(acol[:, :, :, :].rearrange("p a b c -> p (a b c)"), ps[:, 0, 0:80], ACT.Copy)\
                    .then_inc(acol_ready.sem, 1)
                act.drain()
                mlstm(l)
                act.wait_ge(*h_done.at(l, 16))
                for i in range(HM):
                    act.activation(ml_tmp[:, i, :], y_ml[:, i, :], ACT.Square).then_inc(sq_ready.sem, 1)
                for i in range(KB):
                    empty(l, U_MO + i, sig_mo[:, i, :], bcol(B_MO + i), ACT.Sigmoid)
                head_roots(l, U_NORM, ml_tmp, 1.0 / P)
                for i in range(KB):
                    empty_queries(l, U_NQ + i, nq[:, i, :], bcol(B_NQ + i))
                act.drain()
                for i in range(KB):
                    act.activation(na_tmp[:, i, :], nq[:, i, :], ACT.Square).then_inc(sq_ready.sem, 1)
                for j in range(2):
                    for i in (2 * j, 2 * j + 1):
                        empty(l, U_NK[j] + i % 2, nk[:, i, :], bcol(B_NK + i))
                    act.drain()
                    if j == 0:
                        act.wait_ge(*head_normed.at(l, HM))
                    for i in (2 * j, 2 * j + 1):
                        act.activation(ml_tmp[:, i, :], nk[:, i, :], ACT.Square).then_inc(sq_ready.sem, 1)
                    if j == 0:
                        head_roots(l, U_SQ, na_tmp, 1.0 / DN)
                head_roots(l, U_SK, ml_tmp, 1.0 / DN)
                attention(l)
                for i in range(KB):
                    empty(l, u_conv(i, 0), cc_t[:, i, :], bcol(B_CC + i))
                for i in range(3 * KD):
                    if i >= 2:
                        act.wait_ge(*merged_ready.at(l, i - 1))
                    empty(l, U_MG + 2 * i, gate_t[:, i % 2, :], bcol(B_GT + i), ACT.Sigmoid)
                act.wait_ge(*x_mixed.at(l, KD))
                square_x(l, 1)
                root_mean(l, 1)
                norm_x(l, 1)
                act.wait_ge(*logit_shift.at(l, 1))
                act.activation(aff[:, :, :], aff[:, :, :], ACT.Exp).then_inc(logit_exp.sem, 1)
                for n in range(2 * NTILE):
                    t, half = n // 2, n % 2
                    act.wait_ge(*tok_ps.at(l, n + 1))
                    act.activation(h_tok[:, t, half * 512:(half + 1) * 512], ps[:, 4 + n % 4, :], ACT.Copy)\
                        .then_inc(tok_copied.sem, 1)
                for j in range(3):
                    gathered_hi(l * NPAIR, j)
                pair(l, 0, first=True)
                with act.Fori(1, NPAIR - 1) as i:
                    pair(l, i)
                pair(l, NPAIR - 1, last_pair=True)
                for half in range(2):
                    outputs(2 * NPAIR * (l + 1) - 1, 1, half)
                act.wait_ge(*layer_x.at(l, 1))

        @block.vector
        def _(dve):
            def root_x(l, r):
                dve.wait_ge(*x_root.at(l, r + 1))
                dve.reciprocal(rstd[:, :], rstd[:, :])
                dve.drain()
                for k in range(KD):
                    dve.tensor_tensor(h[:, k, :], x[:, k, :], rstd[:, :], ALU.mult).then_inc(x_normed.sem, 1)

            def rope(l, u0, dst):
                for i in range(HM):
                    dve.wait_ge(*unit_full.at(l, u0 + i + 1))
                    dve.tensor_tensor(rope_tmp, ps[:, bank(u0 + i), :], sinT, ALU.mult).then_inc(dve_emptied.sem, 1)
                    dve.tensor_tensor(dst[:, i, TP:T], dst[:, i, TP:T], cosT, ALU.mult)
                    dve.drain()
                    dve.tensor_tensor(dst[:, i, TP:T], dst[:, i, TP:T], rope_tmp, ALU.add).then_inc(roped.sem, 1)
                    dve.drain()

            def gate_rows(l):
                dve.tensor_scalar(rbias[:, :], rowpar[:, 1:2], rowpar[:, 2:3], None, ALU.add)
                dve.memset(row_zero[0:8, :], 0.0)
                dve.drain()
                dve.wait_ge(*unit_full.at(l, U_G + 1))
                dve.tensor_scalar(cols(row_ig[0:8, :]), ps[0:8, bank(U_G):bank(U_G) + 2, 0:HALF], rowpar[:, 0:1],
                                  None, ALU.add).then_inc(dve_emptied.sem, 1)
                b = bank(U_G + 1)
                dve.wait_ge(*unit_full.at(l, U_G + 2))
                dve.tensor_scalar(cols(row_lf[0:8, :]), ps[0:8, b:b + 2, 0:HALF], rbias[:, :], None, ALU.add)\
                    .then_inc(dve_emptied.sem, 1)
                dve.drain()
                dve.scalar_tensor_tensor(row_t[0:8, :], row_lf[0:8, :], -1.0, row_lf[0:8, :], ALU.mult, ALU.max)\
                    .then_inc(lf_abs.sem, 1)
                dve.wait_ge(*lf_log.at(l, 1))
                dve.scalar_tensor_tensor(row_lf[0:8, :], row_lf[0:8, :], 0.0, row_t[0:8, :], ALU.min, ALU.subtract)
                dve.drain()
                for d in range(2):
                    for g, (lo, hi) in enumerate(SEG):
                        order = slice(lo, hi) if d == 0 else (slice(hi - 1, lo - 1 if lo else None, -1))
                        dve.tensor_tensor_scan(rowB[0:8, d, order], row_lf[0:8, order], row_zero[0:8, order], 0.0,
                                               ALU.add, ALU.add)
                        dve.tensor_tensor_scan(rowM[0:8, d, order], row_lf[0:8, order], row_ig[0:8, order],
                                               rowpar[:, 3:4] if g else 0.0, ALU.add, ALU.max)
                dve.drain()
                for d in range(2):
                    dve.tensor_tensor(rowA[0:8, d, :], row_ig[0:8, :], rowB[0:8, d, :], ALU.subtract)
                dve.drain()
                for d in range(2):
                    last = dve.tensor_tensor(rowB[0:8, d, :], rowB[0:8, d, :], rowM[0:8, d, :], ALU.subtract)
                last.then_inc(rows_ready.sem, 1)

            def mlstm(l):
                def exponents(s):
                    g, hd, d = steps[s]
                    dve.wait_ge(*bc_ready.at(l, s + 1))
                    if s >= 2:
                        dve.wait_ge(*nd_ready.at(l, s - 1))
                    if s == 9:
                        dve.wait_ge(*state_out.at(l, 3))
                    w = wmat[:, s % 2, :, :].rearrange("p a b -> p (a b)")
                    if g == 0:
                        dve.tensor_tensor(w[:, 0:P], ps[:, 4, 0:P], tri(d), ALU.add).then_inc(z_ready.sem, 1)
                    else:
                        dve.tensor_tensor(
                            w[:, 0:1920].rearrange("p (i c) -> p i c", c=640)[:, :, 0:P],
                            ps[:, 4, 0:384].rearrange("p (i c) -> p i c", c=P),
                            tri(d)[:, None, :].to_broadcast([P, 3, P]), ALU.add)
                        dve.tensor_tensor(w[:, 1920:2048], ps[:, 4, 384:512], tri(d), ALU.add)\
                            .then_inc(z_ready.sem, 1)

                def weights(s):
                    g, hd, d = steps[s]
                    if g:
                        dve.wait_ge(*qe_ready.at(l, s + 1))
                        dve.tensor_tensor(qi[:, s % 2, :], mq[:, hd, TP:T], qi[:, s % 2, :], ALU.mult)\
                            .then_inc(qi_ready.sem, 1)
                    dve.wait_ge(*st_ready.at(l, s // 2 + 1))
                    for j, (i, t0, t1) in enumerate(stiles(g, d)):
                        dve.wait_ge(*e_ready.at(l, e_before[s] + j + 1))
                        dve.scalar_tensor_tensor(wmat[:, s % 2, i, t0:t1], ps[:, i, t0:t1], ML_SCALE,
                                                 wmat[:, s % 2, i, t0:t1], ALU.mult, ALU.mult)\
                            .then_inc(w_ready.sem, 1)

                def invert(s):
                    n = TS if steps[s][0] else TP
                    e = emm[:, s % 2, 0:n]
                    dve.wait_ge(*am_ready.at(l, s + 1))
                    dve.wait_ge(*nd_ready.at(l, s + 1))
                    dve.scalar_tensor_tensor(e, ps[:, 7, 0:n], -1.0, e, ALU.mult, ALU.max)
                    dve.drain()
                    dve.tensor_tensor(e, ps[:, 7, 0:n], e, ALU.max).then_inc(den_read.sem, 1)
                    dve.drain()
                    dve.reciprocal(e, e)

                def divide(s):
                    g, hd, d = steps[s]
                    lo, hi = SEG[g]
                    n = hi - lo
                    e = emm[:, s % 2, 0:n]
                    dve.drain()
                    dve.wait_ge(*num_copied.at(l, s + 1))
                    if d == 0:
                        dve.tensor_tensor(y_ml[:, hd, lo:hi], num[:, 0:n], e, ALU.mult).then_inc(h_done.sem, 1)
                    else:
                        dve.tensor_tensor(e, num[:, 0:n], e, ALU.mult)
                        dve.drain()
                        dve.tensor_tensor(y_ml[:, hd, lo:hi], y_ml[:, hd, lo:hi], e, ALU.add)\
                            .then_inc(h_done.sem, 1)

                exponents(0)
                for s in range(16):
                    if s == 8:
                        invert(7)
                        divide(7)
                        for c in range(8):
                            hd = c % HM
                            if c >= 2:
                                dve.wait_ge(*state_ps.at(l, c - 1))
                            dve.tensor_scalar(vw[:, c % 2, 0:P], mv[:, 0, hd * P:(hd + 1) * P], wend[:, c:c + 1],
                                              None, ALU.mult)
                            dve.tensor_copy(vw[:, c % 2, P:P + 1], wend[:, c:c + 1]).then_inc(vw_ready.sem, 1)
                        exponents(8)
                    weights(s)
                    if s and s != 8:
                        invert(s - 1)
                    if s not in (7, 15):
                        exponents(s + 1)
                    if s and s != 8:
                        divide(s - 1)
                invert(15)
                divide(15)

            def norm_heads(l, n0, dst, tmp, gain, tiles=range(KB)):
                for i in tiles:
                    dve.wait_ge(*root_ready.at(l, n0 + i + 1))
                    dve.reciprocal(tmp[:, i, :], tmp[:, i, :])
                    dve.drain()
                    dve.scalar_tensor_tensor(dst[:, i, :], dst[:, i, :], gain(i), tmp[:, i, :], ALU.mult, ALU.mult)\
                        .then_inc(head_normed.sem, 1)

            def add_row_bias(l, u, out, at):
                dve.wait_ge(*unit_full.at(l, u + 1))
                return dve.tensor_tensor(out, ps[:, bank(u), :], par[:, Q_BV + at:Q_BV + at + WB], ALU.add)

            def attention(l):
                def maxima(s):
                    n, g = asteps[s]
                    w = TP if n is None else NKEY
                    if s >= 2:
                        dve.wait_ge(*probT_ps.at(l, 4 * (s - 1)))
                    if n is not None:
                        dve.wait_ge(*bias_ready.at(l, s - 1))
                    for a in range(4):
                        dve.wait_ge(*score_ps.at(l, 4 * s + a + 1))
                        dve.sem_inc(dve_passed, 1)
                        add = bias_t[:, 0, a, WINK:NKEY] if n is None else bias_t[:, s % 2, a, :]
                        dve.tensor_tensor_reduce(prob[:, s % 2, a, 0:w], ps[:, a, 0:w], add, 1.0, -3.0e38,
                                                 ALU.add, ALU.max, mx[:, s % 2, a:a + 1])
                    dve.drain()
                    dve.tensor_scalar(mx[:, s % 2, :], mx[:, s % 2, :], -1.0, None, ALU.mult)\
                        .then_inc(score_max.sem, 1)

                def scale(s):
                    w = TP if asteps[s][0] is None else NKEY
                    dve.wait_ge(*prob_exp.at(l, 4 * s + 4))
                    dve.reciprocal(rs[:, s % 2, :], rs[:, s % 2, :])
                    dve.drain()
                    for a in range(4):
                        dve.tensor_scalar(prob[:, s % 2, a, 0:w], prob[:, s % 2, a, 0:w], rs[:, s % 2, a:a + 1],
                                          None, ALU.mult).then_inc(prob_ready.sem, 1)

                def copy_out(nb):
                    dve.wait_ge(*att_ps.at(l, nb + 1))
                    src = ps[:, 6 + nb % 2, :].rearrange("p (j q) -> p j q", j=KB)
                    if nb == 0:
                        dve.tensor_copy(y_na[:, :, 0:TP], src).then_inc(att_copied.sem, 1)
                    else:
                        n = nb - 1
                        for j in range(KB):
                            last = dve.tensor_copy(
                                y_na[:, j, TP:T].rearrange("p (r c) -> p r c", c=GRID)[:, :, n * QB:(n + 1) * QB],
                                src[:, j, :].rearrange("p (r c) -> p r c", c=QB))
                        last.then_inc(att_copied.sem, 1)

                for s in range(10):
                    maxima(s)
                    scale(s)
                    if s % 2 == 1 and s >= 3:
                        copy_out(s // 2 - 1)
                copy_out(4)

            def convolution(l):
                for lo in (0, TP + 2):
                    dve.memset(u_pad[:, lo:lo + 1], 0.0)
                dve.memset(u_pad[:, TP + 1:TP + 2], 0.0)
                dve.memset(u_pad[:, T + 3:T + 4], 0.0)
                for j in range(2):
                    for f in range(2):
                        i = 2 * j + f
                        ct = conv_t[:, f, :]
                        dve.wait_ge(*emptied(l, u_conv(i, 0)))
                        u = u_conv(i, 1)
                        dve.wait_ge(*unit_full.at(l, u + 1))
                        dve.scalar_tensor_tensor(cols(ct), pair_ps(u), par[:, Q_BIN + B_CH + i:Q_BIN + B_CH + i + 1],
                                                 cols(cc_t[:, i, :]), ALU.add, ALU.mult).then_inc(dve_emptied.sem, 1)
                        dve.drain()
                        dve.tensor_copy(u_pad[:, 1:TP + 1], ct[:, 0:TP])
                        dve.tensor_copy(u_pad[:, TP + 3:T + 3], ct[:, TP:T])
                        dve.drain()
                        for tap_at in range(3):
                            tap = par[:, Q_CW + 4 * tap_at + i:Q_CW + 4 * tap_at + i + 1]
                            for (lo, hi), at in zip(SEG, (tap_at, tap_at + 2)):
                                src = u_pad[:, lo + at:hi + at]
                                if tap_at == 0:
                                    dve.tensor_scalar(ct[:, lo:hi], src, tap, None, ALU.mult)
                                else:
                                    dve.scalar_tensor_tensor(ct[:, lo:hi], src, tap, ct[:, lo:hi],
                                                             ALU.mult, ALU.add)
                            dve.drain()
                    for f in range(2):
                        i = 2 * j + f
                        u = u_conv(i, 2)
                        dve.wait_ge(*unit_full.at(l, u + 1))
                        dve.scalar_tensor_tensor(cols(y_cv[:, i, :]), pair_ps(u),
                                                 par[:, Q_BIN + B_CB + i:Q_BIN + B_CB + i + 1],
                                                 cols(conv_t[:, f, :]), ALU.add, ALU.mult)\
                            .then_inc(dve_emptied.sem, 1)
                    dve.drain()
                    dve.sem_inc(conv_done.sem, 2)

            def merge(l):
                for i in range(3 * KD):
                    dt = i % KD
                    dve.wait_ge(*emptied(l, U_MG + 2 * i))
                    dve.wait_ge(*unit_full.at(l, U_MG + 2 * i + 2))
                    out = merged[:, dt, :] if i < KD else prod_t
                    dve.tensor_tensor(cols(out), pair_ps(U_MG + 2 * i + 1), cols(gate_t[:, i % 2, :]), ALU.mult)\
                        .then_inc(dve_emptied.sem, 1)
                    dve.drain()
                    if i >= KD:
                        dve.tensor_tensor(merged[:, dt, :], merged[:, dt, :], prod_t, ALU.add)
                        dve.drain()
                    if i >= 2 * KD:
                        dve.tensor_copy(merged_hi[:, dt, :], merged[:, dt, :])
                        dve.drain()
                        dve.tensor_tensor(merged_lo[:, dt, :], merged[:, dt, :], merged_hi[:, dt, :].bitcast(F32),
                                          ALU.subtract)
                        dve.drain()
                    dve.sem_inc(merged_ready.sem, 1)

            def mix_in(l):
                dve.wait_ge(*x_back.at(l, 1))
                for k in range(KD):
                    u = U_WO + k
                    b = bank(u)
                    dve.wait_ge(*unit_full.at(l, u + 1))
                    for g, half, lo, hi in ((0, 0, 0, TP), (1, 0, TP, HALF), (1, 1, 0, HALF)):
                        t = half * HALF
                        last = dve.scalar_tensor_tensor(
                            x[:, k, t + lo:t + hi], ps[:, b + half, lo:hi], mod[:, 16 + k, g:g + 1],
                            x[:, k, t + lo:t + hi], ALU.mult, ALU.add)
                    last.then_inc(dve_emptied.sem, 1)
                dve.drain()
                dve.sem_inc(x_mixed.sem, KD)

            def route(l):
                lg = ps[:, 0, 0:NTILE * NE].rearrange("p (t e) -> p t e", e=NE)
                dve.wait_ge(*logit_ps.at(l, 1))
                dve.tensor_reduce(smax, lg, AX.X, ALU.max)
                dve.drain()
                dve.tensor_tensor(aff[:, :, :], lg, smax[:, :, None].to_broadcast([P, NTILE, NE]), ALU.subtract)\
                    .then_inc(logit_shift.sem, 1)
                dve.wait_ge(*logit_exp.at(l, 1))
                dve.tensor_reduce(smax, aff[:, :, :], AX.X, ALU.add)
                dve.drain()
                dve.reciprocal(smax, smax)
                dve.drain()
                dve.tensor_tensor(aff[:, :, :], aff[:, :, :], smax[:, :, None].to_broadcast([P, NTILE, NE]),
                                  ALU.mult).then_inc(aff_ready.sem, 1)
                dve.wait_ge(*affT_ps.at(l, 1))
                dve.tensor_copy(work[0:NE, 0:512], ps[0:NE, 1, :])
                dve.tensor_copy(work[0:NE, 512:T], ps[0:NE, 2, 0:P])
                dve.drain()
                for (lo, hi), cap in zip(SEG, (CAP_P, CAP_S)):
                    for r in range(cap // 8):
                        dve.max(top8[0:NE, :], work[0:NE, lo:hi])
                        dve.drain()
                        dve.match_replace(work[0:NE, lo:hi], top8[0:NE, :], work[0:NE, lo:hi], -1.0)
                        dve.drain()
                dve.tensor_scalar(mask_r[0:NE, :], work[0:NE, :], 0.0, None, ALU.is_lt)
                dve.drain()
                dve.memset(work[0:NE, :], 0.0)
                dve.drain()
                for lo, hi in SEG:
                    dve.tensor_tensor_scan(pos_r[0:NE, lo:hi], mask_r[0:NE, lo:hi], work[0:NE, lo:hi], 0.0,
                                           ALU.add, ALU.add)
                dve.drain()
                dve.tensor_tensor(pos_r[0:NE, :], pos_r[0:NE, :], mask_r[0:NE, :], ALU.mult)
                dve.drain()
                dve.tensor_scalar(pos_r[0:NE, :], pos_r[0:NE, :], -1.0, None, ALU.add).then_inc(pos_ready.sem, 1)
                dve.wait_ge(*posT_ps.at(l, 1))
                dve.tensor_copy(posT[:, :, :].rearrange("p t e -> p (t e)"), ps[:, 3, 0:NTILE * NE])\
                    .then_inc(posT_ready.sem, 1)
                dve.memset(y_p[0:64, :], 0.0)
                dve.drain()

            def picks(n, first_expert):
                lat = [P, NTILE - 1, 2, CAP_S]
                con = [P, 2, 32]
                two = bass.ds(first_expert, 2)
                pos_s = posT[:, 1:NTILE, two][:, :, :, None].to_broadcast(lat)
                aff_s = aff[:, 1:NTILE, two][:, :, :, None].to_broadcast(lat)
                pos_p = posT[:, 0, two][:, :, None].to_broadcast(con)
                aff_p = aff[:, 0, two][:, :, None].to_broadcast(con)
                dve.tensor_tensor(pick_s[:, :, :, :], iota[:, None, None, :].to_broadcast(lat), pos_s, ALU.is_equal)
                dve.tensor_tensor(pick_p[:, :, :], iota[:, None, 0:32].to_broadcast(con), pos_p, ALU.is_equal)\
                    .then_inc(pick_ready.sem, 1)
                dve.drain()
                dve.tensor_tensor(gated_s[:, :, :, :], pick_s[:, :, :, :], aff_s, ALU.mult)
                dve.tensor_tensor(gated_p[:, :, :], pick_p[:, :, :], aff_p, ALU.mult).then_inc(gated_ready.sem, 1)

            def gathered_lo(n, j):
                w = 3 if j < 2 else 2
                at = slice(3 * j, 3 * j + w)
                dve.wait_ge(xg_hi_ready.sem, 3 * n + j + 1)
                dve.tensor_tensor(xg_lo[:, at, :, :].rearrange("p a e c -> p (a e c)"),
                                  ps[:, 2 + j, 0:w * 2 * CAP],
                                  xg_hi[:, at, :, :].rearrange("p a e c -> p (a e c)").bitcast(F32),
                                  ALU.subtract).then_inc(xg_ready.sem, 1)

            def add_context(n):
                dve.wait_ge(context_spread.sem, n + 1)
                for dt in range(KD):
                    last = dve.scalar_tensor_tensor(
                        x[:, dt, 0:TP], ps[:, 2 if dt < 4 else 7, dt % 4 * TP:(dt % 4 + 1) * TP],
                        mod[:, 40 + dt, 0:1], x[:, dt, 0:TP], ALU.mult, ALU.add)
                last.then_inc(context_added.sem, 1)

            def add_latent(n, dt):
                dve.wait_ge(spread_ps.sem, KD * n + dt + 1)
                dve.scalar_tensor_tensor(x[:, dt, TP:T], ps[:, dt % 2, :], mod[:, 40 + dt, 1:2], x[:, dt, TP:T],
                                         ALU.mult, ALU.add).then_inc(x_added.sem, 1)

            def pair(l, i, first=False, last_pair=False):
                n = l * NPAIR + i
                for e in range(2):
                    m = 2 * n + e
                    for c in range(EXP_CHUNKS):
                        q = EXP_CHUNKS * e + c
                        if e == 0 and not first:
                            if c == 3:
                                add_context(n - 1)
                            if 4 <= c <= 7:
                                add_latent(n - 1, 2 * c - 8)
                                add_latent(n - 1, 2 * c - 7)
                        if e == 0 and c == 11:
                            dve.wait_ge(scat_ps.sem, n + 1)
                            dve.tensor_copy(scat_s, ps[:, 2, :])
                            dve.tensor_copy(scat_p[0:64, :], ps[0:64, 3, 0:TP]).then_inc(scat_ready.sem, 1)
                        dve.wait_ge(hi_ready, l * SPLIT_LAYER + MIX_SPLITS + i * PAIR_CHUNKS + q + 1)
                        dve.wait_ge(lo_used[q % 2], l * (SPLIT_LAYER // 2) + MIX_SPLITS // 2
                                    + i * (PAIR_CHUNKS // 2) + q // 2 + 1)
                        dve.tensor_tensor(w_lo[:, q % 2, :], ring[:, q % NSLOT, :], w_hi[:, q % 2, :].bitcast(F32),
                                          ALU.subtract).then_inc(slot_used[q % NSLOT], 1)
                        if e == 1 and not last_pair and c == 3:
                            picks(n + 1, 2 * i + 2)
                        if c in (5, 9):
                            half = (c - 5) // 4
                            dve.wait_ge(silu_ready.sem, 2 * m + half + 1)
                            dve.tensor_tensor(act_row[0:CAP, half, :], ps[0:CAP, 4 + 2 * half, :], silu_t[0:CAP, :],
                                              ALU.mult).then_inc(act_ready.sem, 1)
                        if c in (7, 10):
                            half = (c - 7) // 3
                            dve.wait_ge(actT_hi.sem, 2 * m + half + 1)
                            at = slice(4 * half, 4 * half + 4)
                            dve.tensor_tensor(act_lo[:, e, at, :].rearrange("p f c -> p (f c)"),
                                              ps[:, 7, 0:4 * CAP],
                                              act_hi[:, e, at, :].rearrange("p f c -> p (f c)").bitcast(F32),
                                              ALU.subtract).then_inc(actT_ready.sem, 1)
                        if e == 1 and not last_pair and c >= 9:
                            gathered_lo(n + 1, c - 9)

            dve.memset(eps[:, :], EPS).then_inc(consts_set, 1)
            dve.wait_ge(start_in, 48)
            with dve.Fori(0, DEPTH) as l:
                dve.wait_ge(*params_in.at(l, 4))
                root_x(l, 0)
                dve.wait_ge(*mod_ps.at(l, 1))
                dve.tensor_tensor(mod[:, :, :], ps[:, 0, 0:96].rearrange("p (a b) -> p a b", b=2),
                                  par[:, Q_ADAB:Q_ADAB + 48][:, :, None].to_broadcast([P, 48, 2]), ALU.add)
                dve.tensor_scalar(gq[:, :], par[:, Q_GQ:Q_GQ + 1], DN ** -0.5, None, ALU.mult)
                dve.drain()
                for a, c, g in ((a1, 8, Q_G1), (a2, 32, Q_G2)):
                    dve.scalar_tensor_tensor(a[:, :, :], mod[:, c:c + 8, :], 1.0,
                                             par[:, g:g + 8][:, :, None].to_broadcast([P, 8, 2]),
                                             ALU.add, ALU.mult).then_inc(scale_ready.sem, 1)
                for k in range(KD):
                    dve.wait_ge(*h_ready.at(l, k + 1))
                    dve.tensor_tensor(h_lo[:, k, :], h[:, k, :], h_hi[:, k, :].bitcast(F32), ALU.subtract)\
                        .then_inc(h_split.sem, 1)
                rope(l, U_RQ, mq)
                gate_rows(l)
                rope(l, U_RK, mk)
                for t in range(NTILE):
                    add_row_bias(l, U_MV + t, mv[:, t, :], 0).then_inc(dve_emptied.sem, 1)
                mlstm(l)
                norm_heads(l, 0, y_ml, ml_tmp, lambda i: par[:, Q_OG + i:Q_OG + i + 1])
                for i in range(KB):
                    dve.drain()
                    dve.wait_ge(*emptied(l, U_MO + i))
                    dve.tensor_tensor(y_ml[:, i, :], y_ml[:, i, :], sig_mo[:, i, :], ALU.mult)\
                        .then_inc(yml_ready.sem, 1)
                norm_heads(l, HM, nq, na_tmp, lambda i: gq[:, :])
                for t in range(NTILE):
                    if t in (0, 2):
                        norm_heads(l, HM + KB, nk, ml_tmp, lambda i: par[:, Q_GK:Q_GK + 1],
                                   range(3) if t == 0 else range(3, 4))
                    if t >= 3:
                        dve.wait_ge(*nv_stored[t % 2].at(l, t - 2))
                    out = nvp if t == 0 else nvst[:, t % 2, :]
                    add_row_bias(l, U_NV + t, out, WB).then_inc(dve_emptied.sem, 1)
                    dve.drain()
                    dve.sem_inc(nv_staged.sem, 1)
                for b in range(2):
                    last = dve.memset(bias_t[:, b, :, WINK:NKEY], 0.0)
                dve.drain()
                dve.sem_inc(bias_zeroed.sem, 1)
                attention(l)
                convolution(l)
                merge(l)
                mix_in(l)
                root_x(l, 1)
                route(l)
                picks(l * NPAIR, 0)
                for j in range(3):
                    gathered_lo(l * NPAIR, j)
                pair(l, 0, first=True)
                with dve.Fori(1, NPAIR - 1) as i:
                    pair(l, i)
                pair(l, NPAIR - 1, last_pair=True)
                add_context(l * NPAIR + NPAIR - 1)
                for dt in range(KD):
                    add_latent(l * NPAIR + NPAIR - 1, dt)
                dve.drain()
                dve.sem_inc(layer_x.sem, 1)


def constants():
    k = np.zeros((P, NCONST), np.float32)
    k[:, K_ID:K_ID + P] = np.eye(P)
    k[:, K_ONE:K_ONE + P] = 1.0
    for b in range(2):
        k[64 * b:64 * b + 64, K_BLK + 64 * b:K_BLK + 64 * b + 64] = 1.0
    half = 32
    freqs = (np.float32(10000.0) ** (-np.arange(half, dtype=np.float32) / np.float32(half))).astype(np.float32)
    t = np.arange(TS)
    for b, pos in enumerate(((t // GRID).astype(np.float32), (t % GRID).astype(np.float32))):
        ang = freqs[:, None] * pos[None, :]
        for s in range(2):
            at = 64 * b + 32 * s
            k[at:at + 32, K_COS:K_COS + TS] = np.cos(ang)
            k[at:at + 32, K_SIN:K_SIN + TS] = np.sin(ang)
        for i in range(half):
            k[64 * b + 32 + i, K_ROT + 64 * b + i] = -1.0
            k[64 * b + i, K_ROT + 64 * b + 32 + i] = 1.0
    s, q = np.arange(P)[:, None], np.arange(P)[None, :]
    k[:, K_TRI:K_TRI + P] = np.where(q >= s, 0.0, -1e30)
    k[:, K_TRI + P:K_TRI + 2 * P] = np.where(q <= s, 0.0, -1e30)
    for n in range(NBLK):
        qcol = n * QB + np.arange(P)[:, None] % QB
        start = np.clip(qcol - 8, 0, GRID - 16)
        kcol = BAND0[n] + np.arange(KBAND)[None, :]
        k[:, K_MASK + n * KBAND:K_MASK + (n + 1) * KBAND] = np.where((kcol >= start) & (kcol < start + 16), 0.0, -1e30)
    k[:, K_IOTA:K_IOTA + CAP_S] = np.arange(CAP_S)
    return k


def kernel(**inputs):
    import numpy as np
    import concourse.bacc as bacc
    from concourse import mybir
    from concourse.bass_utils import run_bass_kernel_spmd as run

    a = {n: np.ascontiguousarray(v) for n, v in inputs.items()}
    f32 = np.float32
    xT = np.concatenate([a["x_prompt"][0].T, a["x_sample"][0].T], axis=1)
    cond = np.stack([a["c_ctx"], a["c"][0]], axis=1)

    def cols(v):
        return v.reshape(DEPTH, -1, P).transpose(0, 2, 1)

    b_in = a["b_in"]
    b_main = np.concatenate([b_in[:, :C_G], b_in[:, C_CB:]], axis=1)
    fm = a["ml_fbias"].reshape(DEPTH, 8)
    m0 = a["state_mlstm_m"][0].reshape(DEPTH, 8)
    twice = lambda v: np.concatenate([v, v], axis=1)[:, :, None]
    prm = np.concatenate([
        cols(a["ada_b"]), cols(a["norm1_g"]), cols(a["norm2_g"]), cols(b_main), cols(a["ml_out_g"]),
        cols(a["cv_w"].reshape(DEPTH, -1)), twice(a["na_q_g"]), twice(a["na_k_g"]),
        np.broadcast_to(m0[:, None, :], (DEPTH, P, 8)),
        a["state_mlstm_n"][0].reshape(DEPTH, 8, P).transpose(0, 2, 1),
        np.broadcast_to(b_in[:, None, C_MV:C_MV + WB], (DEPTH, P, WB)),
        np.broadcast_to(b_in[:, None, C_NV:C_NV + WB], (DEPTH, P, WB))], axis=2)
    rowp = np.stack([b_in[:, C_G:C_G + 8], b_in[:, C_G + 8:C_G + 16], fm, m0], axis=2)
    rpb = np.pad(a["na_rpb"], ((0, 0), (0, 0), (0, 0), (16, 16)))
    r, q = np.arange(P) // QB, np.arange(P) % QB
    dr = np.arange(ROWS)[None, :] - r[:, None] + 7
    biasT = np.stack([
        rpb[:, :, dr[:, :, None],
            (np.arange(KBAND)[None, :] + BAND0[n] - n * QB - q[:, None] + 15 + 16)[:, None, :]]
        for n in range(NBLK)], axis=1)
    biasT = biasT.transpose(0, 1, 3, 2, 4, 5).reshape(DEPTH, NBLK, P, HN, WINK)
    arrays = {
        "xT": xT, "cond": cond, "const": constants(), "prm": prm, "rowp": rowp, "biasT": biasT,
        "ckT": a["cache_ctx_k"][0].reshape(DEPTH, P, WB).transpose(0, 2, 1),
        "cv": a["cache_ctx_v"][0].reshape(DEPTH, P, WB),
        "c0": a["state_mlstm_c"][0].reshape(DEPTH, 8, P, P),
        **{n: a[n] for n in ("ada_w", "w_in", "w_pa", "w_pb", "w_pc", "w_o", "w_router", "w_gate", "w_up", "w_down")},
    }
    nc = bacc.Bacc("TRN2", target_bir_lowering=False, num_devices=1)
    nc.disable_value_cache = True
    aps = []
    arrays = {n: np.ascontiguousarray(v) for n, v in arrays.items()}
    for n, v in arrays.items():
        aps.append(nc.dram_tensor(n, v.shape, mybir.dt.from_np(v.dtype), kind="ExternalInput").ap())
    outs = {"yT": (D, T), "new_k": (DEPTH, WB, TP), "new_v": (DEPTH, TP, WB), "new_cn": (DEPTH, 8, P, P + 1), "new_m": (DEPTH, 8, 1)}
    for n, s in outs.items():
        aps.append(nc.dram_tensor(n, s, mybir.dt.float32, kind="ExternalOutput").ap())
    aps.append(nc.dram_tensor("nv_copy", (TS, WB), mybir.dt.float32, kind="Internal").ap())
    aps.append(nc.dram_tensor("x_copy", (P, KD, T), mybir.dt.float32, kind="Internal").ap())
    step_program(nc, *aps)
    res = run(nc, [arrays], core_ids=[0]).results[0]
    yT = res["yT"]
    return (yT[:, :TP].T[None], yT[:, TP:].T[None],
            res["new_k"].transpose(0, 2, 1).reshape(1, DEPTH, TP, HN, DN),
            res["new_v"].reshape(1, DEPTH, TP, HN, DN),
            res["new_cn"][..., :P].reshape(1, DEPTH, 2, HM, P, P),
            res["new_cn"][..., P].reshape(1, DEPTH, 2, HM, P),
            res["new_m"].reshape(1, DEPTH, 2, HM))
```
